# Optimizing a Trainium2 kernel written in Bass

```python
import jax, jax.numpy as jnp
from jax import lax
import numpy as np

D_MODEL = 1024
BATCH = 1
SEQ = 512
DEPTH = 2

N_MEM = 256
N_EVEN = (DEPTH + 1) // 2
N_ODD = DEPTH // 2
ALPHA = (2.0 * DEPTH) ** 0.25
BETA = (8.0 * DEPTH) ** -0.25
LN_EPS = 1e-5
NEG = -1e30
POOL_WIDTH = D_MODEL // 2
POOL_WINDOWS = (2, 4, 8, 16)
POOL_GROUP = POOL_WIDTH // len(POOL_WINDOWS)
NSA_HEADS = 8
NSA_KV_HEADS = 2
NSA_HEAD_DIM = (D_MODEL // 2) // NSA_HEADS
NSA_GROUP = NSA_HEADS // NSA_KV_HEADS
CMP_BLOCK = 32
CMP_STRIDE = 16
SEL_BLOCK = 64
SEL_COUNT = 16
WINDOW = 512
Q_BLOCK = 128
N_BRANCH = 3
FORCE_SCORE = 1e4
ROPE_THETA = 500000.0
ROT_DIM = NSA_HEAD_DIM // 4
Q_WIDTH = NSA_HEADS * NSA_HEAD_DIM
KV_WIDTH = NSA_KV_HEADS * NSA_HEAD_DIM
GATE_WIDTH = NSA_HEADS * N_BRANCH
EVEN_SPLITS = (POOL_WIDTH, Q_WIDTH, GATE_WIDTH) + (KV_WIDTH,) * (2 * N_BRANCH)
EVEN_IN_WIDTH = sum(EVEN_SPLITS)
RNN_WIDTH = 1280
RNN_BLOCKS = 10
RNN_BLOCK_W = RNN_WIDTH // RNN_BLOCKS
CONV_WIDTH = 4
LRU_C = 8.0
X_HEADS = 4
X_HEAD_DIM = D_MODEL // X_HEADS
FFN_HIDDEN = ((8 * D_MODEL // 3 + 255) // 256) * 256

kernel_name = "hybrid_pool_nsa_rglru_deepnorm"

def layer_norm(x, g, b):
    xf = x.astype(jnp.float32)
    mu = jnp.mean(xf, axis=-1, keepdims=True)
    var = jnp.mean(jnp.square(xf - mu), axis=-1, keepdims=True)
    y = (xf - mu) * lax.rsqrt(var + LN_EPS)
    return (y * g.astype(jnp.float32) + b.astype(jnp.float32)).astype(x.dtype)

def rotary(x, pos):
    half = ROT_DIM // 2
    inv = ROPE_THETA ** (-jnp.arange(half, dtype=jnp.float32) * 2.0 / ROT_DIM)
    ang = pos.astype(jnp.float32)[..., None] * inv
    cos = jnp.cos(ang)[:, :, None, :].astype(x.dtype)
    sin = jnp.sin(ang)[:, :, None, :].astype(x.dtype)
    x1 = x[..., :half]
    x2 = x[..., half:ROT_DIM]
    return jnp.concatenate([x1 * cos - x2 * sin, x2 * cos + x1 * sin, x[..., ROT_DIM:]], axis=-1)

def masked_softmax(s, valid):
    p = jax.nn.softmax(jnp.where(valid, s, NEG), axis=-1)
    return p * valid.astype(p.dtype)

def multiscale_pool(u, w_pool, scale):
    B, S, C = u.shape
    uf = u.astype(jnp.float32)
    csum = jnp.pad(jnp.cumsum(uf, axis=1), ((0, 0), (1, 0), (0, 0)))
    t = jnp.arange(S)
    outs = []
    for g, w in enumerate(POOL_WINDOWS):
        sl = slice(g * POOL_GROUP, (g + 1) * POOL_GROUP)
        cg = csum[..., sl]
        lo = jnp.maximum(t + 1 - w, 0)
        total = cg[:, 1:] - jnp.take(cg, lo, axis=1)
        count = jnp.minimum(t + 1, w).astype(jnp.float32)[None, :, None]
        outs.append(total / count - uf[..., sl])
    pooled = jnp.stack(outs, axis=2).astype(u.dtype)
    mixed = jnp.einsum('bsgc,gcd->bsgd', pooled, w_pool)
    return mixed.reshape(B, S, C) * scale

def nsa_attention(q, gates, k_cmp, v_cmp, k_sel, v_sel, k_win, v_win, positions,
                  cmp_pos_k, cmp_pos_v, cmp_wk, cmp_wv):
    B, S = q.shape[:2]
    G, R, HD = NSA_KV_HEADS, NSA_GROUP, NSA_HEAD_DIM
    scale = HD ** -0.5
    q = rotary(q, positions)
    k_sel = rotary(k_sel, positions)
    k_win = rotary(k_win, positions)

    n_cmp = (S - CMP_BLOCK) // CMP_STRIDE + 1
    starts = jnp.arange(n_cmp) * CMP_STRIDE
    cmp_end = starts + CMP_BLOCK - 1
    idx = starts[:, None] + jnp.arange(CMP_BLOCK)[None, :]

    def compress(raw, pos_emb, w):
        blocks = raw[:, idx] + pos_emb[None, None, :, None, :]
        blocks = blocks.transpose(0, 1, 3, 2, 4).reshape(B, n_cmp, G, CMP_BLOCK * HD)
        return blocks @ w

    kc = rotary(compress(k_cmp, cmp_pos_k, cmp_wk), positions[:, cmp_end])
    vc = compress(v_cmp, cmp_pos_v, cmp_wv)

    n_sb = S // SEL_BLOCK
    n_pick = min(SEL_COUNT, n_sb)
    jb = jnp.arange(n_sb)
    overlap = ((starts[:, None] < (jb[None, :] + 1) * SEL_BLOCK)
               & (starts[:, None] + CMP_BLOCK > jb[None, :] * SEL_BLOCK)).astype(jnp.float32)
    ks_blk = k_sel.reshape(B, n_sb, SEL_BLOCK, G, HD).transpose(0, 3, 1, 2, 4)
    vs_blk = v_sel.reshape(B, n_sb, SEL_BLOCK, G, HD).transpose(0, 3, 1, 2, 4)
    b_ix = jnp.arange(B)[:, None, None, None]
    g_ix = jnp.arange(G)[None, :, None, None]

    kw_pad = jnp.pad(k_win, ((0, 0), (WINDOW, 0), (0, 0), (0, 0)))
    vw_pad = jnp.pad(v_win, ((0, 0), (WINDOW, 0), (0, 0), (0, 0)))

    n_qb = S // Q_BLOCK
    q_blocks = q.reshape(B, n_qb, Q_BLOCK, G, R, HD).transpose(1, 0, 2, 3, 4, 5)
    g_blocks = gates.reshape(B, n_qb, Q_BLOCK, G, R, N_BRANCH).transpose(1, 0, 2, 3, 4, 5)

    def one_block(args):
        qb_i, qb, gb = args
        q0 = qb_i * Q_BLOCK
        t = q0 + jnp.arange(Q_BLOCK)
        s = jnp.einsum('bqgrd,bngd->bgrqn', qb, kc).astype(jnp.float32) * scale
        p_c = masked_softmax(s, cmp_end[None, :] <= t[:, None])
        o_c = jnp.einsum('bgrqn,bngd->bqgrd', p_c.astype(qb.dtype), vc)
        imp = jnp.einsum('bgrqn,nj->bgqj', p_c, overlap)
        cur = t // SEL_BLOCK
        forced = (jb[None, :] == 0) | (jb[None, :] == cur[:, None]) | (jb[None, :] == cur[:, None] - 1)
        future = jb[None, :] > cur[:, None]
        imp = jnp.where(forced, FORCE_SCORE, jnp.where(future, -1.0, imp))
        _, sel = lax.top_k(imp, n_pick)
        k_g = ks_blk[b_ix, g_ix, sel]
        v_g = vs_blk[b_ix, g_ix, sel]
        kpos = sel[..., None] * SEL_BLOCK + jnp.arange(SEL_BLOCK)
        s = jnp.einsum('bqgrd,bgqnld->bgrqnl', qb, k_g).astype(jnp.float32) * scale
        valid = (kpos <= t[:, None, None])[:, :, None]
        m = n_pick * SEL_BLOCK
        p_s = masked_softmax(s.reshape(B, G, R, Q_BLOCK, m), valid.reshape(B, G, 1, Q_BLOCK, m))
        o_s = jnp.einsum('bgrqm,bgqmd->bqgrd', p_s.astype(qb.dtype), v_g.reshape(B, G, Q_BLOCK, m, HD))
        kwb = lax.dynamic_slice_in_dim(kw_pad, q0, WINDOW + Q_BLOCK, axis=1)
        vwb = lax.dynamic_slice_in_dim(vw_pad, q0, WINDOW + Q_BLOCK, axis=1)
        kpw = q0 - WINDOW + jnp.arange(WINDOW + Q_BLOCK)
        valid_w = ((kpw[None, :] <= t[:, None]) & (kpw[None, :] > t[:, None] - WINDOW)
                   & (kpw[None, :] >= 0))
        s = jnp.einsum('bqgrd,bkgd->bgrqk', qb, kwb).astype(jnp.float32) * scale
        p_w = masked_softmax(s, valid_w)
        o_w = jnp.einsum('bgrqk,bkgd->bqgrd', p_w.astype(qb.dtype), vwb)
        return gb[..., 0:1] * o_c + gb[..., 1:2] * o_s + gb[..., 2:3] * o_w

    out = lax.map(one_block, (jnp.arange(n_qb), q_blocks, g_blocks))
    return out.transpose(1, 0, 2, 3, 4, 5).reshape(B, S, NSA_HEADS * HD)

def pool_nsa_mixer(x, positions, w_in, pool_w, pool_scale, cmp_pos_k, cmp_pos_v,
                   cmp_wk, cmp_wv, w_out):
    B, S, _ = x.shape
    u = x @ w_in
    cuts = [int(c) for c in np.cumsum(EVEN_SPLITS)[:-1]]
    pool_in, q, gate_logits, kc, vc, ks, vs, kw, vw = jnp.split(u, cuts, axis=-1)
    kv = lambda a: a.reshape(B, S, NSA_KV_HEADS, NSA_HEAD_DIM)
    q = q.reshape(B, S, NSA_HEADS, NSA_HEAD_DIM)
    gates = jax.nn.sigmoid(gate_logits).reshape(B, S, NSA_HEADS, N_BRANCH)
    pool_out = multiscale_pool(pool_in, pool_w, pool_scale)
    nsa_out = nsa_attention(q, gates, kv(kc), kv(vc), kv(ks), kv(vs), kv(kw), kv(vw), positions,
                            cmp_pos_k, cmp_pos_v, cmp_wk, cmp_wv)
    return jnp.concatenate([pool_out, nsa_out], axis=-1) @ w_out

def rglru_mixer(x, positions, w_in, conv_w, conv_b, wa, ba, wx, bx, lam, w_out):
    B, S, _ = x.shape
    u = x @ w_in
    gate, xr = u[..., :RNN_WIDTH], u[..., RNN_WIDTH:]
    xp = jnp.pad(xr, ((0, 0), (CONV_WIDTH - 1, 0), (0, 0)))
    xc = conv_b
    for k in range(CONV_WIDTH):
        xc = xc + xp[:, k:k + S] * conv_w[k]
    xb = xc.reshape(B, S, RNN_BLOCKS, RNN_BLOCK_W)
    r = jax.nn.sigmoid(jnp.einsum('bshi,hij->bshj', xb, wa).reshape(B, S, RNN_WIDTH) + ba)
    i = jax.nn.sigmoid(jnp.einsum('bshi,hij->bshj', xb, wx).reshape(B, S, RNN_WIDTH) + bx)
    log_a = -LRU_C * r.astype(jnp.float32) * jax.nn.softplus(-lam.astype(jnp.float32))
    a = jnp.exp(log_a)
    mult = jnp.sqrt(-jnp.expm1(2.0 * log_a))
    reset = (positions == 0)[..., None]
    a = jnp.where(reset, 0.0, a)
    mult = jnp.where(reset, 1.0, mult)
    b = mult * (i * xc).astype(jnp.float32)

    def combine(left, right):
        a1, b1 = left
        a2, b2 = right
        return a1 * a2, a2 * b1 + b2

    _, h = lax.associative_scan(combine, (a, b), axis=1)
    y = h.astype(x.dtype) * jax.nn.gelu(gate)
    return y @ w_out

def memory_cross_attention(x, mem, wq, wkv, wo):
    B, S, D = x.shape
    M = mem.shape[1]
    q = (x @ wq).reshape(B, S, X_HEADS, X_HEAD_DIM)
    kv = mem @ wkv
    k = kv[..., :D].reshape(B, M, X_HEADS, X_HEAD_DIM)
    v = kv[..., D:].reshape(B, M, X_HEADS, X_HEAD_DIM)
    s = jnp.einsum('bshd,bmhd->bhsm', q, k).astype(jnp.float32) * (X_HEAD_DIM ** -0.5)
    p = jax.nn.softmax(s, axis=-1).astype(x.dtype)
    o = jnp.einsum('bhsm,bmhd->bshd', p, v).reshape(B, S, D)
    return o @ wo

def swiglu(x, w_up, w_down):
    h = x @ w_up
    return (jax.nn.silu(h[..., :FFN_HIDDEN]) * h[..., FFN_HIDDEN:]) @ w_down

def setup_inputs(seed: int = 0) -> dict:
    key = jax.random.key(seed)
    ks = iter(jax.random.split(key, 40))
    nrm = lambda shape: jax.random.normal(next(ks), shape, jnp.float32)
    dense = lambda shape, fan_in, gain=1.0: nrm(shape) * (fan_in ** -0.5) * gain
    D, HD = D_MODEL, NSA_HEAD_DIM
    u = jax.random.uniform(next(ks), (N_ODD, RNN_WIDTH), jnp.float32, 0.9, 0.999)
    s = u ** (1.0 / LRU_C)
    return {
        "x": nrm((BATCH, SEQ, D)),
        "mem": nrm((BATCH, N_MEM, D)),
        "positions": jnp.broadcast_to(jnp.arange(SEQ, dtype=jnp.int32), (BATCH, SEQ)),
        "e_w_in": dense((N_EVEN, D, EVEN_IN_WIDTH), D),
        "e_pool_w": dense((N_EVEN, len(POOL_WINDOWS), POOL_GROUP, POOL_GROUP), POOL_GROUP),
        "e_pool_scale": 1.0 + 0.02 * nrm((N_EVEN, POOL_WIDTH)),
        "e_cmp_pos_k": 0.1 * nrm((N_EVEN, CMP_BLOCK, HD)),
        "e_cmp_pos_v": 0.1 * nrm((N_EVEN, CMP_BLOCK, HD)),
        "e_cmp_wk": dense((N_EVEN, CMP_BLOCK * HD, HD), CMP_BLOCK * HD),
        "e_cmp_wv": dense((N_EVEN, CMP_BLOCK * HD, HD), CMP_BLOCK * HD),
        "e_w_out": dense((N_EVEN, D, D), D, BETA),
        "o_w_in": dense((N_ODD, D, 2 * RNN_WIDTH), D),
        "o_conv_w": dense((N_ODD, CONV_WIDTH, RNN_WIDTH), CONV_WIDTH),
        "o_conv_b": 0.01 * nrm((N_ODD, RNN_WIDTH)),
        "o_wa": dense((N_ODD, RNN_BLOCKS, RNN_BLOCK_W, RNN_BLOCK_W), RNN_BLOCK_W),
        "o_ba": 0.01 * nrm((N_ODD, RNN_WIDTH)),
        "o_wx": dense((N_ODD, RNN_BLOCKS, RNN_BLOCK_W, RNN_BLOCK_W), RNN_BLOCK_W),
        "o_bx": 0.01 * nrm((N_ODD, RNN_WIDTH)),
        "o_lambda": jnp.log(s) - jnp.log1p(-s),
        "o_w_out": dense((N_ODD, RNN_WIDTH, D), RNN_WIDTH, BETA),
        "x_wq": dense((DEPTH, D, D), D),
        "x_wkv": dense((DEPTH, D, 2 * D), D),
        "x_wo": dense((DEPTH, D, D), D, BETA),
        "f_w_up": dense((DEPTH, D, 2 * FFN_HIDDEN), D),
        "f_w_down": dense((DEPTH, FFN_HIDDEN, D), FFN_HIDDEN, BETA),
        "ln_g": 1.0 + 0.02 * nrm((DEPTH, 3, D)),
        "ln_b": 0.01 * nrm((DEPTH, 3, D)),
    }

def reference(x, mem, positions, e_w_in, e_pool_w, e_pool_scale, e_cmp_pos_k, e_cmp_pos_v,
              e_cmp_wk, e_cmp_wv, e_w_out, o_w_in, o_conv_w, o_conv_b, o_wa, o_ba, o_wx, o_bx,
              o_lambda, o_w_out, x_wq, x_wkv, x_wo, f_w_up, f_w_down, ln_g, ln_b):
    for layer in range(DEPTH):
        j = layer // 2
        if layer % 2 == 0:
            m = pool_nsa_mixer(x, positions, e_w_in[j], e_pool_w[j], e_pool_scale[j],
                               e_cmp_pos_k[j], e_cmp_pos_v[j], e_cmp_wk[j], e_cmp_wv[j], e_w_out[j])
        else:
            m = rglru_mixer(x, positions, o_w_in[j], o_conv_w[j], o_conv_b[j], o_wa[j], o_ba[j],
                            o_wx[j], o_bx[j], o_lambda[j], o_w_out[j])
        x = layer_norm(ALPHA * x + m, ln_g[layer, 0], ln_b[layer, 0])
        c = memory_cross_attention(x, mem, x_wq[layer], x_wkv[layer], x_wo[layer])
        x = layer_norm(ALPHA * x + c, ln_g[layer, 1], ln_b[layer, 1])
        f = swiglu(x, f_w_up[layer], f_w_down[layer])
        x = layer_norm(ALPHA * x + f, ln_g[layer, 2], ln_b[layer, 2])
    return x


_drawn_inputs = setup_inputs


def setup_inputs(seed=0):
    import zlib

    import numpy as np

    out = dict(_drawn_inputs(seed))
    spreads = {}
    factors = {'e_pool_scale': 65.664,
     'e_cmp_pos_k': 200.0,
     'e_cmp_pos_v': 18.005,
     'o_conv_b': 5.281,
     'o_ba': 200.0,
     'o_bx': 64.0,
     'e_cmp_wk': 8.69}
    for name, (base, spread) in spreads.items():
        noise = np.random.default_rng([zlib.crc32(name.encode()), seed]).standard_normal(out[name].shape)
        drawn = base * np.exp(spread * noise) if base else spread * noise
        out[name] = __import__('jax').numpy.asarray(drawn.astype(out[name].dtype))
    for name, factor in factors.items():
        out[name] = (out[name] * factor).astype(out[name].dtype)
    return out
```

```python
from contextlib import ExitStack

import numpy as np

import concourse.bass as bass
from concourse import mybir

F32 = mybir.dt.float32
F32R = mybir.dt.float32r
BF16 = mybir.dt.bfloat16
I32 = mybir.dt.int32
ALU = mybir.AluOpType
ACT = mybir.ActivationFunctionType
AX = mybir.AxisListType

P = 128
D = 1024
KT = D // P
SEQ = 512
TT = SEQ // P
MEM = 256
MT = MEM // P
DEPTH = 2
ALPHA = (2.0 * DEPTH) ** 0.25
EPS = 1e-5
NEG = -1e30
WINDOWS = (2, 4, 8, 16)
HEADS, KV_HEADS, HD = 8, 2, 64
GROUP = HEADS // KV_HEADS
GATES = HEADS * 3
CMP_BLOCK, CMP_STRIDE = 32, 16
NCMP = (SEQ - CMP_BLOCK) // CMP_STRIDE + 1
ROT = HD // 4
HALF = ROT // 2
RNN = 1280
RT = RNN // P
X_HEADS, X_HD = 4, D // 4
FFN = 2816
FT = FFN // P
PAD = 16
CONV = 4
COLS = 512
BANK = 512
RING = 4

C_ID = 0
C_CAUSAL = C_ID + P
C_PINV = C_CAUSAL + P
C_INVF = C_PINV + 4 * PAD
C_CMASK = C_INVF + HALF
C_ROWOK = C_CMASK + TT * 32
C_END = C_ROWOK + TT

V_POSK, V_POSV = 0, CMP_BLOCK
V_PSCALE = 2 * CMP_BLOCK
V_CONVW = V_PSCALE + 4
V_CONVB = V_CONVW + CONV * RT
V_BA = V_CONVB + RT
V_BX = V_BA + RT
V_LAM = V_BX + RT
V_END = V_LAM + RT

E_Q = 512
E_GATE = 1024
E_KV = E_GATE + GATES
E_KS = E_KV + 256


def shape_constants():
    c = np.zeros((P, C_END), np.float32)
    c[:, C_ID:C_ID + P] = np.eye(P)
    q, k = np.arange(P)[:, None], np.arange(P)[None, :]
    c[:, C_CAUSAL:C_CAUSAL + P] = np.where(k <= q, 0.0, NEG)
    for g, w in enumerate(WINDOWS):
        c[:, C_PINV + g * PAD:C_PINV + (g + 1) * PAD] = 1.0 / np.minimum(np.arange(PAD) + 1, w)
    c[:, C_INVF:C_INVF + HALF] = np.float32(500000.0) ** (-np.arange(HALF, dtype=np.float32) * np.float32(2.0) / np.float32(ROT))
    for t in range(TT):
        ends = np.arange(32) * CMP_STRIDE + CMP_BLOCK - 1
        tok = t * P + np.arange(P)
        c[:, C_CMASK + t * 32:C_CMASK + (t + 1) * 32] = np.where(ends[None, :] <= tok[:, None], 0.0, NEG)
        c[:, C_ROWOK + t] = tok >= CMP_BLOCK - 1
    return c


def plan_groups():
    g = [("x0", 0, 4, 4), ("x1", 0, 4, 4), ("small", 0, 1, 0)]
    g += [("ein0", KT, 4, 0), ("ein1", KT, 4, 0), ("ein2", KT, 4, 0), ("ein3", KT, 3, 0)]
    g += [("mix", 0, 4, 4), ("tq", 0, 4, 0), ("tk", 0, 4, 0), ("cmp", 0, 3, 0), ("tkc", 0, 2, 0)]
    g += [("attn", 0, 0, 0), ("to", 0, 4, 4)]
    g += [("eout0", KT, 0, 4), ("eout1", KT, 0, 4)]
    g += [("tm", 0, 4, 4)]
    g += [("k0_0", KT, 4, 0), ("k0_1", KT, 4, 0), ("v0_0", KT, 2, 0), ("v0_1", KT, 2, 0)]
    for l in range(DEPTH):
        if l:
            for n in (0, 1):
                g += [(f"oin{n}", KT, 4, 0)]
            g += [("ra0", 0, 4, 0), ("ia0", 0, 4, 0), ("oin2", KT, 4, 0), ("ra1", 0, 4, 0), ("ia1", 0, 4, 0)]
            g += [("oin3", KT, 4, 0), ("ra2", 0, 2, 0), ("ia2", 0, 2, 0), ("oin4", KT, 4, 0)]
            g += [("oout0", RT, 0, 4), ("oout1", RT, 0, 4)]
        g += [(f"ln{l}0_0", 0, 4, 4), (f"ln{l}0_1", 0, 4, 4)]
        g += [(f"q{l}_0", KT, 4, 0), (f"q{l}_1", KT, 4, 0), (f"xattn{l}", 0, 0, 0)]
        g += [(f"xo{l}_0", 0, 4, 4), (f"xo{l}_1", 0, 4, 4)]
        g += [(f"wo{l}_0", KT, 0, 4), (f"wo{l}_1", KT, 0, 4)]
        if l == 0:
            g += [("k1_0", KT, 4, 0), ("k1_1", KT, 4, 0)]
        g += [(f"ln{l}1_0", 0, 4, 4), (f"ln{l}1_1", 0, 4, 4)]
        g += [(f"up{l}_{n}", KT, 2, 2) for n in range(FT // 2)]
        g += [(f"dn{l}_0", FT, 0, 4), (f"dn{l}_1", FT, 0, 4)]
        if l == 0:
            g += [("v1_0", KT, 2, 0), ("v1_1", KT, 2, 0)]
            g += [("ln02_0", 0, 4, 4), ("ln02_1", 0, 4, 4)]
    return g


PLAN = plan_groups()
INDEX = {name: i for i, (name, _, _, _) in enumerate(PLAN)}
CHUNK0 = {name: sum(k for _, k, _, _ in PLAN[:i]) for name, i in INDEX.items()}
ACT_BEFORE = {name: sum(a for _, _, a, _ in PLAN[:i]) for name, i in INDEX.items()}
DVE_BEFORE = {name: sum(v for _, _, _, v in PLAN[:i]) for name, i in INDEX.items()}
ACT_AFTER = {name: ACT_BEFORE[name] + PLAN[i][2] for name, i in INDEX.items()}
DVE_AFTER = {name: DVE_BEFORE[name] + PLAN[i][3] for name, i in INDEX.items()}
RG_SETS = [(6, 4, "oin0", 0), (2, 4, "oin1", 0), (0, 2, "oin2", 2)]
GATE_SETS = [(8, 2, "oin2"), (4, 4, "oin3"), (0, 4, "oin4")]
OIN_COL = [2048, 1536, 1024, 512, 0]
BRANCHES = ("sel", "win", "cmp")
UNITS = [(qb, g, b) for qb in range(TT) for g in range(KV_HEADS) for b in BRANCHES]


def unit_blocks(u):
    qb, _, b = UNITS[u]
    return 1 if b == "cmp" else qb + 1


PT_BEFORE = [sum(unit_blocks(v) for v in range(u)) for u in range(len(UNITS) + 1)]


def hybrid_trunk(nc, a, out):
    ctx = ExitStack()
    with ctx:
        def at(name, shape, dt, offset):
            return nc.alloc_sbuf_tensor_at(name, shape, dt, offset=offset)

        cur = [16512]

        def place(name, shape, dt):
            n = int(np.prod(shape[1:])) * mybir.dt.size(dt)
            o = cur[0]
            cur[0] += (n + 31) // 32 * 32
            return at(name, shape, dt, o), o

        x_res, _ = place("x_res", [P, TT, D], F32)
        fm_hi, _ = place("fm_hi", [P, KT, SEQ], F32R)
        fm_lo, _ = place("fm_lo", [P, KT, SEQ], F32R)
        w_raw, _ = place("w_raw", [P, RING, COLS], F32)
        w_hi, _ = place("w_hi", [P, RING, COLS], F32R)
        w_lo, _ = place("w_lo", [P, RING, COLS], F32R)
        k_mem, _ = place("k_mem", [P, KT, MEM], F32)
        v_mem, o_v = place("v_mem", [P, MT, D], F32)
        consts, _ = place("consts", [P, C_END], F32)
        chan, _ = place("chan", [P, V_END], F32)
        ident_b, _ = place("ident_b", [P, P], BF16)
        causal_b, _ = place("causal_b", [P, P], BF16)
        cmask_b, _ = place("cmask_b", [P, TT, 32], BF16)
        stats, _ = place("stats", [P, TT, 2, 6], F32)
        mv, _ = place("mv", [P, TT, 2], F32)
        lnc, _ = place("lnc", [P, 4, TT], F32)
        negmax, _ = place("negmax", [P, 2, 4], F32)
        rowsum, _ = place("rowsum", [P, 2, 4], F32)
        weight, _ = place("weight", [P, 2, 4], F32)
        gates, _ = place("gates", [P, TT, GATES], F32)
        kcT, _ = place("kcT", [P, KV_HEADS, NCMP], F32)
        vc_tok, _ = place("vc_tok", [NCMP, KV_HEADS * HD], F32)
        trig, _ = place("trig", [P, 2, TT + 1, HALF], F32)
        lru_c, _ = place("lru_c", [P, 2, RT], F32)
        ln_g, o_ln = place("ln_g", [P, D], F32)
        ln_b, _ = place("ln_b", [P, D], F32)
        cur[0] = o_ln + 10 * 2 * P * 4
        m0 = cur[0]
        mem_hi, _ = place("mem_hi", [P, KT, MEM], F32R)
        mem_lo, _ = place("mem_lo", [P, KT, MEM], F32R)
        G = cur[0]
        g_hi = at("g_hi", [P, FT, SEQ], F32R, G)
        g_lo = at("g_lo", [P, FT, SEQ], F32R, G + FT * SEQ * 4)
        assert G + 2 * FT * SEQ * 4 <= 229344, G + 2 * FT * SEQ * 4
        q_tok = at("q_tok", [P, TT, 512], F32, G)
        kv_tok = at("kv_tok", [P, TT, 512], F32, G + 8192)
        qT = at("qT", [P, TT, SEQ], F32, G + 16384)
        kT = at("kT", [P, 2, KV_HEADS, SEQ], F32, G + 24576)
        kdup = at("kdup", [P, 2, TT, KV_HEADS, 2, HD], F32, G + 32768)
        probs = at("probs", [P, 2, GROUP, SEQ], F32, G + 40960)
        raw_cmp = at("raw_cmp", [P, 2, SEQ], F32, G + 40960)
        raw_pos = at("raw_pos", [P, 2, 2, SEQ], F32, G + 45056)
        kc_tok = at("kc_tok", [NCMP, KV_HEADS, HD], F32, G)
        kc_dup = at("kc_dup", [NCMP, KV_HEADS, 2, HD], F32, G + 512)
        rot_tmp = at("rot_tmp", [P, 3, TT * HEADS * HALF], F32, G + 53248)
        probsT = at("probsT", [P, TT, GROUP * P], F32, G + 57344)
        o_tok = at("o_tok", [P, TT, 512], F32, G + 65536)
        pool_in = at("pool_in", [P, 4, PAD + SEQ], F32, G + 57344)
        pool_sum = at("pool_sum", [P, 2, PAD + SEQ], F32, G + 65792)
        gateT = at("gateT", [GATES, SEQ], F32, G + 70016)
        cmp_w = at("cmp_w", [P, 2, CMP_BLOCK, HD], F32, G + 73728)
        o_tmp = at("o_tmp", [P, GROUP * HD], F32, G + 73728)
        pool_w = at("pool_w", [P, 4, P], F32, G + 24576)
        mem_tok = at("mem_tok", [P, MT, D], F32, G)
        rows_posk = at("rows_posk", [CMP_BLOCK, 2, HD], F32, G + 8192)
        rows_posv = at("rows_posv", [CMP_BLOCK, 2, HD], F32, G + 8704)
        rows_ps = at("rows_ps", [4, P], F32, G + 9216)
        rows_rg = at("rows_rg", [V_END - V_CONVW, P], F32, G + 9728)
        pos_i = at("pos_i", [P, TT + 1], I32, G + 16384)
        pos_f = at("pos_f", [P, TT + 1], F32, G + 16416)
        ang = at("ang", [P, 4, (TT + 1) * HALF], F32, G + 16448)
        q_x = at("q_x", [P, KT, SEQ], F32, G)
        px = at("px", [P, 2, X_HEADS, MEM], F32, G + 16384)
        pxT = at("pxT", [P, MT, X_HEADS, SEQ], F32, G + 24576)
        silu = at("silu", [P, 2, SEQ], F32, o_v)
        gf = at("gf", [P, 2, SEQ], F32, o_v + 4096)
        R = m0
        x_pad = at("x_pad", [P, 4, CONV - 1 + SEQ], F32, R)
        xc = at("xc", [P, 4, SEQ], F32, R + 8256)
        ra = at("ra", [P, 4, SEQ], F32, R + 8256 + 8192)
        ib = at("ib", [P, 4, SEQ], F32, R + 8256 + 2 * 8192)
        tm = at("tm", [P, 4, SEQ], F32, R + 8256 + 3 * 8192)
        h = at("h", [P, RT, SEQ], F32, R + 8256 + 4 * 8192)
        y_hi = at("y_hi", [P, RT, SEQ], F32R, R + 61504)
        y_lo = at("y_lo", [P, RT, SEQ], F32R, R + 81984)
        gg = at("gg", [P, SEQ], F32, R + 102464)
        w_gates = at("w_gates", [P, 2, RT, P], F32, o_ln)
        keep = at("keep", [P, SEQ], F32, R + 104512)
        posb = at("posb", [P, SEQ], I32, R + 81984)
        assert R + 104512 + 2048 <= 229344, R + 106560

        ps = ctx.enter_context(nc.psum_tensor("ps", [P, 8, BANK], F32))

        def sem(name):
            return ctx.enter_context(nc.semaphore(name))

        w_landed = [sem(f"w_landed{i}") for i in range(RING)]
        s_x = [sem(f"s_x{t}") for t in range(TT)]
        s_consts, s_mem, s_rows, s_pos = sem("s_consts"), sem("s_mem"), sem("s_rows"), sem("s_pos")
        s_cmpw, s_poolw, s_lnp, s_wgates, s_posb = sem("s_cmpw"), sem("s_poolw"), sem("s_lnp"), sem("s_wgates"), sem("s_posb")
        s_out = sem("s_out")
        w_rounded, w_split, w_used = sem("w_rounded"), sem("w_split"), sem("w_used")
        filled = sem("filled")
        evac_a, evac_d = sem("evac_a"), sem("evac_d")
        a_chain, d_chain = sem("a_chain"), sem("d_chain")
        tables_ready, cols_ready = sem("tables_ready"), sem("cols_ready")
        ang_ready, trig_ready = sem("ang_ready"), sem("trig_ready")
        pooled_ready, q_ready, kdup_ready, rawpos_ready = sem("pooled_ready"), sem("q_ready"), sem("kdup_ready"), sem("rawpos_ready")
        kcdup_ready = sem("kcdup_ready")
        scored, maxed, exped = sem("scored"), sem("maxed"), sem("exped")
        turned, pt_d, pt_a, pv_done, o_evac, o_ready = sem("turned"), sem("pt_d"), sem("pt_a"), sem("pv_done"), sem("o_evac"), sem("o_ready")
        x_scored, x_maxed, x_exped, x_scaled = sem("x_scored"), sem("x_maxed"), sem("x_exped"), sem("x_scaled")
        x_turned, xpt_d, xpt_a = sem("x_turned"), sem("xpt_d"), sem("xpt_a")
        ln_var, ln_sd, ln_coef, ln_norm, x_ready = sem("ln_var"), sem("ln_sd"), sem("ln_coef"), sem("ln_norm"), sem("x_ready")
        g_hi_ready, g_ready = sem("g_hi_ready"), sem("g_ready")
        conv_ready, ta_ready, m2_ready, mult_ready, h_ready = sem("conv_ready"), sem("ta_ready"), sem("m2_ready"), sem("mult_ready"), sem("h_ready")
        gg_used, y_hi_ready, y_ready = sem("gg_used"), sem("y_hi_ready"), sem("y_ready")
        sp_ready, sp_exp, lru_ready, pads_ready, keep_ready = sem("sp_ready"), sem("sp_exp"), sem("lru_ready"), sem("pads_ready"), sem("keep_ready")
        

        block = ctx.enter_context(nc.Block())

        ident = consts[:, C_ID:C_ID + P]

        def chunk_sources():
            def rows(w, k, cols, n):
                return [(w[k * P:(k + 1) * P, cols:cols + n], 0, n)]
            for name, steps, _, _ in PLAN:
                for k in range(steps):
                    kind, n = name.split("_")[0], int(name.split("_")[1]) if "_" in name else 0
                    if name in ("ein0", "ein1"):
                        yield rows(a["e_w_in"][0], k, 512 * int(name[3]), 512)
                    elif name == "ein2":
                        yield rows(a["e_w_in"][0], k, E_KS, 512)
                    elif name == "ein3":
                        yield rows(a["e_w_in"][0], k, E_GATE, GATES + 256)
                    elif name[:4] == "eout":
                        yield rows(a["e_w_out"][0], k, 512 * int(name[4]), 512)
                    elif name[:4] == "oout":
                        yield rows(a["o_w_out"][0], k, 512 * int(name[4]), 512)
                    elif name[:3] == "oin":
                        yield rows(a["o_w_in"][0], k, OIN_COL[int(name[3])], 512)
                    elif kind[0] == "k":
                        yield rows(a["x_wkv"][int(kind[1])], k, 512 * n, 512)
                    elif kind[0] == "v":
                        yield rows(a["x_wkv"][int(kind[1])], k, D + 512 * n, 512)
                    elif kind[0] == "q":
                        yield rows(a["x_wq"][int(kind[1])], k, 512 * n, 512)
                    elif kind[:2] == "wo":
                        yield rows(a["x_wo"][int(kind[2])], k, 512 * n, 512)
                    elif kind[:2] == "dn":
                        yield rows(a["f_w_down"][int(kind[2])], k, 512 * n, 512)
                    else:
                        assert kind[:2] == "up", name
                        w = a["f_w_up"][int(kind[2])]
                        yield [(w[k * P:(k + 1) * P, 256 * n:256 * n + 256], 0, 256),
                               (w[k * P:(k + 1) * P, FFN + 256 * n:FFN + 256 * n + 256], 256, 256)]

        CHUNKS = list(chunk_sources())
        LANDS = [0] * RING
        LANDED = []
        for c, pieces in enumerate(CHUNKS):
            LANDS[c % RING] += 16 * len(pieces)
            LANDED.append(LANDS[c % RING])
        WIDTH = [sum(n for _, _, n in pieces) for pieces in CHUNKS]

        TURNED = {}
        for name, steps, na, nd in PLAN:
            if steps == 0 and "attn" not in name:
                TURNED[name] = len(TURNED) + 1

        @block.sync
        def _(sp):
            sp.dma_start(consts[:, :], a["consts"]).then_inc(s_consts, 16)
            for t in range(TT):
                sp.dma_start(x_res[:, t, :], a["x"][0, t * P:(t + 1) * P, :]).then_inc(s_x[t], 16)
            sp.dma_start(pos_i[:, 0:TT], a["positions"][0].rearrange("(t p) -> p t", p=P),
                         allow_slow_non_contiguous=True).then_inc(s_pos, 16)
            sp.dma_start(pos_i[0:NCMP, TT:TT + 1],
                         a["positions"][0, CMP_BLOCK - 1:SEQ].rearrange("(n o) -> n o", o=1)[::CMP_STRIDE, :],
                         allow_slow_non_contiguous=True).then_inc(s_pos, 16)
            sp.dma_start(rows_posk[:, 0, :], a["e_cmp_pos_k"][0]).then_inc(s_rows, 16)
            sp.dma_start(rows_posk[:, 1, :], a["e_cmp_pos_k"][0]).then_inc(s_rows, 16)
            sp.dma_start(rows_posv[:, 0, :], a["e_cmp_pos_v"][0]).then_inc(s_rows, 16)
            sp.dma_start(rows_posv[:, 1, :], a["e_cmp_pos_v"][0]).then_inc(s_rows, 16)
            sp.dma_start(rows_ps[:, :], a["e_pool_scale"][0].rearrange("(g p) -> g p", p=P)).then_inc(s_rows, 16)
            for n in range(CONV):
                sp.dma_start(rows_rg[n * RT:(n + 1) * RT, :],
                             a["o_conv_w"][0, n].rearrange("(j p) -> j p", p=P)).then_inc(s_rows, 16)
            for n, name in enumerate(("o_conv_b", "o_ba", "o_bx", "o_lambda")):
                sp.dma_start(rows_rg[(CONV + n) * RT:(CONV + n + 1) * RT, :],
                             a[name][0].rearrange("(j p) -> j p", p=P)).then_inc(s_rows, 16)

            def weights(first, last):
                for c in range(first, last):
                    if c >= RING:
                        sp.wait_ge(w_split, c - RING + 1)
                    for src, o, n in CHUNKS[c]:
                        sp.dma_start(w_raw[:, c % RING, o:o + n], src).then_inc(w_landed[c % RING], 16)

            def ln_params(l, i):
                sp.dma_start(ln_g[:, :], a["ln_g"][l, i].partition_broadcast(P)).then_inc(s_lnp, 16)
                sp.dma_start(ln_b[:, :], a["ln_b"][l, i].partition_broadcast(P)).then_inc(s_lnp, 16)

            weights(0, CHUNK0["ein1"])
            for half in (0, 1):
                for n, name in enumerate(("e_cmp_wk", "e_cmp_wv")):
                    sp.dma_start(cmp_w[half * HD:(half + 1) * HD, n, :, :],
                                 a[name][0].rearrange("(l d) e -> d l e", d=HD)).then_inc(s_cmpw, 16)
            sp.dma_start(pool_w[:, :, :], a["e_pool_w"][0].rearrange("g c d -> c g d")).then_inc(s_poolw, 16)
            ln_params(0, 0)
            weights(CHUNK0["ein1"], CHUNK0["k0_0"])
            sp.wait_ge(evac_d, DVE_AFTER["to"])
            sp.dma_start(mem_tok[:, :, :], a["mem"][0].rearrange("(t p) d -> p t d", p=P)).then_inc(s_mem, 16)
            weights(CHUNK0["k0_0"], CHUNK0["q0_1"])
            sp.wait_ge(x_ready, TT * 1)
            ln_params(0, 1)
            weights(CHUNK0["q0_1"], CHUNK0["up0_1"])
            sp.wait_ge(x_ready, TT * 2)
            ln_params(0, 2)
            weights(CHUNK0["up0_1"], CHUNK0["oin1"])
            sp.wait_ge(x_ready, TT * 3)
            sp.dma_start(w_gates[:, 0, :, :], a["o_wa"][0].rearrange("h i j -> i h j")).then_inc(s_wgates, 16)
            sp.dma_start(w_gates[:, 1, :, :], a["o_wx"][0].rearrange("h i j -> i h j")).then_inc(s_wgates, 16)
            sp.dma_start(posb[:, :], a["positions"][0].partition_broadcast(P)).then_inc(s_posb, 16)
            weights(CHUNK0["oin1"], CHUNK0["oout0"])
            sp.wait_ge(filled, TURNED["ia2"])
            ln_params(1, 0)
            weights(CHUNK0["oout0"], CHUNK0["q1_1"])
            sp.wait_ge(x_ready, TT * 4)
            ln_params(1, 1)
            weights(CHUNK0["q1_1"], CHUNK0["up1_1"])
            sp.wait_ge(x_ready, TT * 5)
            ln_params(1, 2)
            weights(CHUNK0["up1_1"], len(CHUNKS))
            for t in range(TT):
                sp.wait_ge(x_ready, TT * 5 + t + 1)
                sp.dma_start(out[0, t * P:(t + 1) * P, :], x_res[:, t, :]).then_inc(s_out, 16)
            sp.wait_ge(s_out, 16 * TT)

        @block.gpsimd
        def _(pool):
            for c in range(len(CHUNKS)):
                s, n = c % RING, WIDTH[c]
                pool.wait_ge(w_landed[s], LANDED[c])
                if c >= RING:
                    pool.wait_ge(w_used, c - RING + 1)
                nc.gpsimd.tensor_copy(w_hi[:, s, :n], w_raw[:, s, :n]).then_inc(w_rounded, 1)
                pool.wait_ge(w_rounded, c + 1)
                nc.gpsimd.tensor_tensor(w_lo[:, s, :n], w_raw[:, s, :n], w_hi[:, s, :n].bitcast(F32),
                                        ALU.subtract).then_inc(w_split, 1)

        @block.tensor
        def _(pe):
            def begin(name):
                i = INDEX[name]
                if i >= 2:
                    before = PLAN[i - 2][0]
                    evacuated(before)
                return 4 * (i % 2)

            def evacuated(name):
                if ACT_AFTER[name]:
                    pe.wait_ge(evac_a, ACT_AFTER[name])
                if DVE_AFTER[name]:
                    pe.wait_ge(evac_d, DVE_AFTER[name])

            def passes(outp, k, steps, w, x, w_first):
                for n, (i, j) in enumerate(((0, 0), (0, 1), (1, 0))):
                    lhsT, rhs = (w[i], x[j]) if w_first else (x[j], w[i])
                    last = nc.tensor.matmul(outp, lhsT, rhs, start=(k == 0 and n == 0),
                                            stop=(k == steps - 1 and n == 2))
                return last

            def turn(out_, in_, n=P):
                return nc.tensor.transpose(out_, in_, ident[0:n, 0:n])

            def turn_tokens(name, tok, tiles):
                b0 = begin(name)
                for i, t in enumerate(tiles):
                    for k in range(KT):
                        last = turn(ps[:, b0 + 2 * i + k // 4, (k % 4) * P:(k % 4 + 1) * P], tok[:, t, k * P:(k + 1) * P])
                last.then_inc(filled, 1)

            fm = (fm_hi, fm_lo)
            mem = (mem_hi, mem_lo)

            def product(name, act, tokens, feature_major, col0=(0, P, 2 * P, 3 * P)):
                b0, steps = begin(name), PLAN[INDEX[name]][1]
                hi, lo = act
                for k in range(steps):
                    c = CHUNK0[name] + k
                    s, n = c % RING, WIDTH[c]
                    pe.wait_ge(w_split, c + 1)
                    nb = len(col0) if feature_major else tokens // P
                    for j in range(nb):
                        if feature_major:
                            w = [w_[:, s, col0[j]:col0[j] + P] for w_ in (w_hi, w_lo)]
                            last = passes(ps[:, b0 + j, :tokens], k, steps, w, (hi[:, k, :], lo[:, k, :]), True)
                        else:
                            x = [x_[:, k, j * P:(j + 1) * P] for x_ in (hi, lo)]
                            last = passes(ps[:, b0 + j, :n], k, steps, (w_hi[:, s, :n], w_lo[:, s, :n]), x, False)
                    last.then_inc(w_used, 1)

            pe.wait_ge(s_consts, 16)
            pe.wait_ge(s_x[0], 16)
            pe.wait_ge(s_x[1], 16)
            turn_tokens("x0", x_res, (0, 1))
            pe.wait_ge(s_x[2], 16)
            pe.wait_ge(s_x[3], 16)
            turn_tokens("x1", x_res, (2, 3))
            b0 = begin("small")
            pe.wait_ge(s_rows, 16 * (5 + CONV + 4))
            turn(ps[:, b0, V_POSK:V_POSK + CMP_BLOCK], rows_posk[:, :, :].rearrange("l a d -> l (a d)"), CMP_BLOCK)
            turn(ps[:, b0, V_POSV:V_POSV + CMP_BLOCK], rows_posv[:, :, :].rearrange("l a d -> l (a d)"), CMP_BLOCK)
            turn(ps[:, b0, V_PSCALE:V_PSCALE + 4], rows_ps[:, :], 4)
            turn(ps[:, b0, V_CONVW:V_END], rows_rg[:, :], V_END - V_CONVW).then_inc(filled, 1)

            evacuated("x1")
            product("ein0", fm, SEQ, True)
            product("ein1", fm, SEQ, False)
            product("ein2", fm, SEQ, False)
            product("ein3", fm, SEQ, True, (0, GATES, GATES + P))
            b0 = begin("mix")
            pe.wait_ge(s_poolw, 16)
            pe.wait_ge(pooled_ready, 4)
            for g in range(4):
                last = nc.tensor.matmul(ps[:, b0 + g, :], pool_w[:, g, :], pool_in[:, g, PAD:], start=True, stop=True)
            last.then_inc(filled, 1)
            b0 = begin("tq")
            pe.wait_ge(q_ready, 1)
            for j in range(4):
                for t in range(TT):
                    last = turn(ps[:, b0 + j, t * P:(t + 1) * P], q_tok[:, t, j * P:(j + 1) * P])
            last.then_inc(filled, 1)
            b0 = begin("tk")
            pe.wait_ge(kdup_ready, 2)
            for b in (0, 1):
                for g in range(KV_HEADS):
                    for t in range(TT):
                        last = turn(ps[:, b0 + 2 * b + g, t * P:(t + 1) * P],
                                    kdup[:, b, t, g, :, :].rearrange("p a d -> p (a d)"))
            last.then_inc(filled, 1)
            b0 = begin("cmp")
            pe.wait_ge(rawpos_ready, 4)
            pe.wait_ge(s_cmpw, 64)
            for n in (0, 1):
                for g in range(KV_HEADS):
                    half = slice(g * HD, (g + 1) * HD)
                    for l in range(CMP_BLOCK):
                        src = raw_pos[half, n, l // CMP_STRIDE, l:l + (NCMP - 1) * CMP_STRIDE + 1:CMP_STRIDE]
                        nc.tensor.matmul(ps[0:NCMP, b0 + g, n * HD:(n + 1) * HD], src, cmp_w[half, n, l, :],
                                         start=(l == 0), stop=(l == CMP_BLOCK - 1))
            for t in range(TT):
                last = turn(ps[:, b0 + 2, t * GATES:(t + 1) * GATES], gateT[:, t * P:(t + 1) * P], GATES)
            last.then_inc(filled, 1)
            b0 = begin("tkc")
            pe.wait_ge(kcdup_ready, 1)
            for g in range(KV_HEADS):
                last = turn(ps[:, b0 + g, 0:NCMP], kc_dup[:, g, :, :].rearrange("p a d -> p (a d)"), NCMP)
            last.then_inc(filled, 1)

            evacuated("tkc")
            pe.wait_ge(tables_ready, 3)

            def scores(u):
                qb, g, b = UNITS[u]
                if u:
                    pe.wait_ge(exped, u)
                n = NCMP if b == "cmp" else (qb + 1) * P
                for r in range(GROUP):
                    hh = g * GROUP + r
                    half = slice((hh % 2) * HD, (hh % 2 + 1) * HD)
                    q = qT[half, hh // 2, qb * P:(qb + 1) * P]
                    k = kcT[half, g, :] if b == "cmp" else kT[half, BRANCHES.index(b), g, :n]
                    nc.tensor.matmul(ps[:, r, :n], q, k, start=True, stop=False, skip_group_check=True)
                    mask, o = (cmask_b[:, qb, :NCMP], 0) if b == "cmp" else (causal_b[:, :], qb * P)
                    last = nc.tensor.matmul(ps[:, r, o:n], ident_b[:, :], mask, start=False, stop=True,
                                            skip_group_check=True)
                last.then_inc(scored, 1)

            def weigh(u):
                qb, g, b = UNITS[u]
                pe.wait_ge(exped, u + 1)
                n = NCMP if b == "cmp" else P
                for kb in range(unit_blocks(u)):
                    i = PT_BEFORE[u] + kb
                    if i >= 2:
                        pe.wait_ge(pt_a if i % 2 else pt_d, i // 2)
                    for r in range(GROUP):
                        last = nc.tensor.matmul(ps[0:n, 4 + i % 2, r * P:(r + 1) * P], probs[:, u % 2, r, kb * P:kb * P + n],
                                                ident, start=True, stop=True, is_transpose=True if n == P else None)
                    last.then_inc(turned, 1)
                e = PT_BEFORE[u + 1]
                if (e + 1) // 2:
                    pe.wait_ge(pt_d, (e + 1) // 2)
                if e // 2:
                    pe.wait_ge(pt_a, e // 2)
                if u >= 2:
                    pe.wait_ge(o_evac, u - 1)
                for r in range(GROUP):
                    for kb in range(unit_blocks(u)):
                        if b == "cmp":
                            v = vc_tok[:, g * HD:(g + 1) * HD]
                        else:
                            c0 = 256 * BRANCHES.index(b) + P + g * HD
                            v = kv_tok[:, kb, c0:c0 + HD]
                        last = nc.tensor.matmul(ps[:, 6 + u % 2, r * HD:(r + 1) * HD], probsT[0:n, kb, r * P:(r + 1) * P], v,
                                                start=(kb == 0), stop=(kb == unit_blocks(u) - 1))
                last.then_inc(pv_done, 1)

            scores(0)
            for u in range(len(UNITS)):
                if u + 1 < len(UNITS):
                    scores(u + 1)
                weigh(u)
            pe.wait_ge(o_ready, 2 * TT * KV_HEADS)
            b0 = 4 * (INDEX["to"] % 2)
            for t in range(TT):
                for k in range(4):
                    last = turn(ps[:, b0 + t, k * P:(k + 1) * P], o_tok[:, t, k * P:(k + 1) * P])
            last.then_inc(filled, 1)
            evacuated("to")
            product("eout0", fm, SEQ, False)
            product("eout1", fm, SEQ, False)
            pe.wait_ge(s_mem, 16)
            turn_tokens("tm", mem_tok, (0, 1))
            evacuated("tm")
            product("k0_0", mem, MEM, True)
            product("k0_1", mem, MEM, True)
            product("v0_0", mem, MEM, False)
            product("v0_1", mem, MEM, False)

            for l in range(DEPTH):
                if l:
                    def recurrence_gates(n):
                        first, tiles, _, _ = RG_SETS[n]
                        pe.wait_ge(s_wgates, 32)
                        pe.wait_ge(conv_ready, sum(s[1] for s in RG_SETS[:n + 1]))
                        for i, kind in enumerate(("ra", "ia")):
                            b0 = begin(f"{kind}{n}")
                            for j in range(tiles):
                                last = nc.tensor.matmul(ps[:, b0 + j, :], w_gates[:, i, first + j, :], xc[:, j, :],
                                                        start=True, stop=True)
                            last.then_inc(filled, 1)

                    product("oin0", fm, SEQ, True)
                    product("oin1", fm, SEQ, True)
                    recurrence_gates(0)
                    product("oin2", fm, SEQ, True)
                    recurrence_gates(1)
                    product("oin3", fm, SEQ, True)
                    recurrence_gates(2)
                    product("oin4", fm, SEQ, True)
                    pe.wait_ge(y_ready, RT)
                    product("oout0", (y_hi, y_lo), SEQ, False)
                    product("oout1", (y_hi, y_lo), SEQ, False)

                def turn_normed(i):
                    for n in (0, 1):
                        pe.wait_ge(x_ready, TT * (3 * l + i) + 2 * n + 2)
                        turn_tokens(f"ln{l}{i}_{n}", x_res, (2 * n, 2 * n + 1))
                    evacuated(f"ln{l}{i}_1")

                turn_normed(0)
                product(f"q{l}_0", fm, SEQ, True)
                product(f"q{l}_1", fm, SEQ, True)
                evacuated(f"q{l}_1")

                def x_scores(u):
                    v = l * TT + u
                    if u >= 2:
                        pe.wait_ge(x_exped, v - 1)
                    for r in range(X_HEADS):
                        for k in (0, 1):
                            last = nc.tensor.matmul(ps[:, 2 * (u % 2) + r // 2, (r % 2) * MEM:(r % 2 + 1) * MEM],
                                                    q_x[:, 2 * r + k, u * P:(u + 1) * P], k_mem[:, 2 * r + k, :],
                                                    start=(k == 0), stop=(k == 1))
                    last.then_inc(x_scored, 1)

                x_scores(0)
                for u in range(TT):
                    if u + 1 < TT:
                        x_scores(u + 1)
                    v = l * TT + u
                    pe.wait_ge(x_scaled, v + 1)
                    if v:
                        pe.wait_ge(xpt_d, v)
                        pe.wait_ge(xpt_a, v)
                    for m in range(MT):
                        for r in range(X_HEADS):
                            last = turn(ps[:, 4 + m, r * P:(r + 1) * P], px[:, u % 2, r, m * P:(m + 1) * P])
                        last.then_inc(x_turned, 1)
                pe.wait_ge(xpt_d, (l + 1) * TT)
                pe.wait_ge(xpt_a, (l + 1) * TT)
                for n in (0, 1):
                    b0 = 4 * (INDEX[f"xo{l}_{n}"] % 2)
                    for j in range(4):
                        r = 2 * n + j // 2
                        for m in range(MT):
                            c0 = r * X_HD + (j % 2) * P
                            last = nc.tensor.matmul(ps[:, b0 + j, :], v_mem[:, m, c0:c0 + P], pxT[:, m, r, :],
                                                    start=(m == 0), stop=(m == MT - 1))
                    last.then_inc(filled, 1)
                evacuated(f"xo{l}_1")
                product(f"wo{l}_0", fm, SEQ, False)
                product(f"wo{l}_1", fm, SEQ, False)
                if l == 0:
                    product("k1_0", mem, MEM, True)
                    product("k1_1", mem, MEM, True)
                turn_normed(1)
                for n in range(FT // 2):
                    product(f"up{l}_{n}", fm, SEQ, True)
                pe.wait_ge(g_ready, (l + 1) * FT)
                product(f"dn{l}_0", (g_hi, g_lo), SEQ, False)
                product(f"dn{l}_1", (g_hi, g_lo), SEQ, False)
                if l == 0:
                    product("v1_0", mem, MEM, False)
                    product("v1_1", mem, MEM, False)
                    turn_normed(2)

        def group_filled(eng, name):
            if PLAN[INDEX[name]][1]:
                eng.wait_ge(w_used, CHUNK0[name] + PLAN[INDEX[name]][1])
            else:
                eng.wait_ge(filled, TURNED[name])

        def bank(name, j):
            return ps[:, 4 * (INDEX[name] % 2) + j, :]

        def fm_target(tile_hi, name, j):
            t, k = 2 * int(name[-1] if name != "tm" else 0) + j // 2, 4 * (j % 2)
            return tile_hi[:, k:k + 4, t * P:(t + 1) * P]

        def quarter(p):
            return p.rearrange("p (k s) -> p k s", s=P)

        @block.scalar
        def _(act):
            chain = [0]

            def settle(ins):
                chain[0] += 1
                ins.then_inc(a_chain, 1)
                act.wait_ge(a_chain, chain[0])

            def turn_evac(name, hi):
                group_filled(act, name)
                for j in range(4):
                    nc.scalar.activation(fm_target(hi, name, j), quarter(bank(name, j)), ACT.Copy).then_inc(evac_a, 1)

            turn_evac("x0", fm_hi)
            turn_evac("x1", fm_hi)
            group_filled(act, "small")
            nc.scalar.activation(chan[:, :], bank("small", 0)[:, 0:V_END], ACT.Copy).then_inc(evac_a, 1)
            act.wait_ge(ang_ready, 1)
            nc.scalar.activation(trig[:, 1, :, :].rearrange("p t f -> p (t f)"), ang[:, 0, :], ACT.Sin).then_inc(trig_ready, 1)
            nc.scalar.activation(trig[:, 0, :, :].rearrange("p t f -> p (t f)"), ang[:, 1, :], ACT.Sin).then_inc(trig_ready, 1)
            act.wait_ge(sp_ready, 1)
            nc.scalar.activation(lru_c[:, 1, :], lru_c[:, 0, :], ACT.Exp).then_inc(sp_exp, 1)
            act.wait_ge(pads_ready, 1)
            group_filled(act, "ein0")
            for j in range(4):
                nc.scalar.activation(pool_in[:, j, PAD:], bank("ein0", j), ACT.Copy).then_inc(evac_a, 1)
            group_filled(act, "ein1")
            for j in range(4):
                nc.scalar.activation(q_tok[:, j, :], bank("ein1", j), ACT.Copy, scale=HD ** -0.5).then_inc(evac_a, 1)
            group_filled(act, "ein2")
            for j in range(4):
                nc.scalar.activation(kv_tok[:, j, :], bank("ein2", j), ACT.Copy).then_inc(evac_a, 1)
            group_filled(act, "ein3")
            nc.scalar.activation(gateT[:, :], bank("ein3", 0)[0:GATES, :], ACT.Sigmoid).then_inc(evac_a, 1)
            for n in (0, 1):
                nc.scalar.activation(raw_cmp[:, n, :], bank("ein3", 1 + n), ACT.Copy).then_inc(evac_a, 1)
            group_filled(act, "mix")
            for j in range(4):
                nc.scalar.activation(fm_hi[:, j, :], bank("mix", j), ACT.Copy,
                                     scale=chan[:, V_PSCALE + j:V_PSCALE + j + 1]).then_inc(evac_a, 1)
            group_filled(act, "tq")
            for j in range(4):
                nc.scalar.activation(qT[:, j, :], bank("tq", j), ACT.Copy).then_inc(evac_a, 1)
            group_filled(act, "tk")
            for j in range(4):
                nc.scalar.activation(kT[:, j // 2, j % 2, :], bank("tk", j), ACT.Copy).then_inc(evac_a, 1)
            group_filled(act, "cmp")
            b0 = 4 * (INDEX["cmp"] % 2)
            cmp_banks = ps[0:NCMP, b0:b0 + 2, :]
            nc.scalar.activation(kc_tok[:, :, :], cmp_banks[:, :, 0:HD], ACT.Copy).then_inc(evac_a, 1)
            nc.scalar.activation(vc_tok[:, :].rearrange("n (g d) -> n g d", d=HD), cmp_banks[:, :, HD:2 * HD], ACT.Copy).then_inc(evac_a, 1)
            nc.scalar.activation(gates[:, :, :].rearrange("p t c -> p (t c)"), bank("cmp", 2)[:, 0:TT * GATES], ACT.Copy).then_inc(evac_a, 1)
            group_filled(act, "tkc")
            for g in range(KV_HEADS):
                nc.scalar.activation(kcT[:, g, :], bank("tkc", g)[:, 0:NCMP], ACT.Copy).then_inc(evac_a, 1)

            def exps(u):
                qb, g, b = UNITS[u]
                n = NCMP if b == "cmp" else (qb + 1) * P
                act.wait_ge(maxed, u + 1)
                if u >= 2:
                    act.wait_ge(turned, PT_BEFORE[u - 1])
                for r in range(GROUP):
                    last = nc.scalar.activation(probs[:, u % 2, r, :n], ps[:, r, :n], ACT.Exp,
                                                bias=negmax[:, u % 2, r:r + 1], accum_out=rowsum[:, u % 2, r:r + 1])
                last.then_inc(exped, 1)

            exps(0)
            for u in range(len(UNITS)):
                if u + 1 < len(UNITS):
                    exps(u + 1)
                n = NCMP if UNITS[u][2] == "cmp" else P
                if u:
                    act.wait_ge(pv_done, u)
                for kb in range(unit_blocks(u)):
                    i = PT_BEFORE[u] + kb
                    if i % 2:
                        act.wait_ge(turned, i + 1)
                        nc.scalar.activation(probsT[0:n, kb, :], ps[0:n, 5, :], ACT.Copy).then_inc(pt_a, 1)
            group_filled(act, "to")
            for t in range(TT):
                nc.scalar.activation(fm_hi[:, 4:8, t * P:(t + 1) * P], quarter(bank("to", t)), ACT.Copy).then_inc(evac_a, 1)
            turn_evac("tm", mem_hi)

            def keys_evac(l):
                for n in (0, 1):
                    group_filled(act, f"k{l}_{n}")
                    for j in range(4):
                        nc.scalar.activation(k_mem[:, 4 * n + j, :], bank(f"k{l}_{n}", j)[:, :MEM], ACT.Copy).then_inc(evac_a, 1)

            def values_evac(l):
                for n in (0, 1):
                    group_filled(act, f"v{l}_{n}")
                    for m in range(MT):
                        nc.scalar.activation(v_mem[:, m, 512 * n:512 * (n + 1)], bank(f"v{l}_{n}", m), ACT.Copy).then_inc(evac_a, 1)

            def norm(l, i):
                v = 3 * l + i
                act.wait_ge(ln_var, v + 1)
                nc.scalar.activation(lnc[:, 1, :], lnc[:, 0, :], ACT.Sqrt).then_inc(ln_sd, 1)
                act.wait_ge(ln_coef, v + 1)
                for t in range(TT):
                    nc.scalar.activation(x_res[:, t, :], x_res[:, t, :], ACT.Identity, scale=lnc[:, 2, t:t + 1],
                                         bias=lnc[:, 3, t:t + 1]).then_inc(ln_norm, 1)

            def norm_turned(l, i):
                turn_evac(f"ln{l}{i}_0", fm_hi)
                turn_evac(f"ln{l}{i}_1", fm_hi)

            for l in range(DEPTH):
                if l:
                    gates_done = [0]

                    def gate_evac(n):
                        first, tiles, name = GATE_SETS[n]
                        if name != "oin2":
                            group_filled(act, name)
                        for j in range(tiles):
                            i = gates_done[0]
                            nc.scalar.activation(gg[:, :], bank(name, j), ACT.Gelu_apprx_tanh).then_inc(evac_a, 1)
                            act.wait_ge(gg_used, i + 1)
                            nc.scalar.activation(y_hi[:, first + j, :], h[:, first + j, :], ACT.Copy).then_inc(y_hi_ready, 1)
                            gates_done[0] += 1

                    def x_evac(n):
                        first, tiles, name, b = RG_SETS[n]
                        if n:
                            act.wait_ge(conv_ready, sum(s[1] for s in RG_SETS[:n]))
                        else:
                            act.wait_ge(pads_ready, 2)
                        group_filled(act, name)
                        for j in range(tiles):
                            nc.scalar.activation(x_pad[:, j, CONV - 1:], bank(name, b + j), ACT.Copy).then_inc(evac_a, 1)

                    def lru(n):
                        first, tiles, _, _ = RG_SETS[n]
                        done = sum(s[1] for s in RG_SETS[:n])
                        if n:
                            act.wait_ge(h_ready, done)
                        group_filled(act, f"ra{n}")
                        for j in range(tiles):
                            nc.scalar.activation(ra[:, j, :], bank(f"ra{n}", j), ACT.Sigmoid,
                                                 bias=chan[:, V_BA + first + j:V_BA + first + j + 1]).then_inc(evac_a, 1)
                        group_filled(act, f"ia{n}")
                        for j in range(tiles):
                            nc.scalar.activation(ib[:, j, :], bank(f"ia{n}", j), ACT.Sigmoid,
                                                 bias=chan[:, V_BX + first + j:V_BX + first + j + 1]).then_inc(evac_a, 1)
                        act.wait_ge(evac_a, ACT_AFTER[f"ra{n}"])
                        act.wait_ge(lru_ready, 1)
                        for j in range(tiles):
                            last = nc.scalar.activation(tm[:, j, :], ra[:, j, :], ACT.Tanh, scale=lru_c[:, 0, first + j:first + j + 1])
                        settle(last)
                        for j in range(tiles):
                            nc.scalar.activation(ra[:, j, :], ra[:, j, :], ACT.Exp,
                                                 scale=lru_c[:, 1, first + j:first + j + 1]).then_inc(ta_ready, 1)
                        for j in range(tiles):
                            act.wait_ge(m2_ready, done + j + 1)
                            nc.scalar.activation(tm[:, j, :], tm[:, j, :], ACT.Sqrt).then_inc(mult_ready, 1)

                    x_evac(0)
                    x_evac(1)
                    lru(0)
                    group_filled(act, "oin2")
                    gate_evac(0)
                    x_evac(2)
                    lru(1)
                    gate_evac(1)
                    lru(2)
                    gate_evac(2)
                norm(l, 0)
                if l == 0:
                    keys_evac(0)
                    values_evac(0)
                norm_turned(l, 0)
                for n in (0, 1):
                    group_filled(act, f"q{l}_{n}")
                    for j in range(4):
                        nc.scalar.activation(q_x[:, 4 * n + j, :], bank(f"q{l}_{n}", j), ACT.Copy, scale=X_HD ** -0.5).then_inc(evac_a, 1)

                def x_exps(u):
                    v = l * TT + u
                    act.wait_ge(x_maxed, v + 1)
                    if u >= 2:
                        act.wait_ge(x_turned, MT * (v - 1))
                    for r in range(X_HEADS):
                        c0 = (r % 2) * MEM
                        last = nc.scalar.activation(px[:, u % 2, r, :], ps[:, 2 * (u % 2) + r // 2, c0:c0 + MEM], ACT.Exp,
                                                    bias=negmax[:, u % 2, r:r + 1], accum_out=rowsum[:, u % 2, r:r + 1])
                    last.then_inc(x_exped, 1)

                x_exps(0)
                for u in range(TT):
                    if u + 1 < TT:
                        x_exps(u + 1)
                    act.wait_ge(x_turned, MT * (l * TT + u) + 2)
                    nc.scalar.activation(pxT[:, 1, :, u * P:(u + 1) * P], quarter(ps[:, 5, :]), ACT.Copy).then_inc(xpt_a, 1)
                for n in (0, 1):
                    group_filled(act, f"xo{l}_{n}")
                    for j in range(4):
                        nc.scalar.activation(fm_hi[:, 4 * n + j, :], bank(f"xo{l}_{n}", j), ACT.Copy).then_inc(evac_a, 1)
                norm(l, 1)
                if l == 0:
                    keys_evac(1)
                norm_turned(l, 1)
                for n in range(FT // 2):
                    name = f"up{l}_{n}"
                    group_filled(act, name)
                    for j in (0, 1):
                        if n:
                            act.wait_ge(evac_d, DVE_BEFORE[name] - 1 + j)
                        nc.scalar.activation(silu[:, j, :], bank(name, j), ACT.Silu).then_inc(evac_a, 1)
                    for j in (0, 1):
                        i = l * FT + 2 * n + j
                        act.wait_ge(evac_d, DVE_BEFORE[name] + j + 1)
                        nc.scalar.activation(g_hi[:, 2 * n + j, :], gf[:, j, :], ACT.Copy).then_inc(g_hi_ready, 1)
                norm(l, 2)
                if l == 0:
                    values_evac(1)
                    norm_turned(l, 2)

        @block.vector
        def _(dve):
            chain = [0]

            def settle(ins):
                chain[0] += 1
                ins.then_inc(d_chain, 1)
                dve.wait_ge(d_chain, chain[0])

            def low_part(lo, full, hi, done):
                nc.vector.tensor_tensor(lo, full, hi.bitcast(F32), ALU.subtract).then_inc(done, 1)

            def turn_evac(name, hi, lo):
                for j in range(4):
                    dve.wait_ge(evac_a, ACT_BEFORE[name] + j + 1)
                    low_part(fm_target(lo, name, j), quarter(bank(name, j)), fm_target(hi, name, j), evac_d)

            dve.wait_ge(s_consts, 16)
            nc.vector.tensor_copy(ident_b[:, :], consts[:, C_ID:C_ID + P]).then_inc(tables_ready, 1)
            nc.vector.tensor_copy(causal_b[:, :], consts[:, C_CAUSAL:C_CAUSAL + P]).then_inc(tables_ready, 1)
            nc.vector.tensor_copy(cmask_b[:, :, :].rearrange("p t n -> p (t n)"),
                                  consts[:, C_CMASK:C_CMASK + TT * 32]).then_inc(tables_ready, 1)
            nc.vector.memset(pool_sum[:, :, 0:PAD], 0.0)
            nc.vector.memset(pool_in[:, :, 0:PAD], 0.0).then_inc(pads_ready, 1)
            dve.wait_ge(s_pos, 32)
            settle(nc.vector.memset(pos_f[:, :], 0.0))
            nc.vector.tensor_copy(pos_f[:, 0:TT], pos_i[:, 0:TT])
            settle(nc.vector.tensor_copy(pos_f[0:NCMP, TT:TT + 1], pos_i[0:NCMP, TT:TT + 1]))
            settle(nc.vector.tensor_tensor(ang[:, 0, :].rearrange("p (t f) -> p t f", f=HALF),
                                           pos_f[:, :].unsqueeze(2).to_broadcast([P, TT + 1, HALF]),
                                           consts[:, C_INVF:C_INVF + HALF].unsqueeze(1).to_broadcast([P, TT + 1, HALF]), ALU.mult))
            magic = 1.5 * 2.0 ** 23
            settle(nc.vector.tensor_scalar(ang[:, 1, :], ang[:, 0, :], 1.0 / (2.0 * np.pi), magic, ALU.mult, ALU.add))
            settle(nc.vector.tensor_scalar(ang[:, 1, :], ang[:, 1, :], magic, None, ALU.subtract))
            c1 = 6.28125
            c2 = float(np.float32(np.round((2 * np.pi - c1) * 2 ** 20) / 2 ** 20))
            c3 = 2 * np.pi - c1 - c2
            for c in (c1, c2, c3):
                settle(nc.vector.scalar_tensor_tensor(out=ang[:, 0, :], in0=ang[:, 1, :], scalar=-c, in1=ang[:, 0, :],
                                                      op0=ALU.mult, op1=ALU.add))
            edge = 3.1415925
            settle(nc.vector.tensor_scalar(ang[:, 0, :], ang[:, 0, :], edge, -edge, ALU.min, ALU.max))
            settle(nc.vector.scalar_tensor_tensor(out=ang[:, 1, :], in0=ang[:, 0, :], scalar=-1.0, in1=ang[:, 0, :],
                                                  op0=ALU.mult, op1=ALU.max))
            nc.vector.tensor_scalar(ang[:, 1, :], ang[:, 1, :], -1.0, np.pi / 2, ALU.mult, ALU.add).then_inc(ang_ready, 1)

            turn_evac("x0", fm_hi, fm_lo)
            turn_evac("x1", fm_hi, fm_lo)
            dve.wait_ge(evac_a, ACT_AFTER["small"])
            lam = chan[:, V_LAM:V_LAM + RT]
            settle(nc.vector.tensor_scalar(lru_c[:, 0, :], lam, -1.0, None, ALU.mult))
            nc.vector.tensor_tensor(lru_c[:, 0, :], lru_c[:, 0, :], lam, ALU.min).then_inc(sp_ready, 1)
            dve.wait_ge(sp_exp, 1)
            z, w = lru_c[:, 1, :], lru_c[:, 0, :]
            w2, acc = rot_tmp[:, 0, 0:RT], rot_tmp[:, 1, 0:RT]
            settle(nc.vector.tensor_scalar(w, z, 2.0, None, ALU.add))
            settle(nc.vector.reciprocal(w, w))
            settle(nc.vector.tensor_tensor(w, w, z, ALU.mult))
            settle(nc.vector.tensor_tensor(w2, w, w, ALU.mult))
            settle(nc.vector.tensor_scalar(acc, w2, 1.0 / 17, 1.0 / 15, ALU.mult, ALU.add))
            for n in (13, 11, 9, 7, 5, 3, 1):
                settle(nc.vector.tensor_tensor(acc, acc, w2, ALU.mult))
                settle(nc.vector.tensor_scalar(acc, acc, 1.0 / n, None, ALU.add))
            settle(nc.vector.scalar_tensor_tensor(out=acc, in0=acc, scalar=2.0, in1=w, op0=ALU.mult, op1=ALU.mult))
            settle(nc.vector.tensor_scalar(z, lam, -1.0, 0.0, ALU.mult, ALU.max))
            settle(nc.vector.tensor_tensor(acc, acc, z, ALU.add))
            nc.vector.tensor_scalar(lru_c[:, 0, :], acc, 8.0, None, ALU.mult)
            nc.vector.tensor_scalar(lru_c[:, 1, :], acc, -8.0, None, ALU.mult).then_inc(lru_ready, 1)
            dve.wait_ge(lru_ready, 1)

            for g, win in enumerate(WINDOWS):
                dve.wait_ge(evac_a, ACT_BEFORE["ein0"] + g + 1)
                src, sh, n = pool_in[:, g, :], 1, 0
                while sh < win:
                    dst = pool_sum[:, n % 2, :]
                    settle(nc.vector.tensor_tensor(dst[:, PAD:], src[:, PAD:], src[:, PAD - sh:PAD + SEQ - sh], ALU.add))
                    src, sh, n = dst, 2 * sh, n + 1
                u = pool_in[:, g, :]
                settle(nc.vector.tensor_tensor(src[:, PAD:2 * PAD], src[:, PAD:2 * PAD],
                                               consts[:, C_PINV + g * PAD:C_PINV + (g + 1) * PAD], ALU.mult))
                settle(nc.vector.tensor_tensor(u[:, PAD:2 * PAD], src[:, PAD:2 * PAD], u[:, PAD:2 * PAD], ALU.subtract))
                nc.vector.scalar_tensor_tensor(out=u[:, 2 * PAD:], in0=src[:, 2 * PAD:], scalar=1.0 / win, in1=u[:, 2 * PAD:],
                                               op0=ALU.mult, op1=ALU.subtract).then_inc(pooled_ready, 1)
                dve.wait_ge(pooled_ready, g + 1)

            def rotate(x1, x2, cos, sin, tmp, done=None):
                t0, t1, t2 = tmp
                nc.vector.tensor_tensor(t0, x1, sin, ALU.mult)
                nc.vector.tensor_tensor(t1, x2, sin, ALU.mult)
                settle(nc.vector.tensor_tensor(t2, x1, cos, ALU.mult))
                settle(nc.vector.tensor_tensor(x2, x2, cos, ALU.mult))
                nc.vector.tensor_tensor(x1, t2, t1, ALU.subtract)
                last = nc.vector.tensor_tensor(x2, x2, t0, ALU.add)
                if done is None:
                    settle(last)
                else:
                    last.then_inc(done, 1)

            dve.wait_ge(trig_ready, 2)
            dve.wait_ge(evac_a, ACT_AFTER["ein1"])
            for t in range(TT):
                qh = q_tok[:, t, :].rearrange("p (h d) -> p h d", d=HD)
                tmp = [rot_tmp[:, i, t * 64:(t + 1) * 64].rearrange("p (h d) -> p h d", d=HALF) for i in range(3)]
                cs = [trig[:, i, t, :].unsqueeze(1).to_broadcast([P, HEADS, HALF]) for i in (0, 1)]
                rotate(qh[:, :, 0:HALF], qh[:, :, HALF:ROT], cs[0], cs[1], tmp, None if t < TT - 1 else q_ready)
            dve.wait_ge(evac_a, ACT_AFTER["ein2"])
            for b in (0, 1):
                for t in range(TT):
                    kh = kv_tok[:, t, 256 * b:256 * b + P].rearrange("p (g d) -> p g d", d=HD)
                    tmp = [rot_tmp[:, i, (b * TT + t) * 16:(b * TT + t + 1) * 16].rearrange("p (g d) -> p g d", d=HALF) for i in range(3)]
                    cs = [trig[:, i, t, :].unsqueeze(1).to_broadcast([P, KV_HEADS, HALF]) for i in (0, 1)]
                    rotate(kh[:, :, 0:HALF], kh[:, :, HALF:ROT], cs[0], cs[1], tmp)
                for t in range(TT):
                    src = kv_tok[:, t, 256 * b:256 * b + P].rearrange("p (g d) -> p g d", d=HD)
                    last = nc.vector.tensor_copy(kdup[:, b, t, :, 0, :], src)
                    last = nc.vector.tensor_copy(kdup[:, b, t, :, 1, :], src)
                last.then_inc(kdup_ready, 1)
            for n in (0, 1):
                dve.wait_ge(evac_a, ACT_BEFORE["ein3"] + 2 + n)
                for part in (0, 1):
                    c0 = (V_POSK, V_POSV)[n] + part * CMP_STRIDE
                    nc.vector.tensor_tensor(raw_pos[:, n, part, :].rearrange("p (b l) -> p b l", l=CMP_STRIDE),
                                            raw_cmp[:, n, :].rearrange("p (b l) -> p b l", l=CMP_STRIDE),
                                            chan[:, c0:c0 + CMP_STRIDE].unsqueeze(1).to_broadcast([P, SEQ // CMP_STRIDE, CMP_STRIDE]),
                                            ALU.add).then_inc(rawpos_ready, 1)
            for j in range(4):
                dve.wait_ge(evac_a, ACT_BEFORE["mix"] + j + 1)
                nc.vector.scalar_tensor_tensor(out=fm_lo[:, j, :], in0=bank("mix", j), scalar=chan[:, V_PSCALE + j:V_PSCALE + j + 1],
                                               in1=fm_hi[:, j, :].bitcast(F32), op0=ALU.mult, op1=ALU.subtract).then_inc(evac_d, 1)
            dve.wait_ge(evac_a, ACT_BEFORE["cmp"] + 1)
            kc = kc_tok[:, :, :]
            tmp = [rot_tmp[0:NCMP, i, 128:144].rearrange("p (g d) -> p g d", d=HALF) for i in range(3)]
            cs = [trig[0:NCMP, i, TT, :].unsqueeze(1).to_broadcast([NCMP, KV_HEADS, HALF]) for i in (0, 1)]
            rotate(kc[:, :, 0:HALF], kc[:, :, HALF:ROT], cs[0], cs[1], tmp)
            nc.vector.tensor_copy(kc_dup[:, :, 0, :], kc)
            nc.vector.tensor_copy(kc_dup[:, :, 1, :], kc).then_inc(kcdup_ready, 1)

            def row_max(u):
                qb, _, b = UNITS[u]
                n = NCMP if b == "cmp" else (qb + 1) * P
                dve.wait_ge(scored, u + 1)
                if u >= 2:
                    dve.wait_ge(exped, u - 1)
                nc.vector.tensor_reduce(negmax[:, u % 2, :], ps[:, 0:4, :n], AX.X, ALU.max, negate=True).then_inc(maxed, 1)

            dve.wait_ge(evac_a, ACT_AFTER["cmp"])
            added = [0]
            row_max(0)
            for u, (qb, g, b) in enumerate(UNITS):
                dve.wait_ge(exped, u + 1)
                bi = BRANCHES.index(b)
                br = {"cmp": 0, "sel": 1, "win": 2}[b]
                wt = weight[:, u % 2, :]
                settle(nc.vector.reciprocal(wt, rowsum[:, u % 2, :]))
                gt = gates[:, qb, g * GROUP * 3:(g + 1) * GROUP * 3].rearrange("p (r c) -> p r c", c=3)[:, :, br]
                settle(nc.vector.tensor_tensor(wt, wt, gt, ALU.mult))
                if b == "cmp":
                    settle(nc.vector.tensor_scalar(wt, wt, consts[:, C_ROWOK + qb:C_ROWOK + qb + 1], None, ALU.mult))
                if u + 1 < len(UNITS):
                    row_max(u + 1)
                n = NCMP if b == "cmp" else P
                if u:
                    dve.wait_ge(pv_done, u)
                for kb in range(unit_blocks(u)):
                    i = PT_BEFORE[u] + kb
                    if i % 2 == 0:
                        dve.wait_ge(turned, i + 1)
                        nc.vector.tensor_copy(probsT[0:n, kb, :], ps[0:n, 4, :]).then_inc(pt_d, 1)
                dve.wait_ge(pv_done, u + 1)
                o = ps[:, 6 + u % 2, 0:GROUP * HD].rearrange("p (r d) -> p r d", d=HD)
                wb = wt.unsqueeze(2).to_broadcast([P, GROUP, HD])
                dst = o_tok[:, qb, g * 256:(g + 1) * 256]
                if bi == 0:
                    nc.vector.tensor_tensor(dst.rearrange("p (r d) -> p r d", d=HD), o, wb, ALU.mult).then_inc(o_evac, 1)
                    dve.wait_ge(o_evac, u + 1)
                else:
                    nc.vector.tensor_tensor(o_tmp[:, :].rearrange("p (r d) -> p r d", d=HD), o, wb, ALU.mult).then_inc(o_evac, 1)
                    dve.wait_ge(o_evac, u + 1)
                    nc.vector.tensor_tensor(dst, dst, o_tmp[:, :], ALU.add).then_inc(o_ready, 1)
                    added[0] += 1
                    dve.wait_ge(o_ready, added[0])
            for t in range(TT):
                dve.wait_ge(evac_a, ACT_BEFORE["to"] + t + 1)
                low_part(fm_lo[:, 4:8, t * P:(t + 1) * P], quarter(bank("to", t)), fm_hi[:, 4:8, t * P:(t + 1) * P], evac_d)

            def residual(names):
                for n, name in enumerate(names):
                    group_filled(dve, name)
                    for t in range(TT):
                        xs = x_res[:, t, 512 * n:512 * (n + 1)]
                        nc.vector.scalar_tensor_tensor(out=xs, in0=xs, scalar=ALPHA, in1=bank(name, t), op0=ALU.mult,
                                                       op1=ALU.add).then_inc(evac_d, 1)

            def norm(l, i, names):
                v = 3 * l + i
                for t in range(TT):
                    for n in (0, 1):
                        dve.wait_ge(evac_d, DVE_BEFORE[names[n]] + t + 1)
                        last = nc.vector.bn_stats(stats[:, t, n, :], x_res[:, t, 512 * n:512 * (n + 1)])
                settle(last)
                for t in range(TT):
                    last = nc.vector.bn_aggr(mv[:, t, :], stats[:, t, :, :].rearrange("p a b -> p (a b)"))
                settle(last)
                nc.vector.tensor_scalar(lnc[:, 0, :], mv[:, :, 1], EPS, None, ALU.add).then_inc(ln_var, 1)
                dve.wait_ge(ln_sd, v + 1)
                settle(nc.vector.reciprocal(lnc[:, 2, :], lnc[:, 1, :]))
                nc.vector.scalar_tensor_tensor(out=lnc[:, 3, :], in0=mv[:, :, 0], scalar=-1.0, in1=lnc[:, 2, :],
                                               op0=ALU.mult, op1=ALU.mult).then_inc(ln_coef, 1)
                dve.wait_ge(s_lnp, 32 * (v + 1))
                for t in range(TT):
                    dve.wait_ge(ln_norm, TT * v + t + 1)
                    settle(nc.vector.tensor_tensor(x_res[:, t, :], x_res[:, t, :], ln_g[:, :], ALU.mult))
                    nc.vector.tensor_tensor(x_res[:, t, :], x_res[:, t, :], ln_b[:, :], ALU.add).then_inc(x_ready, 1)
                if (l, i) != (DEPTH - 1, 2):
                    turn_evac(f"ln{l}{i}_0", fm_hi, fm_lo)
                    turn_evac(f"ln{l}{i}_1", fm_hi, fm_lo)

            for l in range(DEPTH):
                if l == 0:
                    residual(("eout0", "eout1"))
                    turn_evac("tm", mem_hi, mem_lo)
                    norm(0, 0, ("eout0", "eout1"))
                if l:
                    nc.vector.memset(x_pad[:, :, 0:CONV - 1], 0.0).then_inc(pads_ready, 1)
                    dve.wait_ge(s_posb, 16)
                    settle(nc.vector.tensor_copy(keep[:, :], posb[:, :]))
                    settle(nc.vector.tensor_scalar(keep[:, :], keep[:, :], 0.0, None, ALU.not_equal))

                    def conv(n):
                        first, tiles, name, b = RG_SETS[n]
                        for j in range(tiles):
                            dve.wait_ge(evac_a, ACT_BEFORE[name] + b + j + 1)
                            cw = lambda k: chan[:, V_CONVW + k * RT + first + j:V_CONVW + k * RT + first + j + 1]
                            settle(nc.vector.tensor_scalar(xc[:, j, :], x_pad[:, j, 0:SEQ], cw(0),
                                                           chan[:, V_CONVB + first + j:V_CONVB + first + j + 1], ALU.mult, ALU.add))
                            for k in range(1, CONV):
                                ins = nc.vector.scalar_tensor_tensor(out=xc[:, j, :], in0=x_pad[:, j, k:k + SEQ], scalar=cw(k),
                                                                     in1=xc[:, j, :], op0=ALU.mult, op1=ALU.add)
                                if k < CONV - 1:
                                    settle(ins)
                            ins.then_inc(conv_ready, 1)

                    def lru(n):
                        first, tiles, _, _ = RG_SETS[n]
                        done = sum(s[1] for s in RG_SETS[:n])
                        dve.wait_ge(evac_a, ACT_AFTER[f"ia{n}"])
                        for j in range(tiles):
                            dve.wait_ge(ta_ready, done + j + 1)
                            settle(nc.vector.tensor_tensor(ra[:, j, :], ra[:, j, :], keep[:, :], ALU.mult))
                            settle(nc.vector.tensor_tensor(gg[:, :], ra[:, j, :], ra[:, j, :], ALU.mult))
                            nc.vector.tensor_tensor(ib[:, j, :], ib[:, j, :], xc[:, j, :], ALU.mult)
                            settle(nc.vector.scalar_tensor_tensor(out=tm[:, j, :], in0=keep[:, :], scalar=0.0, in1=tm[:, j, :],
                                                                  op0=ALU.is_equal, op1=ALU.max))
                            nc.vector.scalar_tensor_tensor(out=tm[:, j, :], in0=gg[:, :], scalar=1.0, in1=tm[:, j, :],
                                                           op0=ALU.add, op1=ALU.mult).then_inc(m2_ready, 1)
                            dve.wait_ge(m2_ready, done + j + 1)
                        for j in range(tiles):
                            dve.wait_ge(mult_ready, done + j + 1)
                            settle(nc.vector.tensor_tensor(ib[:, j, :], ib[:, j, :], tm[:, j, :], ALU.mult))
                            nc.vector.tensor_tensor_scan(h[:, first + j, :], ra[:, j, :], ib[:, j, :], 0.0,
                                                         ALU.mult, ALU.add).then_inc(h_ready, 1)
                        dve.wait_ge(h_ready, done + tiles)

                    gates_done = [0]

                    def outputs(n):
                        first, tiles, name = GATE_SETS[n]
                        for j in range(tiles):
                            i = gates_done[0]
                            dve.wait_ge(evac_a, ACT_BEFORE[name] + j + 1)
                            hj = h[:, first + j, :]
                            nc.vector.tensor_tensor(hj, hj, gg[:, :], ALU.mult).then_inc(gg_used, 1)
                            dve.wait_ge(y_hi_ready, i + 1)
                            low_part(y_lo[:, first + j, :], hj, y_hi[:, first + j, :], y_ready)
                            gates_done[0] += 1

                    conv(0)
                    lru(0)
                    conv(1)
                    outputs(0)
                    lru(1)
                    conv(2)
                    outputs(1)
                    lru(2)
                    outputs(2)
                    residual(("oout0", "oout1"))
                    norm(1, 0, ("oout0", "oout1"))

                def x_max(u):
                    dve.wait_ge(x_scored, l * TT + u + 1)
                    s = ps[:, 2 * (u % 2):2 * (u % 2) + 2, :].rearrange("p b (h m) -> p (b h) m", m=MEM)
                    nc.vector.tensor_reduce(negmax[:, u % 2, :], s, AX.X, ALU.max, negate=True).then_inc(x_maxed, 1)

                x_max(0)
                for u in range(TT):
                    v = l * TT + u
                    if u + 1 < TT:
                        if u >= 1:
                            dve.wait_ge(x_exped, v)
                        x_max(u + 1)
                    dve.wait_ge(x_exped, v + 1)
                    wt = weight[:, u % 2, :]
                    settle(nc.vector.reciprocal(wt, rowsum[:, u % 2, :]))
                    nc.vector.tensor_tensor(px[:, u % 2, :, :], px[:, u % 2, :, :], wt.unsqueeze(2).to_broadcast([P, X_HEADS, MEM]),
                                            ALU.mult).then_inc(x_scaled, 1)
                    dve.wait_ge(x_turned, MT * v + 1)
                    nc.vector.tensor_copy(pxT[:, 0, :, u * P:(u + 1) * P], quarter(ps[:, 4, :])).then_inc(xpt_d, 1)
                for n in (0, 1):
                    name = f"xo{l}_{n}"
                    for j in range(4):
                        dve.wait_ge(evac_a, ACT_BEFORE[name] + j + 1)
                        low_part(fm_lo[:, 4 * n + j, :], bank(name, j), fm_hi[:, 4 * n + j, :], evac_d)
                residual((f"wo{l}_0", f"wo{l}_1"))
                norm(l, 1, (f"wo{l}_0", f"wo{l}_1"))
                for n in range(FT // 2):
                    name = f"up{l}_{n}"
                    group_filled(dve, name)
                    for j in (0, 1):
                        i = l * FT + 2 * n + j
                        dve.wait_ge(evac_a, ACT_BEFORE[name] + j + 1)
                        if i >= 2:
                            dve.wait_ge(g_ready, i - 1)
                            dve.wait_ge(g_hi_ready, i - 1)
                        nc.vector.tensor_tensor(gf[:, j, :], silu[:, j, :], bank(name, 2 + j), ALU.mult).then_inc(evac_d, 1)
                    for j in (0, 1):
                        i = l * FT + 2 * n + j
                        dve.wait_ge(g_hi_ready, i + 1)
                        low_part(g_lo[:, 2 * n + j, :], gf[:, j, :], g_hi[:, 2 * n + j, :], g_ready)
                residual((f"dn{l}_0", f"dn{l}_1"))
                norm(l, 2, (f"dn{l}_0", f"dn{l}_1"))


INPUTS = ["x", "mem", "positions", "e_w_in", "e_pool_w", "e_pool_scale", "e_cmp_pos_k", "e_cmp_pos_v", "e_cmp_wk",
          "e_cmp_wv", "e_w_out", "o_w_in", "o_conv_w", "o_conv_b", "o_wa", "o_ba", "o_wx", "o_bx", "o_lambda",
          "o_w_out", "x_wq", "x_wkv", "x_wo", "f_w_up", "f_w_down", "ln_g", "ln_b"]


def kernel(**inputs):
    import concourse.bacc as bacc
    from concourse.bass_utils import run_bass_kernel_spmd

    nc = bacc.Bacc("TRN2", target_bir_lowering=False, num_devices=1)
    arrays, aps = {}, {}
    for name in INPUTS + ["consts"]:
        v = shape_constants() if name == "consts" else np.ascontiguousarray(inputs[name])
        arrays[f"in_{name}"] = v
        aps[name] = nc.dram_tensor(f"in_{name}", v.shape, mybir.dt.from_np(v.dtype), kind="ExternalInput").ap()
    out = nc.dram_tensor("out_x", (1, SEQ, D), F32, kind="ExternalOutput").ap()
    hybrid_trunk(nc, aps, out)
    r = run_bass_kernel_spmd(nc, [arrays], core_ids=[0])
    return r.results[0]["out_x"]
```

```python
from contextlib import ExitStack

import numpy as np

import concourse.bass as bass
from concourse import mybir

F32 = mybir.dt.float32
F32R = mybir.dt.float32r
BF16 = mybir.dt.bfloat16
I32 = mybir.dt.int32
ALU = mybir.AluOpType
ACT = mybir.ActivationFunctionType
AX = mybir.AxisListType

P = 128
D = 1024
KT = D // P
SEQ = 512
TT = SEQ // P
MEM = 256
MT = MEM // P
DEPTH = 2
ALPHA = (2.0 * DEPTH) ** 0.25
EPS = 1e-5
NEG = -1e30
WINDOWS = (2, 4, 8, 16)
HEADS, KV_HEADS, HD = 8, 2, 64
GROUP = HEADS // KV_HEADS
GATES = HEADS * 3
CMP_BLOCK, CMP_STRIDE = 32, 16
NCMP = (SEQ - CMP_BLOCK) // CMP_STRIDE + 1
ROT = HD // 4
HALF = ROT // 2
RNN = 1280
RT = RNN // P
X_HEADS, X_HD = 4, D // 4
FFN = 2816
FT = FFN // P
PAD = 16
CONV = 4
COLS = 512
BANK = 512
RING = 4

C_ID = 0
C_CAUSAL = C_ID + P
C_PINV = C_CAUSAL + P
C_INVF = C_PINV + 4 * PAD
C_CMASK = C_INVF + HALF
C_ROWOK = C_CMASK + TT * 32
C_SEL = C_ROWOK + TT
C_LOW = C_SEL + KT
C_END = C_LOW + 2

V_POSK, V_POSV = 0, CMP_BLOCK
V_PSCALE = 2 * CMP_BLOCK
V_CONVW = V_PSCALE + 4
V_CONVB = V_CONVW + CONV * RT
V_BA = V_CONVB + RT
V_BX = V_BA + RT
V_LAM = V_BX + RT
V_END = V_LAM + RT

E_Q = 512
E_GATE = 1024
E_KV = E_GATE + GATES
E_KS = E_KV + 256


def shape_constants():
    c = np.zeros((P, C_END), np.float32)
    c[:, C_ID:C_ID + P] = np.eye(P)
    q, k = np.arange(P)[:, None], np.arange(P)[None, :]
    c[:, C_CAUSAL:C_CAUSAL + P] = np.where(k <= q, 0.0, NEG)
    for g, w in enumerate(WINDOWS):
        c[:, C_PINV + g * PAD:C_PINV + (g + 1) * PAD] = 1.0 / np.minimum(np.arange(PAD) + 1, w)
    c[:, C_INVF:C_INVF + HALF] = np.float32(500000.0) ** (-np.arange(HALF, dtype=np.float32) * np.float32(2.0) / np.float32(ROT))
    for t in range(TT):
        ends = np.arange(32) * CMP_STRIDE + CMP_BLOCK - 1
        tok = t * P + np.arange(P)
        c[:, C_CMASK + t * 32:C_CMASK + (t + 1) * 32] = np.where(ends[None, :] <= tok[:, None], 0.0, NEG)
        c[:, C_ROWOK + t] = tok >= CMP_BLOCK - 1
    row = np.arange(P)
    c[:, C_SEL:C_SEL + KT] = row[:, None] % KT == np.arange(KT)
    c[:, C_LOW] = row // KT % 2
    c[:, C_LOW + 1] = 1 - 2 * c[:, C_LOW]
    return c


def plan_groups():
    g = [("x0", 0, 4, 4), ("x1", 0, 4, 4), ("small", 0, 1, 0)]
    g += [("ein0", KT, 4, 0), ("tm", 0, 4, 4), ("ein1", KT, 4, 0), ("ein2", KT, 4, 0), ("ein3", KT, 3, 0)]
    g += [("mix", 0, 4, 4), ("tq", 0, 4, 0), ("tk", 0, 4, 0), ("cmp", 0, 3, 0), ("tkc", 0, 2, 0)]
    g += [("attn", 0, 0, 0), ("to", 0, 4, 4)]
    g += [("eout0", KT, 0, 4), ("eout1", KT, 0, 4)]
    g += [("k0_0", KT, 4, 0), ("k0_1", KT, 4, 0), ("v0_0", KT, 2, 0), ("v0_1", KT, 2, 0)]
    for l in range(DEPTH):
        if l:
            g += [("oin0", KT, 4, 0), ("oin1", KT, 4, 0), ("ra0", 0, 4, 0), ("ia0", 0, 4, 0)]
            g += [("oin2", KT, 4, 0), ("ra1", 0, 4, 0), ("ia1", 0, 4, 0)]
            g += [("oin3", KT, 4, 0), ("ra2", 0, 4, 0), ("oin4", KT, 4, 0)]
            g += [("oout0", RT, 0, 4), ("oout1", RT, 0, 4)]
        g += [(f"ln{l}0_0", 0, 4, 4), (f"ln{l}0_1", 0, 4, 4)]
        g += [(f"q{l}_0", KT, 4, 0), (f"q{l}_1", KT, 4, 0), (f"xattn{l}", 0, 0, 0)]
        g += [(f"xo{l}_0", 0, 4, 4), (f"xo{l}_1", 0, 4, 4)]
        g += [(f"wo{l}_0", KT, 0, 4), (f"wo{l}_1", KT, 0, 4)]
        if l == 0:
            g += [("k1_0", KT, 4, 0), ("k1_1", KT, 4, 0)]
        g += [(f"ln{l}1_0", 0, 4, 4), (f"ln{l}1_1", 0, 4, 4)]
        g += [(f"up{l}_{n}", KT, 2, 2) for n in range(FT // 2)]
        g += [(f"dn{l}_0", FT, 0, 4), (f"dn{l}_1", FT, 0, 4)]
        if l == 0:
            g += [("v1_0", KT, 2, 0), ("v1_1", KT, 2, 0)]
            g += [("ln02_0", 0, 4, 4), ("ln02_1", 0, 4, 4)]
    return g


PLAN = plan_groups()
INDEX = {name: i for i, (name, _, _, _) in enumerate(PLAN)}
CHUNK0 = {name: sum(k for _, k, _, _ in PLAN[:i]) for name, i in INDEX.items()}
ACT_BEFORE = {name: sum(a for _, _, a, _ in PLAN[:i]) for name, i in INDEX.items()}
DVE_BEFORE = {name: sum(v for _, _, _, v in PLAN[:i]) for name, i in INDEX.items()}
ACT_AFTER = {name: ACT_BEFORE[name] + PLAN[i][2] for name, i in INDEX.items()}
DVE_AFTER = {name: DVE_BEFORE[name] + PLAN[i][3] for name, i in INDEX.items()}
RG_SETS = [(6, 4, "oin0", 0), (2, 4, "oin1", 0), (0, 2, "oin2", 2)]
GATE_SETS = [(8, 2, "oin2"), (4, 4, "oin3"), (0, 4, "oin4")]
Y_ORDER = [first + j for first, tiles, _ in GATE_SETS for j in range(tiles)]
OIN_COL = [2048, 1536, 1024, 512, 0]
BRANCHES = ("sel", "win", "cmp")
UNIT_HEADS = [8, 4, 2, 2]
UNITS = [u for qb in range(TT) for u in
         [(qb, "cmp", 0, HEADS)] + [(qb, b, hh, UNIT_HEADS[qb]) for b in ("sel", "win")
                                    for hh in range(0, HEADS, UNIT_HEADS[qb])]]
GATE_OF = {"cmp": 0, "sel": 1, "win": 2}


def unit_width(u):
    return 32 if UNITS[u][1] == "cmp" else (UNITS[u][0] + 1) * P


def unit_blocks(u):
    qb, b, _, heads = UNITS[u]
    return [(kb, r) for kb in range(1 if b == "cmp" else qb + 1) for r in range(heads)]


PT_BEFORE = [sum((len(unit_blocks(v)) + 3) // 4 for v in range(u)) for u in range(len(UNITS) + 1)]


def hybrid_trunk(nc, a, out):
    ctx = ExitStack()
    with ctx:
        def at(name, shape, dt, offset):
            return nc.alloc_sbuf_tensor_at(name, shape, dt, offset=offset)

        cur = [16512]

        def place(name, shape, dt):
            n = int(np.prod(shape[1:])) * mybir.dt.size(dt)
            o = cur[0]
            cur[0] += (n + 31) // 32 * 32
            return at(name, shape, dt, o), o

        x_res, _ = place("x_res", [P, TT, D], F32)
        fm_hi, _ = place("fm_hi", [P, KT, SEQ], F32R)
        fm_lo, _ = place("fm_lo", [P, KT, SEQ], F32R)
        w_raw, _ = place("w_raw", [P, RING, COLS], F32)
        w_hi, _ = place("w_hi", [P, RING, COLS], F32R)
        w_lo, _ = place("w_lo", [P, RING, COLS], F32R)
        k_mem, _ = place("k_mem", [P, KT, MEM], F32)
        v_mem, o_v = place("v_mem", [P, MT, D], F32)
        consts, _ = place("consts", [P, C_END], F32)
        chan, _ = place("chan", [P, V_END], F32)
        ident_b, _ = place("ident_b", [P, P], BF16)
        causal_b, _ = place("causal_b", [P, P], BF16)
        cmask_b, _ = place("cmask_b", [P, TT, 32], BF16)
        stats, _ = place("stats", [P, TT, 2, 6], F32)
        mv, _ = place("mv", [P, TT, 2], F32)
        lnc, _ = place("lnc", [P, 4, TT], F32)
        negmax, _ = place("negmax", [P, 2, HEADS], F32)
        rowsum, _ = place("rowsum", [P, 2, HEADS], F32)
        weight, _ = place("weight", [P, 2, HEADS], F32)
        gates, _ = place("gates", [P, TT, GATES], F32)
        kcT, _ = place("kcT", [P, KV_HEADS, NCMP], F32)
        vc_tok, _ = place("vc_tok", [NCMP, KV_HEADS * HD], F32)
        trig, _ = place("trig", [P, 2, TT + 1, HALF], F32)
        lru_c, _ = place("lru_c", [P, 2, RT], F32)
        bias_sel, _ = place("bias_sel", [2 * KT, KT], F32R)
        ln_g, o_ln = place("ln_g", [P, D], F32)
        ln_b, _ = place("ln_b", [P, D], F32)
        bias_raw, _ = place("bias_raw", [2 * KT, P], F32)
        bias_hi, _ = place("bias_hi", [2 * KT, P], F32R)
        bias_rows, _ = place("bias_rows", [2 * KT, P], F32R)
        cur[0] = o_ln + 10 * 2 * P * 4
        m0 = cur[0]
        mem_hi, _ = place("mem_hi", [P, KT, MEM], F32R)
        mem_lo, _ = place("mem_lo", [P, KT, MEM], F32R)
        G = cur[0]
        g_hi = at("g_hi", [P, FT, SEQ], F32R, G)
        g_lo = at("g_lo", [P, FT, SEQ], F32R, G + FT * SEQ * 4)
        assert G + 2 * FT * SEQ * 4 <= 229344, G + 2 * FT * SEQ * 4
        q_tok = at("q_tok", [P, TT, 512], F32, G)
        kv_tok = at("kv_tok", [P, TT, 512], F32, G + 8192)
        qT = at("qT", [P, TT, SEQ], F32, G + 16384)
        kT = at("kT", [P, 2, KV_HEADS, SEQ], F32, G + 24576)
        kdup = at("kdup", [P, 2, TT, KV_HEADS, 2, HD], F32, G + 32768)
        probs = at("probs", [P, 2, 2 * SEQ], F32, G + 40960)
        raw_cmp = at("raw_cmp", [P, 2, SEQ], F32, G + 40960)
        raw_pos = at("raw_pos", [P, 2, 2, SEQ], F32, G + 45056)
        kc_tok = at("kc_tok", [NCMP, KV_HEADS, HD], F32, G)
        kc_dup = at("kc_dup", [NCMP, KV_HEADS, 2, HD], F32, G + 512)
        rot_tmp = at("rot_tmp", [P, 3, TT * HEADS * HALF], F32, G + 53248)
        probsT = at("probsT", [P, 2, 2 * TT, P], F32, G + 57344)
        o_tok = at("o_tok", [P, TT, 512], F32, G + 65536)
        pool_in = at("pool_in", [P, 4, PAD + SEQ], F32, G + 57344)
        pool_sum = at("pool_sum", [P, 2, PAD + SEQ], F32, G + 65792)
        gateT = at("gateT", [GATES, SEQ], F32, G + 70016)
        cmp_w = at("cmp_w", [P, 2, CMP_BLOCK, HD], F32, G + 73728)
        o_tmp = at("o_tmp", [P, HEADS * HD], F32, G + 73728)
        pool_w = at("pool_w", [P, 4, P], F32, G + 24576)
        mem_tok = at("mem_tok", [P, MT, D], F32, G)
        rows_posk = at("rows_posk", [CMP_BLOCK, 2, HD], F32, G + 8192)
        rows_posv = at("rows_posv", [CMP_BLOCK, 2, HD], F32, G + 8704)
        rows_ps = at("rows_ps", [4, P], F32, G + 9216)
        rows_rg = at("rows_rg", [V_END - V_CONVW, P], F32, G + 9728)
        pos_i = at("pos_i", [P, TT + 1], I32, G + 16384)
        pos_f = at("pos_f", [P, TT + 1], F32, G + 16416)
        ang = at("ang", [P, 4, (TT + 1) * HALF], F32, G + 16448)
        q_x = at("q_x", [P, KT, SEQ], F32, G)
        px = at("px", [P, 2, X_HEADS, MEM], F32, G + 16384)
        pxT = at("pxT", [P, MT, X_HEADS, SEQ], F32, G + 24576)
        silu = at("silu", [P, 2, SEQ], F32, o_v)
        gf = at("gf", [P, 2, SEQ], F32, o_v + 4096)
        R = m0
        x_pad = at("x_pad", [P, 2, 4, CONV - 1 + SEQ], F32, R)
        ra = at("ra", [P, 4, SEQ], F32, R + 16512)
        ib = at("ib", [P, 4, SEQ], F32, R + 16512 + 8192)
        tm = at("tm", [P, 4, SEQ], F32, R + 16512 + 2 * 8192)
        h = at("h", [P, RT, SEQ], F32, R + 16512 + 3 * 8192)
        y_hi = at("y_hi", [P, RT, SEQ], F32R, R + 61568)
        y_lo = at("y_lo", [P, RT, SEQ], F32R, R + 82048)
        gelu = at("gelu", [P, RT, SEQ], F32, R + 61568)
        ra_alt = at("ra_alt", [P, 4, SEQ], F32, R + 82048)
        ib_alt = at("ib_alt", [P, 4, SEQ], F32, R + 82048 + 8192)
        RA, IB = (ra, ra_alt, ra), (ib, ib_alt, ib)
        a_sq = at("a_sq", [P, SEQ], F32, R + 102528)
        w_gates = at("w_gates", [P, 2, RT, P], F32, o_ln)
        keep = at("keep", [P, SEQ], F32, R + 104576)
        posb = at("posb", [P, SEQ], I32, R + 82048)
        assert R + 104576 + 2048 <= 229344, R + 106624

        ps = ctx.enter_context(nc.psum_tensor("ps", [P, 8, BANK], F32))

        def sem(name):
            return ctx.enter_context(nc.semaphore(name))

        w_landed = [sem(f"w_landed{i}") for i in range(RING)]
        s_x = [sem(f"s_x{t}") for t in range(TT)]
        s_consts, s_mem, s_rows, s_pos = sem("s_consts"), sem("s_mem"), sem("s_rows"), sem("s_pos")
        s_cmpw, s_poolw, s_lnp, s_wgates, s_posb = sem("s_cmpw"), sem("s_poolw"), sem("s_lnp"), sem("s_wgates"), sem("s_posb")
        s_out = sem("s_out")
        w_rounded, w_split, w_used = sem("w_rounded"), sem("w_split"), sem("w_used")
        filled = sem("filled")
        evac_a, evac_d = sem("evac_a"), sem("evac_d")
        a_chain, d_chain = sem("a_chain"), sem("d_chain")
        tables_ready, cols_ready = sem("tables_ready"), sem("cols_ready")
        ang_ready, trig_ready = sem("ang_ready"), sem("trig_ready")
        pooled_ready, q_ready, kdup_ready, rawpos_ready = sem("pooled_ready"), sem("q_ready"), sem("kdup_ready"), sem("rawpos_ready")
        kcdup_ready = sem("kcdup_ready")
        scored, maxed, exped = sem("scored"), sem("maxed"), sem("exped")
        turned, pt_d, summed, pv_done, o_evac, o_ready = sem("turned"), sem("pt_d"), sem("summed"), sem("pv_done"), sem("o_evac"), sem("o_ready")
        x_scored, x_maxed, x_exped, x_scaled = sem("x_scored"), sem("x_maxed"), sem("x_exped"), sem("x_scaled")
        x_turned, xpt_d, xpt_a = sem("x_turned"), sem("xpt_d"), sem("xpt_a")
        ln_var, ln_sd, ln_coef, x_ready = sem("ln_var"), sem("ln_sd"), sem("ln_coef"), sem("x_ready")
        tile_turned, x_whole, x_whole_pool = sem("tile_turned"), sem("x_whole"), sem("x_whole_pool")
        bias_ready = sem("bias_ready")
        g_hi_ready, g_ready = sem("g_hi_ready"), sem("g_ready")
        conv_ready, ta_ready, m2_ready, mult_ready, h_ready = sem("conv_ready"), sem("ta_ready"), sem("m2_ready"), sem("mult_ready"), sem("h_ready")
        y_full, y_hi_ready, y_ready = sem("y_full"), sem("y_hi_ready"), sem("y_ready")
        sp_ready, sp_exp, lru_ready, pads_ready, keep_ready = sem("sp_ready"), sem("sp_exp"), sem("lru_ready"), sem("pads_ready"), sem("keep_ready")
        

        block = ctx.enter_context(nc.Block())

        ident = consts[:, C_ID:C_ID + P]

        def chunk_sources():
            def rows(w, k, cols, n):
                return [(w[k * P:(k + 1) * P, cols:cols + n], 0, n)]
            for name, steps, _, _ in PLAN:
                for k in range(steps):
                    kind, n = name.split("_")[0], int(name.split("_")[1]) if "_" in name else 0
                    if name in ("ein0", "ein1"):
                        yield rows(a["e_w_in"][0], k, 512 * int(name[3]), 512)
                    elif name == "ein2":
                        yield rows(a["e_w_in"][0], k, E_KS, 512)
                    elif name == "ein3":
                        yield rows(a["e_w_in"][0], k, E_GATE, GATES + 256)
                    elif name[:4] == "eout":
                        yield rows(a["e_w_out"][0], k, 512 * int(name[4]), 512)
                    elif name[:4] == "oout":
                        yield rows(a["o_w_out"][0], Y_ORDER[k], 512 * int(name[4]), 512)
                    elif name[:3] == "oin":
                        yield rows(a["o_w_in"][0], k, OIN_COL[int(name[3])], 512)
                    elif kind[0] == "k":
                        yield rows(a["x_wkv"][int(kind[1])], k, 512 * n, 512)
                    elif kind[0] == "v":
                        yield rows(a["x_wkv"][int(kind[1])], k, D + 512 * n, 512)
                    elif kind[0] == "q":
                        yield rows(a["x_wq"][int(kind[1])], k, 512 * n, 512)
                    elif kind[:2] == "wo":
                        yield rows(a["x_wo"][int(kind[2])], k, 512 * n, 512)
                    elif kind[:2] == "dn":
                        yield rows(a["f_w_down"][int(kind[2])], k, 512 * n, 512)
                    else:
                        assert kind[:2] == "up", name
                        w = a["f_w_up"][int(kind[2])]
                        yield [(w[k * P:(k + 1) * P, 256 * n:256 * n + 256], 0, 256),
                               (w[k * P:(k + 1) * P, FFN + 256 * n:FFN + 256 * n + 256], 256, 256)]

        CHUNKS = list(chunk_sources())
        LANDS = [0] * RING
        LANDED = []
        for c, pieces in enumerate(CHUNKS):
            LANDS[c % RING] += 16 * len(pieces)
            LANDED.append(LANDS[c % RING])
        WIDTH = [sum(n for _, _, n in pieces) for pieces in CHUNKS]

        TURNED = {}
        for name, steps, na, nd in PLAN:
            if steps == 0 and "attn" not in name and name[:2] != "ln":
                TURNED[name] = len(TURNED) + 1

        @block.sync
        def _(sp):
            sp.dma_start(consts[:, :], a["consts"]).then_inc(s_consts, 16)
            for t in range(TT):
                sp.dma_start(x_res[:, t, :], a["x"][0, t * P:(t + 1) * P, :]).then_inc(s_x[t], 16)
            sp.dma_start(pos_i[:, 0:TT], a["positions"][0].rearrange("(t p) -> p t", p=P),
                         allow_slow_non_contiguous=True).then_inc(s_pos, 16)
            sp.dma_start(pos_i[0:NCMP, TT:TT + 1],
                         a["positions"][0, CMP_BLOCK - 1:SEQ].rearrange("(n o) -> n o", o=1)[::CMP_STRIDE, :],
                         allow_slow_non_contiguous=True).then_inc(s_pos, 16)
            sp.dma_start(rows_posk[:, 0, :], a["e_cmp_pos_k"][0]).then_inc(s_rows, 16)
            sp.dma_start(rows_posk[:, 1, :], a["e_cmp_pos_k"][0]).then_inc(s_rows, 16)
            sp.dma_start(rows_posv[:, 0, :], a["e_cmp_pos_v"][0]).then_inc(s_rows, 16)
            sp.dma_start(rows_posv[:, 1, :], a["e_cmp_pos_v"][0]).then_inc(s_rows, 16)
            sp.dma_start(rows_ps[:, :], a["e_pool_scale"][0].rearrange("(g p) -> g p", p=P)).then_inc(s_rows, 16)
            for n in range(CONV):
                sp.dma_start(rows_rg[n * RT:(n + 1) * RT, :],
                             a["o_conv_w"][0, n].rearrange("(j p) -> j p", p=P)).then_inc(s_rows, 16)
            for n, name in enumerate(("o_conv_b", "o_ba", "o_bx", "o_lambda")):
                sp.dma_start(rows_rg[(CONV + n) * RT:(CONV + n + 1) * RT, :],
                             a[name][0].rearrange("(j p) -> j p", p=P)).then_inc(s_rows, 16)

            def weights(first, last):
                for c in range(first, last):
                    if c >= RING:
                        sp.wait_ge(w_split, c - RING + 1)
                    for src, o, n in CHUNKS[c]:
                        sp.dma_start(w_raw[:, c % RING, o:o + n], src).then_inc(w_landed[c % RING], 16)

            def ln_params(l, i):
                sp.dma_start(ln_g[:, :], a["ln_g"][l, i].partition_broadcast(P)).then_inc(s_lnp, 16)
                sp.dma_start(ln_b[:, :], a["ln_b"][l, i].partition_broadcast(P)).then_inc(s_lnp, 16)
                for half in (0, 1):
                    sp.dma_start(bias_raw[half * KT:(half + 1) * KT, :],
                                 a["ln_b"][l, i].rearrange("(k p) -> k p", p=P)).then_inc(s_lnp, 16)

            weights(0, RING)
            sp.dma_start(mem_tok[:, :, :], a["mem"][0].rearrange("(t p) d -> p t d", p=P)).then_inc(s_mem, 16)
            weights(RING, CHUNK0["ein1"])
            for half in (0, 1):
                for n, name in enumerate(("e_cmp_wk", "e_cmp_wv")):
                    sp.dma_start(cmp_w[half * HD:(half + 1) * HD, n, :, :],
                                 a[name][0].rearrange("(l d) e -> d l e", d=HD)).then_inc(s_cmpw, 16)
            sp.dma_start(pool_w[:, :, :], a["e_pool_w"][0].rearrange("g c d -> c g d")).then_inc(s_poolw, 16)
            ln_params(0, 0)
            weights(CHUNK0["ein1"], CHUNK0["k0_0"])
            weights(CHUNK0["k0_0"], CHUNK0["q0_1"])
            sp.wait_ge(x_whole, TT * 1)
            ln_params(0, 1)
            weights(CHUNK0["q0_1"], CHUNK0["up0_1"])
            sp.wait_ge(x_whole, TT * 2)
            ln_params(0, 2)
            weights(CHUNK0["up0_1"], CHUNK0["oin1"])
            sp.wait_ge(x_whole, TT * 3)
            sp.dma_start(w_gates[:, 0, :, :], a["o_wa"][0].rearrange("h i j -> i h j")).then_inc(s_wgates, 16)
            sp.dma_start(w_gates[:, 1, :, :], a["o_wx"][0].rearrange("h i j -> i h j")).then_inc(s_wgates, 16)
            sp.dma_start(posb[:, :], a["positions"][0].partition_broadcast(P)).then_inc(s_posb, 16)
            weights(CHUNK0["oin1"], CHUNK0["oout0"])
            sp.wait_ge(filled, TURNED["ra2"])
            ln_params(1, 0)
            weights(CHUNK0["oout0"], CHUNK0["q1_1"])
            sp.wait_ge(x_whole, TT * 4)
            ln_params(1, 1)
            weights(CHUNK0["q1_1"], CHUNK0["up1_1"])
            sp.wait_ge(x_whole, TT * 5)
            ln_params(1, 2)
            weights(CHUNK0["up1_1"], len(CHUNKS))
            for t in range(TT):
                if t < TT - 1:
                    sp.wait_ge(x_whole_pool, t + 1)
                else:
                    sp.wait_ge(x_whole, TT * 5 + 1)
                sp.dma_start(out[0, t * P:(t + 1) * P, :], x_res[:, t, :]).then_inc(s_out, 16)
            sp.wait_ge(s_out, 16 * TT)

        @block.gpsimd
        def _(pool):
            for c in range(len(CHUNKS)):
                s, n = c % RING, WIDTH[c]
                pool.wait_ge(w_rounded, c + 1)
                nc.gpsimd.tensor_tensor(w_lo[:, s, :n], w_raw[:, s, :n], w_hi[:, s, :n].bitcast(F32),
                                        ALU.subtract).then_inc(w_split, 1)
            pool.wait_ge(s_lnp, 64 * 3 * DEPTH)
            for t in range(TT - 1):
                pool.wait_ge(x_ready, TT * (3 * DEPTH - 1) + t + 1)
                nc.gpsimd.tensor_tensor(x_res[:, t, :], x_res[:, t, :], ln_b[:, :], ALU.add).then_inc(x_whole_pool, 1)

        def group_filled(eng, name):
            if PLAN[INDEX[name]][1]:
                eng.wait_ge(w_used, CHUNK0[name] + PLAN[INDEX[name]][1])
            else:
                eng.wait_ge(filled, TURNED[name])

        def probs_of(u, r):
            n = unit_width(u)
            return probs[:, u % 2, r * n:(r + 1) * n]

        def bank(name, j):
            return ps[:, 4 * (INDEX[name] % 2) + j, :]

        def fm_target(tile_hi, name, j):
            t, k = 2 * int(name[-1] if name != "tm" else 0) + j // 2, 4 * (j % 2)
            return tile_hi[:, k:k + 4, t * P:(t + 1) * P]

        def quarter(p):
            return p.rearrange("p (k s) -> p k s", s=P)

        @block.tensor
        def _(pe):
            def begin(name):
                i = INDEX[name]
                if i >= 2:
                    before = PLAN[i - 2][0]
                    evacuated(before)
                return 4 * (i % 2)

            def evacuated(name):
                if ACT_AFTER[name]:
                    pe.wait_ge(evac_a, ACT_AFTER[name])
                if DVE_AFTER[name]:
                    pe.wait_ge(evac_d, DVE_AFTER[name])

            def passes(outp, k, steps, w, x, w_first):
                for n, (i, j) in enumerate(((0, 0), (0, 1), (1, 0))):
                    lhsT, rhs = (w[i], x[j]) if w_first else (x[j], w[i])
                    last = nc.tensor.matmul(outp, lhsT, rhs, start=(k == 0 and n == 0),
                                            stop=(k == steps - 1 and n == 2))
                return last

            def turn(out_, in_, n=P):
                return nc.tensor.transpose(out_, in_, ident[0:n, 0:n])

            def turn_tokens(name, tok, tiles):
                b0 = begin(name)
                for i, t in enumerate(tiles):
                    for k in range(KT):
                        last = turn(ps[:, b0 + 2 * i + k // 4, (k % 4) * P:(k % 4 + 1) * P], tok[:, t, k * P:(k + 1) * P])
                last.then_inc(filled, 1)

            fm = (fm_hi, fm_lo)
            mem = (mem_hi, mem_lo)

            def product(name, act, tokens, feature_major, col0=(0, P, 2 * P, 3 * P), ready=None, order=None):
                b0, steps = begin(name), PLAN[INDEX[name]][1]
                hi, lo = act
                for k in range(steps):
                    c = CHUNK0[name] + k
                    s, n = c % RING, WIDTH[c]
                    pe.wait_ge(w_split, c + 1)
                    if ready:
                        ready(k)
                    kk = order[k] if order else k
                    nb = len(col0) if feature_major else tokens // P
                    for j in range(nb):
                        if feature_major:
                            w = [w_[:, s, col0[j]:col0[j] + P] for w_ in (w_hi, w_lo)]
                            last = passes(ps[:, b0 + j, :tokens], k, steps, w, (hi[:, kk, :], lo[:, kk, :]), True)
                        else:
                            x = [x_[:, kk, j * P:(j + 1) * P] for x_ in (hi, lo)]
                            last = passes(ps[:, b0 + j, :n], k, steps, (w_hi[:, s, :n], w_lo[:, s, :n]), x, False)
                    last.then_inc(w_used, 1)

            pe.wait_ge(s_consts, 16)
            pe.wait_ge(s_x[0], 16)
            pe.wait_ge(s_x[1], 16)
            turn_tokens("x0", x_res, (0, 1))
            pe.wait_ge(s_x[2], 16)
            pe.wait_ge(s_x[3], 16)
            turn_tokens("x1", x_res, (2, 3))
            b0 = begin("small")
            pe.wait_ge(s_rows, 16 * (5 + CONV + 4))
            turn(ps[:, b0, V_POSK:V_POSK + CMP_BLOCK], rows_posk[:, :, :].rearrange("l a d -> l (a d)"), CMP_BLOCK)
            turn(ps[:, b0, V_POSV:V_POSV + CMP_BLOCK], rows_posv[:, :, :].rearrange("l a d -> l (a d)"), CMP_BLOCK)
            turn(ps[:, b0, V_PSCALE:V_PSCALE + 4], rows_ps[:, :], 4)
            turn(ps[:, b0, V_CONVW:V_END], rows_rg[:, :], V_END - V_CONVW).then_inc(filled, 1)

            evacuated("x1")
            product("ein0", fm, SEQ, True)
            pe.wait_ge(s_mem, 16)
            turn_tokens("tm", mem_tok, (0, 1))
            product("ein1", fm, SEQ, False)
            product("ein2", fm, SEQ, False)
            product("ein3", fm, SEQ, True, (0, GATES, GATES + P))
            b0 = begin("mix")
            pe.wait_ge(s_poolw, 16)
            pe.wait_ge(pooled_ready, 4)
            for g in range(4):
                last = nc.tensor.matmul(ps[:, b0 + g, :], pool_w[:, g, :], pool_in[:, g, PAD:], start=True, stop=True)
            last.then_inc(filled, 1)
            b0 = begin("tq")
            pe.wait_ge(q_ready, 1)
            for j in range(4):
                for t in range(TT):
                    last = turn(ps[:, b0 + j, t * P:(t + 1) * P], q_tok[:, t, j * P:(j + 1) * P])
            last.then_inc(filled, 1)
            b0 = begin("tk")
            pe.wait_ge(kdup_ready, 2)
            for b in (0, 1):
                for g in range(KV_HEADS):
                    for t in range(TT):
                        last = turn(ps[:, b0 + 2 * b + g, t * P:(t + 1) * P],
                                    kdup[:, b, t, g, :, :].rearrange("p a d -> p (a d)"))
            last.then_inc(filled, 1)
            b0 = begin("cmp")
            pe.wait_ge(rawpos_ready, 4)
            pe.wait_ge(s_cmpw, 64)
            for n in (0, 1):
                for g in range(KV_HEADS):
                    half = slice(g * HD, (g + 1) * HD)
                    for l in range(CMP_BLOCK):
                        src = raw_pos[half, n, l // CMP_STRIDE, l:l + (NCMP - 1) * CMP_STRIDE + 1:CMP_STRIDE]
                        nc.tensor.matmul(ps[0:NCMP, b0 + g, n * HD:(n + 1) * HD], src, cmp_w[half, n, l, :],
                                         start=(l == 0), stop=(l == CMP_BLOCK - 1))
            for t in range(TT):
                last = turn(ps[:, b0 + 2, t * GATES:(t + 1) * GATES], gateT[:, t * P:(t + 1) * P], GATES)
            last.then_inc(filled, 1)
            b0 = begin("tkc")
            pe.wait_ge(kcdup_ready, 1)
            for g in range(KV_HEADS):
                last = turn(ps[:, b0 + g, 0:NCMP], kc_dup[:, g, :, :].rearrange("p a d -> p (a d)"), NCMP)
            last.then_inc(filled, 1)

            evacuated("tkc")
            pe.wait_ge(tables_ready, 3)

            def scores(u):
                qb, b, h0, heads = UNITS[u]
                b0 = 2 * (u % 2)
                if b == "cmp":
                    for i in (0, 1):
                        nc.tensor.matmul(ps[:, b0 + i, 0:P].rearrange("p (r n) -> p r n", n=32)[:, :, 0:NCMP], ident_b[:, :],
                                         cmask_b[:, qb, 0:NCMP].unsqueeze(1).to_broadcast([P, HEADS // 2, NCMP]),
                                         start=True, stop=False, skip_group_check=True)
                for hh in range(h0, h0 + heads):
                    half = slice((hh % 2) * HD, (hh % 2 + 1) * HD)
                    c0 = (hh - h0) // 2 * unit_width(u)
                    q, g, bank_ = qT[half, hh // 2, qb * P:(qb + 1) * P], hh // GROUP, b0 + hh % 2
                    if b == "cmp":
                        last = nc.tensor.matmul(ps[:, bank_, c0:c0 + NCMP], q, kcT[half, g, :], start=False, stop=True,
                                                skip_group_check=True)
                    else:
                        n = (qb + 1) * P
                        nc.tensor.matmul(ps[:, bank_, c0:c0 + n], q, kT[half, BRANCHES.index(b), g, :n], start=True, stop=False,
                                         skip_group_check=True)
                        last = nc.tensor.matmul(ps[:, bank_, c0 + qb * P:c0 + n], ident_b[:, :], causal_b[:, :], start=False,
                                                stop=True, skip_group_check=True)
                last.then_inc(scored, 1)

            def turn_probs(u):
                qb, b, h0, heads = UNITS[u]
                pe.wait_ge(exped, u + 1)
                blocks = unit_blocks(u)
                n = NCMP if b == "cmp" else P
                for j in range(0, len(blocks), 4):
                    i = PT_BEFORE[u] + j // 4
                    if i >= 2:
                        pe.wait_ge(pt_d, i - 1)
                    for jj, (kb, r) in enumerate(blocks[j:j + 4]):
                        p = probs_of(u, r)[:, kb * P:kb * P + n]
                        last = nc.tensor.matmul(ps[0:n, 4 + i % 2, jj * P:(jj + 1) * P], p, ident, start=True, stop=True,
                                                is_transpose=True if n == P else None)
                    last.then_inc(turned, 1)

            def weigh(u):
                qb, b, h0, heads = UNITS[u]
                pe.wait_ge(pt_d, PT_BEFORE[u + 1])
                if u >= 2:
                    pe.wait_ge(o_evac, u - 1)
                blocks = unit_blocks(u)
                for r in range(heads):
                    g = (h0 + r) // GROUP
                    mine = [(i, kb) for i, (kb, rr) in enumerate(blocks) if rr == r]
                    for i, kb in mine:
                        if b == "cmp":
                            p, v = probsT[0:NCMP, u % 2, i, :], vc_tok[:, g * HD:(g + 1) * HD]
                        else:
                            c0 = 256 * BRANCHES.index(b) + P + g * HD
                            p, v = probsT[:, u % 2, i, :], kv_tok[:, kb, c0:c0 + HD]
                        last = nc.tensor.matmul(ps[:, 6 + u % 2, r * HD:(r + 1) * HD], p, v, start=(i == mine[0][0]),
                                                stop=(i == mine[-1][0]))
                last.then_inc(pv_done, 1)

            scores(0)
            scores(1)
            for u in range(len(UNITS)):
                turn_probs(u)
                if u + 2 < len(UNITS):
                    scores(u + 2)
                weigh(u)
            pe.wait_ge(o_ready, len(UNITS) - TT)
            b0 = 4 * (INDEX["to"] % 2)
            for t in range(TT):
                for k in range(4):
                    last = turn(ps[:, b0 + t, k * P:(k + 1) * P], o_tok[:, t, k * P:(k + 1) * P])
            last.then_inc(filled, 1)
            product("eout0", fm, SEQ, False, ready=lambda k: evacuated(("mix", "to")[k // 4]) if k % 4 == 0 else None)
            product("eout1", fm, SEQ, False)
            product("k0_0", mem, MEM, True)
            product("k0_1", mem, MEM, True)
            product("v0_0", mem, MEM, False)
            product("v0_1", mem, MEM, False)

            for l in range(DEPTH):
                if l:
                    def recurrence_gates(n):
                        first, tiles, _, _ = RG_SETS[n]
                        pe.wait_ge(s_wgates, 32)
                        pe.wait_ge(conv_ready, sum(s[1] for s in RG_SETS[:n + 1]))
                        for i, kind in enumerate(("ra", "ia")):
                            b0 = begin(f"{kind}{n}") if (n, i) != (2, 1) else b0 + tiles
                            for j in range(tiles):
                                last = nc.tensor.matmul(ps[:, b0 + j, :], w_gates[:, i, first + j, :], h[:, first + j, :],
                                                        start=True, stop=True)
                            if (n, i) != (2, 0):
                                last.then_inc(filled, 1)

                    product("oin0", fm, SEQ, True)
                    product("oin1", fm, SEQ, True)
                    recurrence_gates(0)
                    product("oin2", fm, SEQ, True)
                    recurrence_gates(1)
                    product("oin3", fm, SEQ, True)
                    recurrence_gates(2)
                    product("oin4", fm, SEQ, True)
                    for n in (0, 1):
                        product(f"oout{n}", (y_hi, y_lo), SEQ, False, order=Y_ORDER,
                                ready=None if n else lambda k: pe.wait_ge(y_ready, k + 1))

                def turn_normed(i):
                    v = 3 * l + i
                    pe.wait_ge(bias_ready, v + 1)
                    for t in range(TT):
                        if t % 2 == 0:
                            b0 = begin(f"ln{l}{i}_{t // 2}")
                        pe.wait_ge(x_ready, TT * v + t + 1)
                        for half in (0, 1):
                            dst = ps[:, b0 + 2 * (t % 2) + half, :]
                            for kk in range(4):
                                k = 4 * half + kk
                                nc.tensor.matmul(dst[:, kk * P:(kk + 1) * P], x_res[:, t, k * P:(k + 1) * P], ident,
                                                 start=(kk == 0), stop=False, is_transpose=True, skip_group_check=True)
                            last = nc.tensor.matmul(dst.rearrange("p (k s) -> p k s", s=P), bias_rows[:, :],
                                                    bias_sel[:, 4 * half:4 * half + 4].unsqueeze(2).to_broadcast([2 * KT, 4, P]),
                                                    start=False, stop=True, skip_group_check=True)
                        last.then_inc(tile_turned, 1)
                    evacuated(f"ln{l}{i}_1")

                turn_normed(0)
                product(f"q{l}_0", fm, SEQ, True)
                product(f"q{l}_1", fm, SEQ, True)
                def x_scores(u, heads):
                    for r in heads:
                        for k in (0, 1):
                            last = nc.tensor.matmul(ps[:, 4 + 2 * (u % 2) + r // 2, (r % 2) * MEM:(r % 2 + 1) * MEM],
                                                    q_x[:, 2 * r + k, u * P:(u + 1) * P], k_mem[:, 2 * r + k, :],
                                                    start=(k == 0), stop=(k == 1))
                    return last

                def x_scores_again(u):
                    pe.wait_ge(x_exped, l * TT + u - 1)
                    x_scores(u, range(X_HEADS)).then_inc(x_scored, 1)

                def x_turn(u):
                    pe.wait_ge(x_scaled, l * TT + u + 1)
                    if u >= 2:
                        copied(u - 2)
                    for m in range(MT):
                        for r in range(X_HEADS):
                            last = turn(ps[:, 2 * (u % 2) + m, r * P:(r + 1) * P], px[:, u % 2, r, m * P:(m + 1) * P])
                        last.then_inc(x_turned, 1)

                def copied(u):
                    pe.wait_ge(xpt_d, l * TT + u + 1)
                    pe.wait_ge(xpt_a, l * TT + u + 1)

                def x_weigh(b0, j, r, t0, t1):
                    for m in range(MT):
                        c0 = r * X_HD + (j % 2) * P
                        last = nc.tensor.matmul(ps[:, b0 + j, t0 * P:t1 * P], v_mem[:, m, c0:c0 + P], pxT[:, m, r, t0 * P:t1 * P],
                                                start=(m == 0), stop=(m == MT - 1))
                    return last

                evacuated(f"q{l}_0")
                x_scores(0, (0, 1))
                x_scores(1, (0, 1))
                evacuated(f"q{l}_1")
                x_scores(0, (2, 3)).then_inc(x_scored, 1)
                x_scores(1, (2, 3)).then_inc(x_scored, 1)
                x_scores_again(2)
                x_turn(0)
                x_scores_again(3)
                x_turn(1)
                x_turn(2)
                copied(TT - 2)
                for j in (0, 1):
                    x_weigh(0, j, 0, 0, TT - 1)
                x_turn(TT - 1)
                copied(TT - 1)
                for j in (0, 1):
                    x_weigh(0, j, 0, TT - 1, TT)
                for j in (2, 3):
                    last = x_weigh(0, j, 1, 0, TT)
                last.then_inc(filled, 1)
                for j in range(4):
                    last = x_weigh(4, j, 2 + j // 2, 0, TT)
                last.then_inc(filled, 1)
                product(f"wo{l}_0", fm, SEQ, False, ready=lambda k: evacuated(f"xo{l}_{k // 4}") if k % 4 == 0 else None)
                product(f"wo{l}_1", fm, SEQ, False)
                if l == 0:
                    product("k1_0", mem, MEM, True)
                    product("k1_1", mem, MEM, True)
                turn_normed(1)
                for n in range(FT // 2):
                    product(f"up{l}_{n}", fm, SEQ, True)
                product(f"dn{l}_0", (g_hi, g_lo), SEQ, False, ready=lambda k: pe.wait_ge(g_ready, l * FT + k + 1))
                product(f"dn{l}_1", (g_hi, g_lo), SEQ, False)
                if l == 0:
                    product("v1_0", mem, MEM, False)
                    product("v1_1", mem, MEM, False)
                    turn_normed(2)

        @block.scalar
        def _(act):
            chain = [0]

            def settle(ins):
                chain[0] += 1
                ins.then_inc(a_chain, 1)
                act.wait_ge(a_chain, chain[0])

            rounded = [0]

            def round_weights(last):
                for c in range(rounded[0], min(last, len(CHUNKS))):
                    s, n = c % RING, WIDTH[c]
                    act.wait_ge(w_landed[s], LANDED[c])
                    if c >= RING:
                        act.wait_ge(w_used, c - RING + 1)
                    nc.scalar.activation(w_hi[:, s, :n], w_raw[:, s, :n], ACT.Copy).then_inc(w_rounded, 1)
                rounded[0] = max(rounded[0], last)

            def round_on(n, name, step=None):
                limit = CHUNK0[name] + (PLAN[INDEX[name]][1] if step is None else step) + RING - 1
                round_weights(min(rounded[0] + n, limit))

            def filled_by(name):
                round_weights(CHUNK0[name] + PLAN[INDEX[name]][1] + RING - 1)
                group_filled(act, name)

            def turn_evac(name, hi):
                filled_by(name)
                for j in range(4):
                    copy_turned(name, hi, j)

            def copy_turned(name, hi, j):
                nc.scalar.activation(fm_target(hi, name, j), quarter(bank(name, j)), ACT.Copy).then_inc(evac_a, 1)

            turn_evac("x0", fm_hi)
            turn_evac("x1", fm_hi)
            filled_by("small")
            nc.scalar.activation(chan[:, :], bank("small", 0)[:, 0:V_END], ACT.Copy).then_inc(evac_a, 1)
            act.wait_ge(ang_ready, 1)
            nc.scalar.activation(trig[:, 1, :, :].rearrange("p t f -> p (t f)"), ang[:, 0, :], ACT.Sin).then_inc(trig_ready, 1)
            nc.scalar.activation(trig[:, 0, :, :].rearrange("p t f -> p (t f)"), ang[:, 1, :], ACT.Sin).then_inc(trig_ready, 1)
            act.wait_ge(sp_ready, 1)
            nc.scalar.activation(lru_c[:, 1, :], lru_c[:, 0, :], ACT.Exp).then_inc(sp_exp, 1)
            act.wait_ge(pads_ready, 1)
            filled_by("ein0")
            for j in range(4):
                nc.scalar.activation(pool_in[:, j, PAD:], bank("ein0", j), ACT.Copy).then_inc(evac_a, 1)
            turn_evac("tm", mem_hi)
            filled_by("ein1")
            for j in range(4):
                nc.scalar.activation(q_tok[:, j, :], bank("ein1", j), ACT.Copy, scale=HD ** -0.5).then_inc(evac_a, 1)
            filled_by("ein2")
            for j in range(4):
                nc.scalar.activation(kv_tok[:, j, :], bank("ein2", j), ACT.Copy).then_inc(evac_a, 1)
            filled_by("ein3")
            nc.scalar.activation(gateT[:, :], bank("ein3", 0)[0:GATES, :], ACT.Sigmoid).then_inc(evac_a, 1)
            for n in (0, 1):
                nc.scalar.activation(raw_cmp[:, n, :], bank("ein3", 1 + n), ACT.Copy).then_inc(evac_a, 1)
            filled_by("mix")
            for j in range(4):
                nc.scalar.activation(fm_hi[:, j, :], bank("mix", j), ACT.Copy,
                                     scale=chan[:, V_PSCALE + j:V_PSCALE + j + 1]).then_inc(evac_a, 1)
            filled_by("tq")
            for j in range(4):
                nc.scalar.activation(qT[:, j, :], bank("tq", j), ACT.Copy).then_inc(evac_a, 1)
            filled_by("tk")
            for j in range(4):
                nc.scalar.activation(kT[:, j // 2, j % 2, :], bank("tk", j), ACT.Copy).then_inc(evac_a, 1)
            filled_by("cmp")
            b0 = 4 * (INDEX["cmp"] % 2)
            cmp_banks = ps[0:NCMP, b0:b0 + 2, :]
            nc.scalar.activation(kc_tok[:, :, :], cmp_banks[:, :, 0:HD], ACT.Copy).then_inc(evac_a, 1)
            nc.scalar.activation(vc_tok[:, :].rearrange("n (g d) -> n g d", d=HD), cmp_banks[:, :, HD:2 * HD], ACT.Copy).then_inc(evac_a, 1)
            nc.scalar.activation(gates[:, :, :].rearrange("p t c -> p (t c)"), bank("cmp", 2)[:, 0:TT * GATES], ACT.Copy).then_inc(evac_a, 1)
            filled_by("tkc")
            for g in range(KV_HEADS):
                nc.scalar.activation(kcT[:, g, :], bank("tkc", g)[:, 0:NCMP], ACT.Copy).then_inc(evac_a, 1)

            def exps(u):
                qb, b, h0, heads = UNITS[u]
                act.wait_ge(maxed, u + 1)
                for r in range(heads):
                    hh = h0 + r
                    n, c0 = NCMP if b == "cmp" else (qb + 1) * P, r // 2 * unit_width(u)
                    last = nc.scalar.activation(probs_of(u, r)[:, :n], ps[:, 2 * (u % 2) + hh % 2, c0:c0 + n], ACT.Exp,
                                                bias=negmax[:, u % 2, r:r + 1], accum_out=rowsum[:, u % 2, r:r + 1])
                last.then_inc(exped, 1)

            for u in range(len(UNITS)):
                if u >= 2:
                    act.wait_ge(summed, u - 1)
                exps(u)
            filled_by("to")
            for t in range(TT):
                nc.scalar.activation(fm_hi[:, 4:8, t * P:(t + 1) * P], quarter(bank("to", t)), ACT.Copy).then_inc(evac_a, 1)

            def keys_evac(l):
                for n in (0, 1):
                    filled_by(f"k{l}_{n}")
                    for j in range(4):
                        nc.scalar.activation(k_mem[:, 4 * n + j, :], bank(f"k{l}_{n}", j)[:, :MEM], ACT.Copy).then_inc(evac_a, 1)

            def values_evac(l):
                for n in (0, 1):
                    filled_by(f"v{l}_{n}")
                    for m in range(MT):
                        nc.scalar.activation(v_mem[:, m, 512 * n:512 * (n + 1)], bank(f"v{l}_{n}", m), ACT.Copy).then_inc(evac_a, 1)

            def norm(l, i, spread):
                v = 3 * l + i
                last = (("eout1", "oout1")[l], f"wo{l}_1", f"dn{l}_1")[i]
                round_weights(CHUNK0[last] + PLAN[INDEX[last]][1] + RING - 1)
                if spread:
                    round_weights(rounded[0] + 4)
                settle(nc.scalar.activation(lnc[:, 1, 0:1], consts[:, C_ROWOK + 1:C_ROWOK + 2], ACT.Sqrt))
                for t in range(TT):
                    act.wait_ge(ln_var, TT * v + t + 1)
                    nc.scalar.activation(lnc[:, 1, t:t + 1], lnc[:, 0, t:t + 1], ACT.Sqrt).then_inc(ln_sd, 1)
                    if spread and t % 2 == 0:
                        round_weights(rounded[0] + 1)
                    act.wait_ge(ln_coef, TT * v + t + 1)
                    nc.scalar.activation(x_res[:, t, :], x_res[:, t, :], ACT.Copy, scale=lnc[:, 2, t:t + 1]).then_inc(x_ready, 1)
                    if spread:
                        round_weights(rounded[0] + 1)

            def norm_turned(l, i):
                for n in (0, 1):
                    name = f"ln{l}{i}_{n}"
                    round_weights(CHUNK0[name] + RING - 1)
                    for j in range(4):
                        act.wait_ge(tile_turned, TT * (3 * l + i) + 2 * n + j // 2 + 1)
                        copy_turned(name, fm_hi, j)

            for l in range(DEPTH):
                if l:
                    def gelus(n):
                        first, tiles, name = GATE_SETS[n]
                        filled_by(name)
                        for j in range(tiles):
                            nc.scalar.activation(gelu[:, first + j, :], bank(name, j), ACT.Gelu_apprx_tanh).then_inc(evac_a, 1)

                    def y_rounded(n, meanwhile):
                        first, tiles, _ = GATE_SETS[n]
                        for j in range(tiles):
                            i = sum(s[1] for s in GATE_SETS[:n]) + j
                            act.wait_ge(y_full, i + 1)
                            nc.scalar.activation(y_hi[:, first + j, :], h[:, first + j, :], ACT.Copy).then_inc(y_hi_ready, 1)
                            if n == 2:
                                round_on(1, "oout0", i)
                            elif j % 2:
                                round_on(1, meanwhile)

                    def x_evac(n):
                        first, tiles, name, b = RG_SETS[n]
                        if n >= 2:
                            act.wait_ge(conv_ready, sum(s[1] for s in RG_SETS[:n - 1]))
                        act.wait_ge(pads_ready, 2)
                        filled_by(name)
                        for j in range(tiles):
                            nc.scalar.activation(x_pad[:, n % 2, j, CONV - 1:], bank(name, b + j), ACT.Copy).then_inc(evac_a, 1)

                    def decays(n, meanwhile):
                        first, tiles, _, _ = RG_SETS[n]
                        done = sum(s[1] for s in RG_SETS[:n])
                        filled_by(f"ra{n}")
                        for j in range(tiles):
                            nc.scalar.activation(RA[n][:, j, :], bank(f"ra{n}", j), ACT.Sigmoid,
                                                 bias=chan[:, V_BA + first + j:V_BA + first + j + 1]).then_inc(evac_a, 1)
                        round_on(1, meanwhile)
                        if n < 2:
                            group_filled(act, f"ia{n}")
                        for j in range(tiles):
                            src = bank(f"ia{n}", j) if n < 2 else bank("ra2", tiles + j)
                            nc.scalar.activation(IB[n][:, j, :], src, ACT.Sigmoid,
                                                 bias=chan[:, V_BX + first + j:V_BX + first + j + 1]).then_inc(evac_a, 1)
                        round_on(1, meanwhile)
                        act.wait_ge(evac_a, ACT_BEFORE[f"ra{n}"] + tiles)
                        act.wait_ge(lru_ready, 1)
                        for j in range(tiles):
                            if n:
                                act.wait_ge(h_ready, sum(s[1] for s in RG_SETS[:n - 1]) + j + 1)
                            last = nc.scalar.activation(tm[:, j, :], RA[n][:, j, :], ACT.Tanh, scale=lru_c[:, 0, first + j:first + j + 1])
                        settle(last)
                        round_on(1, meanwhile)
                        for j in range(tiles):
                            nc.scalar.activation(RA[n][:, j, :], RA[n][:, j, :], ACT.Exp,
                                                 scale=lru_c[:, 1, first + j:first + j + 1]).then_inc(ta_ready, 1)

                    def multipliers(n, meanwhile):
                        done = sum(s[1] for s in RG_SETS[:n])
                        for j in range(RG_SETS[n][1]):
                            round_on(1 + (j == 0), meanwhile)
                            act.wait_ge(m2_ready, done + j + 1)
                            nc.scalar.activation(tm[:, j, :], tm[:, j, :], ACT.Sqrt).then_inc(mult_ready, 1)

                    x_evac(0)
                    x_evac(1)
                    decays(0, "oin2")
                    multipliers(0, "oin2")
                    gelus(0)
                    x_evac(2)
                    decays(1, "oin3")
                    y_rounded(0, "oin3")
                    multipliers(1, "oin3")
                    gelus(1)
                    decays(2, "oin4")
                    y_rounded(1, "oin4")
                    multipliers(2, "oin4")
                    gelus(2)
                    y_rounded(2, "oout0")
                norm(l, 0, l == 0)
                if l == 0:
                    keys_evac(0)
                    values_evac(0)
                norm_turned(l, 0)
                for n in (0, 1):
                    filled_by(f"q{l}_{n}")
                    for j in range(4):
                        nc.scalar.activation(q_x[:, 4 * n + j, :], bank(f"q{l}_{n}", j), ACT.Copy, scale=X_HD ** -0.5).then_inc(evac_a, 1)

                def x_exps(u):
                    v = l * TT + u
                    act.wait_ge(x_maxed, v + 1)
                    if u >= 2:
                        act.wait_ge(x_turned, MT * (v - 1))
                    for r in range(X_HEADS):
                        c0 = (r % 2) * MEM
                        last = nc.scalar.activation(px[:, u % 2, r, :], ps[:, 4 + 2 * (u % 2) + r // 2, c0:c0 + MEM], ACT.Exp,
                                                    bias=negmax[:, u % 2, r:r + 1], accum_out=rowsum[:, u % 2, r:r + 1])
                    last.then_inc(x_exped, 1)

                def x_copy(u):
                    act.wait_ge(x_turned, MT * (l * TT + u) + 2)
                    nc.scalar.activation(pxT[:, 1, :, u * P:(u + 1) * P], quarter(ps[:, 2 * (u % 2) + 1, :]), ACT.Copy).then_inc(xpt_a, 1)

                x_exps(0)
                x_exps(1)
                x_copy(0)
                x_exps(2)
                x_copy(1)
                x_exps(3)
                x_copy(2)
                x_copy(3)
                for n in (0, 1):
                    filled_by(f"xo{l}_{n}")
                    for j in range(4):
                        nc.scalar.activation(fm_hi[:, 4 * n + j, :], bank(f"xo{l}_{n}", j), ACT.Copy).then_inc(evac_a, 1)
                norm(l, 1, l == 0)
                if l == 0:
                    keys_evac(1)
                norm_turned(l, 1)
                for n in range(FT // 2):
                    name = f"up{l}_{n}"
                    filled_by(name)
                    for j in (0, 1):
                        if n:
                            act.wait_ge(evac_d, DVE_BEFORE[name] - 1 + j)
                        nc.scalar.activation(silu[:, j, :], bank(name, j), ACT.Silu).then_inc(evac_a, 1)
                    for j in (0, 1):
                        i = l * FT + 2 * n + j
                        act.wait_ge(evac_d, DVE_BEFORE[name] + j + 1)
                        nc.scalar.activation(g_hi[:, 2 * n + j, :], gf[:, j, :], ACT.Copy).then_inc(g_hi_ready, 1)
                norm(l, 2, l == 0)
                if l == 0:
                    values_evac(1)
                    norm_turned(l, 2)

        @block.vector
        def _(dve):
            chain = [0]

            def settle(ins):
                chain[0] += 1
                ins.then_inc(d_chain, 1)
                dve.wait_ge(d_chain, chain[0])

            def low_part(lo, full, hi, done):
                nc.vector.tensor_tensor(lo, full, hi.bitcast(F32), ALU.subtract).then_inc(done, 1)

            def turn_evac(name, hi, lo):
                for j in range(4):
                    dve.wait_ge(evac_a, ACT_BEFORE[name] + j + 1)
                    low_part(fm_target(lo, name, j), quarter(bank(name, j)), fm_target(hi, name, j), evac_d)

            dve.wait_ge(s_consts, 16)
            nc.vector.tensor_copy(ident_b[:, :], consts[:, C_ID:C_ID + P]).then_inc(tables_ready, 1)
            nc.vector.tensor_copy(bias_sel[:, :], consts[0:2 * KT, C_SEL:C_SEL + KT])
            nc.vector.tensor_copy(causal_b[:, :], consts[:, C_CAUSAL:C_CAUSAL + P]).then_inc(tables_ready, 1)
            nc.vector.tensor_copy(cmask_b[:, :, :].rearrange("p t n -> p (t n)"),
                                  consts[:, C_CMASK:C_CMASK + TT * 32]).then_inc(tables_ready, 1)
            nc.vector.memset(pool_sum[:, :, 0:PAD], 0.0)
            nc.vector.memset(pool_in[:, :, 0:PAD], 0.0).then_inc(pads_ready, 1)
            dve.wait_ge(s_pos, 32)
            settle(nc.vector.memset(pos_f[:, :], 0.0))
            nc.vector.tensor_copy(pos_f[:, 0:TT], pos_i[:, 0:TT])
            settle(nc.vector.tensor_copy(pos_f[0:NCMP, TT:TT + 1], pos_i[0:NCMP, TT:TT + 1]))
            settle(nc.vector.tensor_tensor(ang[:, 0, :].rearrange("p (t f) -> p t f", f=HALF),
                                           pos_f[:, :].unsqueeze(2).to_broadcast([P, TT + 1, HALF]),
                                           consts[:, C_INVF:C_INVF + HALF].unsqueeze(1).to_broadcast([P, TT + 1, HALF]), ALU.mult))
            magic = 1.5 * 2.0 ** 23
            settle(nc.vector.tensor_scalar(ang[:, 1, :], ang[:, 0, :], 1.0 / (2.0 * np.pi), magic, ALU.mult, ALU.add))
            settle(nc.vector.tensor_scalar(ang[:, 1, :], ang[:, 1, :], magic, None, ALU.subtract))
            c1 = 6.28125
            c2 = float(np.float32(np.round((2 * np.pi - c1) * 2 ** 20) / 2 ** 20))
            c3 = 2 * np.pi - c1 - c2
            for c in (c1, c2, c3):
                settle(nc.vector.scalar_tensor_tensor(out=ang[:, 0, :], in0=ang[:, 1, :], scalar=-c, in1=ang[:, 0, :],
                                                      op0=ALU.mult, op1=ALU.add))
            edge = 3.1415925
            settle(nc.vector.tensor_scalar(ang[:, 0, :], ang[:, 0, :], edge, -edge, ALU.min, ALU.max))
            settle(nc.vector.scalar_tensor_tensor(out=ang[:, 1, :], in0=ang[:, 0, :], scalar=-1.0, in1=ang[:, 0, :],
                                                  op0=ALU.mult, op1=ALU.max))
            nc.vector.tensor_scalar(ang[:, 1, :], ang[:, 1, :], -1.0, np.pi / 2, ALU.mult, ALU.add).then_inc(ang_ready, 1)

            turn_evac("x0", fm_hi, fm_lo)
            turn_evac("x1", fm_hi, fm_lo)
            dve.wait_ge(evac_a, ACT_AFTER["small"])
            lam = chan[:, V_LAM:V_LAM + RT]
            settle(nc.vector.tensor_scalar(lru_c[:, 0, :], lam, -1.0, None, ALU.mult))
            nc.vector.tensor_tensor(lru_c[:, 0, :], lru_c[:, 0, :], lam, ALU.min).then_inc(sp_ready, 1)
            dve.wait_ge(sp_exp, 1)
            z, w = lru_c[:, 1, :], lru_c[:, 0, :]
            w2, acc = rot_tmp[:, 0, 0:RT], rot_tmp[:, 1, 0:RT]
            settle(nc.vector.tensor_scalar(w, z, 2.0, None, ALU.add))
            settle(nc.vector.reciprocal(w, w))
            settle(nc.vector.tensor_tensor(w, w, z, ALU.mult))
            settle(nc.vector.tensor_tensor(w2, w, w, ALU.mult))
            settle(nc.vector.tensor_scalar(acc, w2, 1.0 / 17, 1.0 / 15, ALU.mult, ALU.add))
            for n in (13, 11, 9, 7, 5, 3, 1):
                settle(nc.vector.tensor_tensor(acc, acc, w2, ALU.mult))
                settle(nc.vector.tensor_scalar(acc, acc, 1.0 / n, None, ALU.add))
            settle(nc.vector.scalar_tensor_tensor(out=acc, in0=acc, scalar=2.0, in1=w, op0=ALU.mult, op1=ALU.mult))
            settle(nc.vector.tensor_scalar(z, lam, -1.0, 0.0, ALU.mult, ALU.max))
            settle(nc.vector.tensor_tensor(acc, acc, z, ALU.add))
            nc.vector.tensor_scalar(lru_c[:, 0, :], acc, 8.0, None, ALU.mult)
            nc.vector.tensor_scalar(lru_c[:, 1, :], acc, -8.0, None, ALU.mult).then_inc(lru_ready, 1)
            dve.wait_ge(lru_ready, 1)

            turn_evac("tm", mem_hi, mem_lo)

            for g, win in enumerate(WINDOWS):
                dve.wait_ge(evac_a, ACT_BEFORE["ein0"] + g + 1)
                src, sh, n = pool_in[:, g, :], 1, 0
                while sh < win:
                    dst = pool_sum[:, n % 2, :]
                    settle(nc.vector.tensor_tensor(dst[:, PAD:], src[:, PAD:], src[:, PAD - sh:PAD + SEQ - sh], ALU.add))
                    src, sh, n = dst, 2 * sh, n + 1
                u = pool_in[:, g, :]
                settle(nc.vector.tensor_tensor(src[:, PAD:2 * PAD], src[:, PAD:2 * PAD],
                                               consts[:, C_PINV + g * PAD:C_PINV + (g + 1) * PAD], ALU.mult))
                settle(nc.vector.tensor_tensor(u[:, PAD:2 * PAD], src[:, PAD:2 * PAD], u[:, PAD:2 * PAD], ALU.subtract))
                nc.vector.scalar_tensor_tensor(out=u[:, 2 * PAD:], in0=src[:, 2 * PAD:], scalar=1.0 / win, in1=u[:, 2 * PAD:],
                                               op0=ALU.mult, op1=ALU.subtract).then_inc(pooled_ready, 1)
                dve.wait_ge(pooled_ready, g + 1)

            def rotate(x1, x2, cos, sin, tmp, done=None):
                t0, t1, t2 = tmp
                nc.vector.tensor_tensor(t0, x1, sin, ALU.mult)
                nc.vector.tensor_tensor(t1, x2, sin, ALU.mult)
                settle(nc.vector.tensor_tensor(t2, x1, cos, ALU.mult))
                settle(nc.vector.tensor_tensor(x2, x2, cos, ALU.mult))
                nc.vector.tensor_tensor(x1, t2, t1, ALU.subtract)
                last = nc.vector.tensor_tensor(x2, x2, t0, ALU.add)
                if done is None:
                    settle(last)
                else:
                    last.then_inc(done, 1)

            dve.wait_ge(trig_ready, 2)
            dve.wait_ge(evac_a, ACT_AFTER["ein1"])
            for t in range(TT):
                qh = q_tok[:, t, :].rearrange("p (h d) -> p h d", d=HD)
                tmp = [rot_tmp[:, i, t * 64:(t + 1) * 64].rearrange("p (h d) -> p h d", d=HALF) for i in range(3)]
                cs = [trig[:, i, t, :].unsqueeze(1).to_broadcast([P, HEADS, HALF]) for i in (0, 1)]
                rotate(qh[:, :, 0:HALF], qh[:, :, HALF:ROT], cs[0], cs[1], tmp, None if t < TT - 1 else q_ready)
            dve.wait_ge(evac_a, ACT_AFTER["ein2"])
            for b in (0, 1):
                for t in range(TT):
                    kh = kv_tok[:, t, 256 * b:256 * b + P].rearrange("p (g d) -> p g d", d=HD)
                    tmp = [rot_tmp[:, i, (b * TT + t) * 16:(b * TT + t + 1) * 16].rearrange("p (g d) -> p g d", d=HALF) for i in range(3)]
                    cs = [trig[:, i, t, :].unsqueeze(1).to_broadcast([P, KV_HEADS, HALF]) for i in (0, 1)]
                    rotate(kh[:, :, 0:HALF], kh[:, :, HALF:ROT], cs[0], cs[1], tmp)
                for t in range(TT):
                    src = kv_tok[:, t, 256 * b:256 * b + P].rearrange("p (g d) -> p g d", d=HD)
                    last = nc.vector.tensor_copy(kdup[:, b, t, :, 0, :], src)
                    last = nc.vector.tensor_copy(kdup[:, b, t, :, 1, :], src)
                last.then_inc(kdup_ready, 1)
            for n in (0, 1):
                dve.wait_ge(evac_a, ACT_BEFORE["ein3"] + 2 + n)
                for part in (0, 1):
                    c0 = (V_POSK, V_POSV)[n] + part * CMP_STRIDE
                    nc.vector.tensor_tensor(raw_pos[:, n, part, :].rearrange("p (b l) -> p b l", l=CMP_STRIDE),
                                            raw_cmp[:, n, :].rearrange("p (b l) -> p b l", l=CMP_STRIDE),
                                            chan[:, c0:c0 + CMP_STRIDE].unsqueeze(1).to_broadcast([P, SEQ // CMP_STRIDE, CMP_STRIDE]),
                                            ALU.add).then_inc(rawpos_ready, 1)
            for j in range(4):
                dve.wait_ge(evac_a, ACT_BEFORE["mix"] + j + 1)
                nc.vector.scalar_tensor_tensor(out=fm_lo[:, j, :], in0=bank("mix", j), scalar=chan[:, V_PSCALE + j:V_PSCALE + j + 1],
                                               in1=fm_hi[:, j, :].bitcast(F32), op0=ALU.mult, op1=ALU.subtract).then_inc(evac_d, 1)
            dve.wait_ge(evac_a, ACT_BEFORE["cmp"] + 1)
            kc = kc_tok[:, :, :]
            tmp = [rot_tmp[0:NCMP, i, 128:144].rearrange("p (g d) -> p g d", d=HALF) for i in range(3)]
            cs = [trig[0:NCMP, i, TT, :].unsqueeze(1).to_broadcast([NCMP, KV_HEADS, HALF]) for i in (0, 1)]
            rotate(kc[:, :, 0:HALF], kc[:, :, HALF:ROT], cs[0], cs[1], tmp)
            nc.vector.tensor_copy(kc_dup[:, :, 0, :], kc)
            nc.vector.tensor_copy(kc_dup[:, :, 1, :], kc).then_inc(kcdup_ready, 1)

            def row_max(u):
                qb, b, h0, heads = UNITS[u]
                dve.wait_ge(scored, u + 1)
                w, n = unit_width(u), NCMP if b == "cmp" else (qb + 1) * P
                s = ps[:, 2 * (u % 2):2 * (u % 2) + 2, 0:heads // 2 * w].rearrange("p i (r n) -> p i r n", n=w)[:, :, :, 0:n]
                m = negmax[:, u % 2, 0:heads].rearrange("p (r i) -> p i r", i=2)
                nc.vector.tensor_reduce(m, s, AX.X, ALU.max, negate=True).then_inc(maxed, 1)

            dve.wait_ge(evac_a, ACT_AFTER["cmp"])
            added = 0
            row_max(0)
            row_max(1)
            for u, (qb, b, h0, heads) in enumerate(UNITS):
                n = NCMP if b == "cmp" else P
                blocks = unit_blocks(u)
                for j in range(0, len(blocks), 4):
                    i, m = PT_BEFORE[u] + j // 4, min(4, len(blocks) - j)
                    dve.wait_ge(turned, i + 1)
                    nc.vector.tensor_copy(probsT[0:n, u % 2, j:j + m, :].rearrange("p b q -> p (b q)"),
                                          ps[0:n, 4 + i % 2, 0:m * P]).then_inc(pt_d, 1)
                if u + 2 < len(UNITS):
                    row_max(u + 2)
                wt = weight[:, u % 2, 0:heads]
                nc.vector.reciprocal(wt, rowsum[:, u % 2, 0:heads]).then_inc(summed, 1)
                dve.wait_ge(summed, u + 1)
                gt = gates[:, qb, h0 * 3:(h0 + heads) * 3].rearrange("p (r c) -> p r c", c=3)[:, :, GATE_OF[b]]
                settle(nc.vector.tensor_tensor(wt, wt, gt, ALU.mult))
                if b == "cmp":
                    settle(nc.vector.tensor_scalar(wt, wt, consts[:, C_ROWOK + qb:C_ROWOK + qb + 1], None, ALU.mult))
                dve.wait_ge(pv_done, u + 1)
                o = ps[:, 6 + u % 2, 0:heads * HD].rearrange("p (r d) -> p r d", d=HD)
                wb = wt.unsqueeze(2).to_broadcast([P, heads, HD])
                dst = o_tok[:, qb, h0 * HD:(h0 + heads) * HD]
                if b == "cmp":
                    nc.vector.tensor_tensor(dst.rearrange("p (r d) -> p r d", d=HD), o, wb, ALU.mult).then_inc(o_evac, 1)
                    dve.wait_ge(o_evac, u + 1)
                else:
                    nc.vector.tensor_tensor(o_tmp[:, 0:heads * HD].rearrange("p (r d) -> p r d", d=HD), o, wb, ALU.mult).then_inc(o_evac, 1)
                    dve.wait_ge(o_evac, u + 1)
                    added += 1
                    nc.vector.tensor_tensor(dst, dst, o_tmp[:, 0:heads * HD], ALU.add).then_inc(o_ready, 1)
                    dve.wait_ge(o_ready, added)
            for t in range(TT):
                dve.wait_ge(evac_a, ACT_BEFORE["to"] + t + 1)
                low_part(fm_lo[:, 4:8, t * P:(t + 1) * P], quarter(bank("to", t)), fm_hi[:, 4:8, t * P:(t + 1) * P], evac_d)

            def add_residual(n, name, t):
                xs = x_res[:, t, 512 * n:512 * (n + 1)]
                if whole[0]:
                    dve.wait_ge(x_whole, whole[0])
                nc.vector.scalar_tensor_tensor(out=xs, in0=xs, scalar=ALPHA, in1=bank(name, t), op0=ALU.mult,
                                               op1=ALU.add).then_inc(evac_d, 1)

            def half_stats(n, name, t):
                dve.wait_ge(evac_d, DVE_BEFORE[name] + t + 1)
                return nc.vector.bn_stats(stats[:, t, n, :], x_res[:, t, 512 * n:512 * (n + 1)])

            whole = [0]

            def norm(l, i, names):
                v = 3 * l + i
                group_filled(dve, names[0])
                for t in range(TT):
                    add_residual(0, names[0], t)
                for t in range(TT):
                    half_stats(0, names[0], t)
                dve.wait_ge(s_lnp, 64 * (v + 1))
                settle(nc.vector.tensor_copy(bias_hi[:, :], bias_raw[:, :]))
                rows = slice(0, 2 * KT)
                settle(nc.vector.tensor_scalar(bias_raw[:, :], bias_raw[:, :], consts[rows, C_LOW:C_LOW + 1], None, ALU.mult))
                nc.vector.scalar_tensor_tensor(out=bias_rows[:, :], in0=bias_hi[:, :].bitcast(F32), scalar=consts[rows, C_LOW + 1:C_LOW + 2],
                                               in1=bias_raw[:, :], op0=ALU.mult, op1=ALU.add).then_inc(bias_ready, 1)
                group_filled(dve, names[1])
                add_residual(1, names[1], 0)
                settle(half_stats(1, names[1], 0))
                for t in range(TT):
                    if t + 1 < TT:
                        add_residual(1, names[1], t + 1)
                    settle(nc.vector.bn_aggr(mv[:, t, :], stats[:, t, :, :].rearrange("p a b -> p (a b)")))
                    nc.vector.tensor_scalar(lnc[:, 0, t:t + 1], mv[:, t, 1:2], EPS, None, ALU.add).then_inc(ln_var, 1)
                    settle(nc.vector.scalar_tensor_tensor(out=x_res[:, t, :], in0=x_res[:, t, :], scalar=mv[:, t, 0:1], in1=ln_g[:, :],
                                                          op0=ALU.subtract, op1=ALU.mult))
                    dve.wait_ge(ln_sd, TT * v + t + 1)
                    nc.vector.reciprocal(lnc[:, 2, t:t + 1], lnc[:, 1, t:t + 1]).then_inc(ln_coef, 1)
                    if t + 1 < TT:
                        settle(half_stats(1, names[1], t + 1))

                def bias(t):
                    nc.vector.tensor_tensor(x_res[:, t, :], x_res[:, t, :], ln_b[:, :], ALU.add).then_inc(x_whole, 1)

                if (l, i) == (DEPTH - 1, 2):
                    dve.wait_ge(x_ready, TT * (v + 1))
                    bias(TT - 1)
                else:
                    turn_evac(f"ln{l}{i}_0", fm_hi, fm_lo)
                    turn_evac(f"ln{l}{i}_1", fm_hi, fm_lo)
                    for t in range(TT):
                        bias(t)
                    whole[0] += TT

            for l in range(DEPTH):
                if l == 0:
                    norm(0, 0, ("eout0", "eout1"))
                if l:
                    nc.vector.memset(x_pad[:, :, :, 0:CONV - 1].rearrange("p i j c -> p (i j) c"), 0.0).then_inc(pads_ready, 1)
                    dve.wait_ge(s_posb, 16)
                    settle(nc.vector.tensor_copy(keep[:, :], posb[:, :]))
                    settle(nc.vector.tensor_scalar(keep[:, :], keep[:, :], 0.0, None, ALU.not_equal))

                    def conv(n):
                        first, tiles, name, b = RG_SETS[n]
                        for j in range(tiles):
                            dve.wait_ge(evac_a, ACT_BEFORE[name] + b + j + 1)
                            cw = lambda k: chan[:, V_CONVW + k * RT + first + j:V_CONVW + k * RT + first + j + 1]
                            settle(nc.vector.tensor_scalar(h[:, first + j, :], x_pad[:, n % 2, j, 0:SEQ], cw(0),
                                                           chan[:, V_CONVB + first + j:V_CONVB + first + j + 1], ALU.mult, ALU.add))
                            for k in range(1, CONV):
                                ins = nc.vector.scalar_tensor_tensor(out=h[:, first + j, :], in0=x_pad[:, n % 2, j, k:k + SEQ], scalar=cw(k),
                                                                     in1=h[:, first + j, :], op0=ALU.mult, op1=ALU.add)
                                if k < CONV - 1:
                                    settle(ins)
                            ins.then_inc(conv_ready, 1)

                    def multipliers_squared(n):
                        first, tiles, _, _ = RG_SETS[n]
                        done = sum(s[1] for s in RG_SETS[:n])
                        dve.wait_ge(evac_a, ACT_AFTER[f"ia{n}" if n < 2 else "ra2"])
                        for j in range(tiles):
                            a_, i_ = RA[n][:, j, :], IB[n][:, j, :]
                            dve.wait_ge(ta_ready, done + j + 1)
                            settle(nc.vector.tensor_tensor(a_, a_, keep[:, :], ALU.mult))
                            nc.vector.tensor_tensor(a_sq[:, :], a_, a_, ALU.mult)
                            nc.vector.tensor_tensor(i_, i_, h[:, first + j, :], ALU.mult)
                            settle(nc.vector.scalar_tensor_tensor(out=tm[:, j, :], in0=keep[:, :], scalar=0.0, in1=tm[:, j, :],
                                                                  op0=ALU.is_equal, op1=ALU.max))
                            nc.vector.scalar_tensor_tensor(out=tm[:, j, :], in0=a_sq[:, :], scalar=1.0, in1=tm[:, j, :],
                                                           op0=ALU.add, op1=ALU.mult).then_inc(m2_ready, 1)
                            dve.wait_ge(m2_ready, done + j + 1)

                    def recurrence(n):
                        first, tiles, _, _ = RG_SETS[n]
                        done = sum(s[1] for s in RG_SETS[:n])
                        for j in range(tiles):
                            a_, i_ = RA[n][:, j, :], IB[n][:, j, :]
                            dve.wait_ge(mult_ready, done + j + 1)
                            settle(nc.vector.tensor_tensor(i_, i_, tm[:, j, :], ALU.mult))
                            nc.vector.tensor_tensor_scan(h[:, first + j, :], a_, i_, 0.0, ALU.mult, ALU.add).then_inc(h_ready, 1)
                        dve.wait_ge(h_ready, done + tiles)

                    def y_tile(n, j):
                        first, _, name = GATE_SETS[n]
                        dve.wait_ge(evac_a, ACT_BEFORE[name] + j + 1)
                        hj = h[:, first + j, :]
                        nc.vector.tensor_tensor(hj, hj, gelu[:, first + j, :], ALU.mult).then_inc(y_full, 1)

                    def y_low(n, j):
                        first = GATE_SETS[n][0]
                        i = sum(s[1] for s in GATE_SETS[:n]) + j
                        dve.wait_ge(y_hi_ready, i + 1)
                        low_part(y_lo[:, first + j, :], h[:, first + j, :], y_hi[:, first + j, :], y_ready)

                    conv(0)
                    conv(1)
                    multipliers_squared(0)
                    recurrence(0)
                    y_tile(0, 0)
                    y_tile(0, 1)
                    conv(2)
                    multipliers_squared(1)
                    y_low(0, 0)
                    y_low(0, 1)
                    recurrence(1)
                    for j in range(4):
                        y_tile(1, j)
                    multipliers_squared(2)
                    for j in range(4):
                        y_low(1, j)
                    recurrence(2)
                    for j in range(5):
                        if j < 4:
                            y_tile(2, j)
                        if j:
                            y_low(2, j - 1)
                    norm(1, 0, ("oout0", "oout1"))

                def x_max(u):
                    dve.wait_ge(x_scored, l * TT + u + 1)
                    s = ps[:, 4 + 2 * (u % 2):6 + 2 * (u % 2), :].rearrange("p b (h m) -> p (b h) m", m=MEM)
                    nc.vector.tensor_reduce(negmax[:, u % 2, 0:X_HEADS], s, AX.X, ALU.max, negate=True).then_inc(x_maxed, 1)

                def x_scale(u):
                    dve.wait_ge(x_exped, l * TT + u + 1)
                    wt = weight[:, u % 2, 0:X_HEADS]
                    settle(nc.vector.reciprocal(wt, rowsum[:, u % 2, 0:X_HEADS]))
                    nc.vector.tensor_tensor(px[:, u % 2, :, :], px[:, u % 2, :, :], wt.unsqueeze(2).to_broadcast([P, X_HEADS, MEM]),
                                            ALU.mult).then_inc(x_scaled, 1)

                def x_copy(u):
                    dve.wait_ge(x_turned, MT * (l * TT + u) + 1)
                    nc.vector.tensor_copy(pxT[:, 0, :, u * P:(u + 1) * P], quarter(ps[:, 2 * (u % 2), :])).then_inc(xpt_d, 1)

                x_max(0)
                x_max(1)
                x_scale(0)
                x_scale(1)
                x_max(2)
                x_copy(0)
                x_scale(2)
                x_max(3)
                x_copy(1)
                x_copy(2)
                x_scale(3)
                x_copy(3)
                for n in (0, 1):
                    name = f"xo{l}_{n}"
                    for j in range(4):
                        dve.wait_ge(evac_a, ACT_BEFORE[name] + j + 1)
                        low_part(fm_lo[:, 4 * n + j, :], bank(name, j), fm_hi[:, 4 * n + j, :], evac_d)
                norm(l, 1, (f"wo{l}_0", f"wo{l}_1"))
                for n in range(FT // 2):
                    name = f"up{l}_{n}"
                    group_filled(dve, name)
                    for j in (0, 1):
                        i = l * FT + 2 * n + j
                        dve.wait_ge(evac_a, ACT_BEFORE[name] + j + 1)
                        if i >= 2:
                            dve.wait_ge(g_ready, i - 1)
                            dve.wait_ge(g_hi_ready, i - 1)
                        nc.vector.tensor_tensor(gf[:, j, :], silu[:, j, :], bank(name, 2 + j), ALU.mult).then_inc(evac_d, 1)
                    for j in (0, 1):
                        i = l * FT + 2 * n + j
                        dve.wait_ge(g_hi_ready, i + 1)
                        low_part(g_lo[:, 2 * n + j, :], gf[:, j, :], g_hi[:, 2 * n + j, :], g_ready)
                norm(l, 2, (f"dn{l}_0", f"dn{l}_1"))


INPUTS = ["x", "mem", "positions", "e_w_in", "e_pool_w", "e_pool_scale", "e_cmp_pos_k", "e_cmp_pos_v", "e_cmp_wk",
          "e_cmp_wv", "e_w_out", "o_w_in", "o_conv_w", "o_conv_b", "o_wa", "o_ba", "o_wx", "o_bx", "o_lambda",
          "o_w_out", "x_wq", "x_wkv", "x_wo", "f_w_up", "f_w_down", "ln_g", "ln_b"]


def kernel(**inputs):
    import concourse.bacc as bacc
    from concourse.bass_utils import run_bass_kernel_spmd

    nc = bacc.Bacc("TRN2", target_bir_lowering=False, num_devices=1)
    arrays, aps = {}, {}
    for name in INPUTS + ["consts"]:
        v = shape_constants() if name == "consts" else np.ascontiguousarray(inputs[name])
        arrays[f"in_{name}"] = v
        aps[name] = nc.dram_tensor(f"in_{name}", v.shape, mybir.dt.from_np(v.dtype), kind="ExternalInput").ap()
    out = nc.dram_tensor("out_x", (1, SEQ, D), F32, kind="ExternalOutput").ap()
    hybrid_trunk(nc, aps, out)
    r = run_bass_kernel_spmd(nc, [arrays], core_ids=[0])
    return r.results[0]["out_x"]
```

```python
from contextlib import ExitStack

import numpy as np

import concourse.bass as bass
from concourse import mybir

F32 = mybir.dt.float32
F32R = mybir.dt.float32r
BF16 = mybir.dt.bfloat16
I32 = mybir.dt.int32
ALU = mybir.AluOpType
ACT = mybir.ActivationFunctionType
AX = mybir.AxisListType

P = 128
D = 1024
KT = D // P
SEQ = 512
TT = SEQ // P
MEM = 256
MT = MEM // P
DEPTH = 2
ALPHA = (2.0 * DEPTH) ** 0.25
EPS = 1e-5
NEG = -1e30
WINDOWS = (2, 4, 8, 16)
HEADS, KV_HEADS, HD = 8, 2, 64
GROUP = HEADS // KV_HEADS
GATES = HEADS * 3
CMP_BLOCK, CMP_STRIDE = 32, 16
NCMP = (SEQ - CMP_BLOCK) // CMP_STRIDE + 1
ROT = HD // 4
HALF = ROT // 2
RNN = 1280
RT = RNN // P
X_HEADS, X_HD = 4, D // 4
FFN = 2816
FT = FFN // P
PAD = 16
CONV = 4
COLS = 512
BANK = 512
RING = 4
HALVES = (slice(0, D // 2), slice(D // 2, D))

C_ID = 0
C_CAUSAL = C_ID + P
C_PINV = C_CAUSAL + P
C_INVF = C_PINV + 4 * PAD
C_CMASK = C_INVF + HALF
C_ROWOK = C_CMASK + TT * 32
C_SEL = C_ROWOK + TT
C_LOW = C_SEL + KT
C_END = C_LOW + 2

V_POSK, V_POSV = 0, CMP_BLOCK
V_PSCALE = 2 * CMP_BLOCK
V_CONVW = V_PSCALE + 4
V_CONVB = V_CONVW + CONV * RT
V_BA = V_CONVB + RT
V_BX = V_BA + RT
V_LAM = V_BX + RT
V_END = V_LAM + RT

E_GATE = 1024
E_KV = E_GATE + GATES
E_KS = E_KV + 256


def shape_constants():
    c = np.zeros((P, C_END), np.float32)
    c[:, C_ID:C_ID + P] = np.eye(P)
    q, k = np.arange(P)[:, None], np.arange(P)[None, :]
    c[:, C_CAUSAL:C_CAUSAL + P] = np.where(k <= q, 0.0, NEG)
    for g, w in enumerate(WINDOWS):
        c[:, C_PINV + g * PAD:C_PINV + (g + 1) * PAD] = 1.0 / np.minimum(np.arange(PAD) + 1, w)
    c[:, C_INVF:C_INVF + HALF] = np.float32(500000.0) ** (-np.arange(HALF, dtype=np.float32) * np.float32(2.0) / np.float32(ROT))
    for t in range(TT):
        ends = np.arange(32) * CMP_STRIDE + CMP_BLOCK - 1
        tok = t * P + np.arange(P)
        c[:, C_CMASK + t * 32:C_CMASK + (t + 1) * 32] = np.where(ends[None, :] <= tok[:, None], 0.0, NEG)
        c[:, C_ROWOK + t] = tok >= CMP_BLOCK - 1
    row = np.arange(P)
    c[:, C_SEL:C_SEL + KT] = row[:, None] % KT == np.arange(KT)
    c[:, C_LOW] = row // KT % 2
    c[:, C_LOW + 1] = 1 - 2 * c[:, C_LOW]
    return c


def plan_groups():
    g = [("x0", 0, 4, 4), ("x1", 0, 4, 4)]
    g += [("ein0", KT, 4, 0), ("tm", 0, 4, 4), ("ein1", KT, 4, 0), ("ein2", KT, 4, 0), ("ein3", KT, 4, 0)]
    g += [("k0_0", KT, 4, 0), ("mix", 0, 4, 4), ("tq0", 0, 2, 2), ("tq1", 0, 2, 2), ("tk", 0, 4, 4), ("cmp", 0, 3, 0), ("k0_1", KT, 4, 0), ("tkc", 0, 2, 0)]
    g += [("attn", 0, 0, 0), ("to", 0, 4, 4)]
    g += [("eout0", KT, 0, 4), ("eout1", KT, 0, 4)]
    def norm(l, i, fillers=(None, None)):
        groups = [(f"ln{l}{i}_0", 0, 8, 0), (f"ln{l}{i}_1", 0, 6, 2)] if l else [(f"ln{l}{i}_0", 0, 4, 4), (f"ln{l}{i}_1", 0, 4, 4)]
        return [f for f in fillers[:1] if f] + groups + [f for f in fillers[1:] if f]

    for l in range(DEPTH):
        if l:
            g += [("oin0", KT, 4, 0), ("oin1", KT, 4, 0), ("ra0", 0, 4, 0), ("ia0", 0, 4, 0)]
            g += [("oin2", KT, 4, 0), ("ra1", 0, 4, 0), ("ia1", 0, 4, 0)]
            g += [("oin3", KT, 4, 0), ("ra2", 0, 4, 0), ("oin4", KT, 4, 0)]
            g += [("oout0", RT, 0, 4), ("oout1", RT, 0, 4)]
            g += norm(1, 0)
        else:
            g += norm(0, 0, (("v0_0", KT, 2, 0), ("v0_1", KT, 2, 0)))
        g += [(f"q{l}_0", KT, 4, 4), (f"q{l}_1", KT, 4, 4), (f"xattn{l}", 0, 0, 0)]
        g += [(f"xo{l}_0", 0, 4, 4), (f"xo{l}_1", 0, 4, 4)]
        g += [(f"wo{l}_0", KT, 0, 4), (f"wo{l}_1", KT, 0, 4)]
        g += norm(l, 1) if l else norm(0, 1, (("k1_0", KT, 4, 0), ("k1_1", KT, 4, 0)))
        g += [(f"up{l}_{n}", KT, 2, 2) for n in range(FT // 2)]
        g += [(f"dn{l}_0", FT, 0, 4), (f"dn{l}_1", FT, 0, 4)]
        if l == 0:
            g += norm(0, 2, (("v1_0", KT, 2, 0), ("v1_1", KT, 2, 0)))
    return g


PLAN = plan_groups()
INDEX = {name: i for i, (name, _, _, _) in enumerate(PLAN)}
CHUNK0 = {name: sum(k for _, k, _, _ in PLAN[:i]) for name, i in INDEX.items()}
ACT_BEFORE = {name: sum(a for _, _, a, _ in PLAN[:i]) for name, i in INDEX.items()}
DVE_BEFORE = {name: sum(v for _, _, _, v in PLAN[:i]) for name, i in INDEX.items()}
ACT_AFTER = {name: ACT_BEFORE[name] + PLAN[i][2] for name, i in INDEX.items()}
DVE_AFTER = {name: DVE_BEFORE[name] + PLAN[i][3] for name, i in INDEX.items()}
RG_SETS = [(6, 4, "oin0", 0), (2, 4, "oin1", 0), (0, 2, "oin2", 2)]
GATE_SETS = [(8, 2, "oin2"), (4, 4, "oin3"), (0, 4, "oin4")]
Y_ORDER = [first + j for first, tiles, _ in GATE_SETS for j in range(tiles)]
POOL_AFTER = {"ln10_0": 4, "ln10_1": 6, "ln11_0": 10, "ln11_1": 12}
OIN_COL = [2048, 1536, 1024, 512, 0]
BRANCHES = ("sel", "win", "cmp")
UNIT_HEADS = [8, 4, 2, 2]
UNITS = [u for qb in range(TT) for u in
         [(qb, "cmp", 0, HEADS)] + [(qb, b, hh, UNIT_HEADS[qb]) for b in ("sel", "win")
                                    for hh in range(0, HEADS, UNIT_HEADS[qb])]]
GATE_OF = {"cmp": 0, "sel": 1, "win": 2}


def unit_width(u):
    return 32 if UNITS[u][1] == "cmp" else (UNITS[u][0] + 1) * P


def unit_blocks(u):
    qb, b, _, heads = UNITS[u]
    return [(kb, r) for kb in range(1 if b == "cmp" else qb + 1) for r in range(heads)]


assert all(4 < len(unit_blocks(u)) <= 8 for u in range(len(UNITS)))


def hybrid_trunk(nc, a, out):
    ctx = ExitStack()
    with ctx:
        def at(name, shape, dt, offset):
            return nc.alloc_sbuf_tensor_at(name, shape, dt, offset=offset)

        cur = [16512]

        def place(name, shape, dt):
            n = int(np.prod(shape[1:])) * mybir.dt.size(dt)
            o = cur[0]
            cur[0] += (n + 31) // 32 * 32
            return at(name, shape, dt, o), o

        x_res, _ = place("x_res", [P, TT, D], F32)
        fm_hi, _ = place("fm_hi", [P, KT, SEQ], F32R)
        fm_lo, _ = place("fm_lo", [P, KT, SEQ], F32R)
        w_raw, _ = place("w_raw", [P, RING, COLS], F32)
        w_hi, _ = place("w_hi", [P, RING, COLS], F32R)
        w_lo, _ = place("w_lo", [P, RING, COLS], F32R)
        k_mem, o_k = place("k_mem", [P, KT, MEM], F32)
        v_mem, o_v = place("v_mem", [P, MT, D], F32)
        consts, _ = place("consts", [P, C_END], F32)
        chan, _ = place("chan", [P, V_END], F32)
        ident_b, _ = place("ident_b", [P, P], BF16)
        causal_b, _ = place("causal_b", [P, P], BF16)
        cmask_b, _ = place("cmask_b", [P, TT, 32], BF16)
        stats, _ = place("stats", [P, TT, 2, 6], F32)
        mv, _ = place("mv", [P, TT, 2], F32)
        lnc, _ = place("lnc", [P, 4, TT], F32)
        negmax, _ = place("negmax", [P, 2, HEADS], F32)
        rowsum, _ = place("rowsum", [P, 2, HEADS], F32)
        weight, _ = place("weight", [P, 2, HEADS], F32)
        gates, _ = place("gates", [P, TT, GATES], F32)
        kcT, _ = place("kcT", [P, KV_HEADS, NCMP], F32)
        vc_tok, _ = place("vc_tok", [NCMP, KV_HEADS * HD], F32)
        trig, _ = place("trig", [P, 2, TT + 1, HALF], F32)
        lru_c, _ = place("lru_c", [P, 2, RT], F32)
        bias_sel, _ = place("bias_sel", [2 * KT, KT], F32R)
        ln_g, o_ln = place("ln_g", [P, D], F32)
        ln_b, _ = place("ln_b", [P, D], F32)
        bias_raw, _ = place("bias_raw", [2 * KT, P], F32)
        bias_hi, _ = place("bias_hi", [2 * KT, P], F32R)
        bias_rows, _ = place("bias_rows", [2 * KT, P], F32R)
        cur[0] = o_ln + 10 * 2 * P * 4
        m0 = cur[0]
        mem_hi, _ = place("mem_hi", [P, KT, MEM], F32R)
        mem_lo, _ = place("mem_lo", [P, KT, MEM], F32R)
        G = cur[0]
        g_hi = at("g_hi", [P, FT, SEQ], F32R, G)
        g_lo = at("g_lo", [P, FT, SEQ], F32R, G + FT * SEQ * 4)
        assert G + 2 * FT * SEQ * 4 <= 229344, G + 2 * FT * SEQ * 4
        q_tok = at("q_tok", [P, TT, HEADS, 2, HD], F32R, G)
        o_tok = at("o_tok", [P, TT, 512], F32, G)
        o_tmp = at("o_tmp", [P, HEADS * HD], F32, G + 8192)
        kc_tok = at("kc_tok", [NCMP, KV_HEADS, HD], F32, G + 12288)
        kc_dup = at("kc_dup", [NCMP, KV_HEADS, 2, HD], F32, G + 12800)
        kc_tmp = at("kc_tmp", [NCMP, 3, KV_HEADS * HALF], F32, G + 13824)
        kv_tok = at("kv_tok", [P, TT, 512], F32, G + 16384)
        qT = at("qT", [P, HEADS, SEQ], F32R, G + 24576)
        pool_w = at("pool_w", [P, 4, P], F32, G + 24576)
        kT_hi = at("kT_hi", [P, 2, KV_HEADS, SEQ], F32R, G + 40960)
        kT_lo = at("kT_lo", [P, 2, KV_HEADS, SEQ], F32R, G + 49152)
        pool_in = at("pool_in", [P, 4, PAD + SEQ], F32, G + 40960)
        pool_sum = at("pool_sum", [P, 2, PAD + SEQ], F32, G + 49408)
        rot_tmp = at("rot_tmp", [P, 3, TT * HEADS * HALF], F32, G + 53632)
        kdup = at("kdup", [P, 2, TT, KV_HEADS, 2, HD], F32, G + 57344)
        probs = at("probs", [P, 2, 2 * SEQ], F32, G + 57344)
        raw_pos = at("raw_pos", [P, 2, 2, SEQ], F32, G + 65536)
        probsT = at("probsT", [P, 2, 2 * TT, P], F32, G + 65536)
        cmp_w = at("cmp_w", [P, 2, CMP_BLOCK, HD], F32, G + 73728)
        gateT = at("gateT", [GATES, SEQ], F32, o_v)
        raw_cmp = at("raw_cmp", [P, 2, SEQ], F32, o_v + 2048)
        mem_tok = at("mem_tok", [P, MT, D], F32, G)
        rows_posk = at("rows_posk", [CMP_BLOCK, 2, HD], F32, G + 28672)
        rows_posv = at("rows_posv", [CMP_BLOCK, 2, HD], F32, G + 29184)
        rows_ps = at("rows_ps", [4, P], F32, G + 29696)
        rows_rg = at("rows_rg", [V_END - V_CONVW, P], F32, G + 30208)
        pos_i = at("pos_i", [P, TT + 1], I32, G + 16384)
        pos_f = at("pos_f", [P, TT + 1], F32, G + 16416)
        ang = at("ang", [P, 4, (TT + 1) * HALF], F32, G + 16448)
        turned_raw = at("turned_raw", [P, TT - 1, KT, P], F32, G + 16384)
        q_hi = at("q_hi", [P, KT, SEQ], F32R, G)
        q_lo = at("q_lo", [P, KT, SEQ], F32R, G + 16384)
        pxT_hi = at("pxT_hi", [P, MT, X_HEADS, SEQ], F32R, G + 32768)
        pxT_lo = at("pxT_lo", [P, MT, X_HEADS, SEQ], F32R, G + 49152)
        px = at("px", [P, 2, X_HEADS, MEM], F32, G + 65536)
        k_hi = at("k_hi", [P, KT, MEM], F32R, G + 73728)
        k_lo = at("k_lo", [P, KT, MEM], F32R, o_k)
        v_hi = at("v_hi", [P, MT, D], F32R, G + 81920)
        v_lo = at("v_lo", [P, MT, D], F32R, o_v)
        silu = at("silu", [P, 2, SEQ], F32, o_v)
        gf = at("gf", [P, 2, SEQ], F32, o_v + 4096)
        R = m0
        x_pad = at("x_pad", [P, 2, 4, CONV - 1 + SEQ], F32, R)
        ra = at("ra", [P, 4, SEQ], F32, R + 16512)
        ib = at("ib", [P, 4, SEQ], F32, R + 16512 + 8192)
        tm = at("tm", [P, 4, SEQ], F32, R + 16512 + 2 * 8192)
        h = at("h", [P, RT, SEQ], F32, R + 16512 + 3 * 8192)
        y_hi = at("y_hi", [P, RT, SEQ], F32R, R + 61568)
        y_lo = at("y_lo", [P, RT, SEQ], F32R, R + 82048)
        gelu = at("gelu", [P, RT, SEQ], F32, R + 61568)
        ra_alt = at("ra_alt", [P, 4, SEQ], F32, R + 82048)
        ib_alt = at("ib_alt", [P, 4, SEQ], F32, R + 82048 + 8192)
        RA, IB = (ra, ra_alt, ra), (ib, ib_alt, ib)
        a_sq = at("a_sq", [P, SEQ], F32, R + 102528)
        w_gates = at("w_gates", [P, 2, RT, P], F32, o_ln)
        keep = at("keep", [P, SEQ], F32, R + 104576)
        posb = at("posb", [P, SEQ], I32, R + 82048)
        assert R + 104576 + 2048 <= 229344, R + 106624

        ps = ctx.enter_context(nc.psum_tensor("ps", [P, 8, BANK], F32))

        def sem(name):
            return ctx.enter_context(nc.semaphore(name))

        w_landed = [sem(f"w_landed{i}") for i in range(RING)]
        s_x = [sem(f"s_x{t}") for t in range(TT)]
        s_consts, s_mem, s_rows, s_pos = sem("s_consts"), sem("s_mem"), sem("s_rows"), sem("s_pos")
        s_cmpw, s_poolw, s_lnp = sem("s_cmpw"), sem("s_poolw"), sem("s_lnp")
        s_wgates, s_posb, s_out = sem("s_wgates"), sem("s_posb"), sem("s_out")
        w_rounded, w_split, w_used = sem("w_rounded"), sem("w_split"), sem("w_used")
        tile_filled = sem("tile_filled")
        filled, evac_a, evac_d, lows_p = sem("filled"), sem("evac_a"), sem("evac_d"), sem("lows_p")
        a_chain, d_chain = sem("a_chain"), sem("d_chain")
        tables_ready, ang_ready, trig_ready, pads_ready = sem("tables_ready"), sem("ang_ready"), sem("trig_ready"), sem("pads_ready")
        pooled_ready, q_rotated, q_hi_ready, q_ready = sem("pooled_ready"), sem("q_rotated"), sem("q_hi_ready"), sem("q_ready")
        kdup_ready, rawpos_ready, kcdup_ready = sem("kdup_ready"), sem("rawpos_ready"), sem("kcdup_ready")
        scored, maxed, exped, turned = sem("scored"), sem("maxed"), sem("exped"), sem("turned")
        copied_d, copied_a, summed = sem("copied_d"), sem("copied_a"), sem("summed")
        pv_done, o_evac, o_ready = sem("pv_done"), sem("o_evac"), sem("o_ready")
        kv_hi_ready, kv_ready = sem("kv_hi_ready"), sem("kv_ready")
        x_scored, x_maxed, x_exped, x_scaled = sem("x_scored"), sem("x_maxed"), sem("x_exped"), sem("x_scaled")
        x_turned, x_rounded, x_split = sem("x_turned"), sem("x_rounded"), sem("x_split")
        ln_var, ln_sd, ln_coef, x_ready = sem("ln_var"), sem("ln_sd"), sem("ln_coef"), sem("x_ready")
        bias_ready, tile_turned = sem("bias_ready"), sem("tile_turned")
        x_whole, x_whole_pool = sem("x_whole"), sem("x_whole_pool")
        g_hi_ready, g_ready = sem("g_hi_ready"), sem("g_ready")
        sp_ready, sp_exp, lru_ready = sem("sp_ready"), sem("sp_exp"), sem("lru_ready")
        conv_ready, decay_ready, m2_ready, mult_ready = sem("conv_ready"), sem("decay_ready"), sem("m2_ready"), sem("mult_ready")
        h_ready, y_full, y_hi_ready, y_ready = sem("h_ready"), sem("y_full"), sem("y_hi_ready"), sem("y_ready")

        block = ctx.enter_context(nc.Block())

        ident = consts[:, C_ID:C_ID + P]

        def chunk_sources():
            def rows(w, k, cols, n):
                return [(w[k * P:(k + 1) * P, cols:cols + n], 0, n)]
            for name, steps, _, _ in PLAN:
                for k in range(steps):
                    kind, n = name.split("_")[0], int(name.split("_")[1]) if "_" in name else 0
                    if name in ("ein0", "ein1"):
                        yield rows(a["e_w_in"][0], k, 512 * int(name[3]), 512)
                    elif name == "ein2":
                        yield rows(a["e_w_in"][0], k, E_KS, 512)
                    elif name == "ein3":
                        yield rows(a["e_w_in"][0], k, E_GATE, GATES + 256)
                    elif name[:4] == "eout":
                        yield rows(a["e_w_out"][0], k, 512 * int(name[4]), 512)
                    elif name[:4] == "oout":
                        yield rows(a["o_w_out"][0], Y_ORDER[k], 512 * int(name[4]), 512)
                    elif name[:3] == "oin":
                        yield rows(a["o_w_in"][0], k, OIN_COL[int(name[3])], 512)
                    elif kind[0] == "k":
                        yield rows(a["x_wkv"][int(kind[1])], k, 512 * n, 512)
                    elif kind[0] == "v":
                        yield rows(a["x_wkv"][int(kind[1])], k, D + 512 * n, 512)
                    elif kind[0] == "q":
                        yield rows(a["x_wq"][int(kind[1])], k, 512 * n, 512)
                    elif kind[:2] == "wo":
                        yield rows(a["x_wo"][int(kind[2])], k, 512 * n, 512)
                    elif kind[:2] == "dn":
                        yield rows(a["f_w_down"][int(kind[2])], k, 512 * n, 512)
                    else:
                        assert kind[:2] == "up", name
                        w = a["f_w_up"][int(kind[2])]
                        yield [(w[k * P:(k + 1) * P, 256 * n:256 * n + 256], 0, 256),
                               (w[k * P:(k + 1) * P, FFN + 256 * n:FFN + 256 * n + 256], 256, 256)]

        CHUNKS = list(chunk_sources())
        LANDS = [0] * RING
        LANDED = []
        for c, pieces in enumerate(CHUNKS):
            LANDS[c % RING] += 16 * len(pieces)
            LANDED.append(LANDS[c % RING])
        WIDTH = [sum(n for _, _, n in pieces) for pieces in CHUNKS]

        UP_FIRST = 3
        UP_PAIRS = (FT // 2 - UP_FIRST) // 2
        PAIR_CHUNKS, PAIR_EVACS, PAIR_TILES = 2 * KT, 4, 4
        PAIR_LANDS = PAIR_CHUNKS // RING * 32
        assert PAIR_CHUNKS % RING == 0 and UP_FIRST + 2 * UP_PAIRS == FT // 2

        TURNED = {}
        for name, steps, na, nd in PLAN:
            if name == "k0_0":
                TURNED["chan"] = len(TURNED) + 1
            if steps == 0 and "attn" not in name and name[:2] != "ln":
                TURNED[name] = len(TURNED) + 1

        @block.sync
        def _(sp):
            sp.dma_start(consts[:, :], a["consts"]).then_inc(s_consts, 16)
            for t in range(TT):
                sp.dma_start(x_res[:, t, :], a["x"][0, t * P:(t + 1) * P, :]).then_inc(s_x[t], 16)

            def weights(first, last):
                for c in range(first, last):
                    if c >= RING:
                        sp.wait_ge(w_split, c - RING + 1)
                    for src, o, n in CHUNKS[c]:
                        sp.dma_start(w_raw[:, c % RING, o:o + n], src).then_inc(w_landed[c % RING], 16)

            def up_weights(l):
                weights(CHUNK0[f"up{l}_1"], CHUNK0[f"up{l}_{UP_FIRST}"])
                w = a["f_w_up"][l]
                with sp.Fori(0, UP_PAIRS) as m:
                    for i in range(PAIR_CHUNKS):
                        c, k, col = CHUNK0[f"up{l}_{UP_FIRST}"] + i, i % KT, 256 * (UP_FIRST + i // KT)
                        sp.wait_ge(w_split, c - RING + 1 + PAIR_CHUNKS * m)
                        for part in (0, 1):
                            sp.dma_start(w_raw[:, c % RING, 256 * part:256 * part + 256],
                                         w[k * P:(k + 1) * P, bass.ds(FFN * part + col + 512 * m, 256)]).then_inc(w_landed[c % RING], 16)

            def ln_params(l, i):
                sp.dma_start(ln_g[:, :], a["ln_g"][l, i].partition_broadcast(P)).then_inc(s_lnp, 16)
                sp.dma_start(ln_b[:, :], a["ln_b"][l, i].partition_broadcast(P)).then_inc(s_lnp, 16)
                for half in (0, 1):
                    sp.dma_start(bias_raw[half * KT:(half + 1) * KT, :],
                                 a["ln_b"][l, i].rearrange("(k p) -> k p", p=P)).then_inc(s_lnp, 16)

            weights(0, RING)
            sp.dma_start(pos_i[:, 0:TT], a["positions"][0].rearrange("(t p) -> p t", p=P),
                         allow_slow_non_contiguous=True).then_inc(s_pos, 16)
            sp.dma_start(pos_i[0:NCMP, TT:TT + 1],
                         a["positions"][0, CMP_BLOCK - 1:SEQ].rearrange("(n o) -> n o", o=1)[::CMP_STRIDE, :],
                         allow_slow_non_contiguous=True).then_inc(s_pos, 16)
            sp.dma_start(mem_tok[:, :, :], a["mem"][0].rearrange("(t p) d -> p t d", p=P)).then_inc(s_mem, 16)
            pieces = [(cmp_w[half * HD:(half + 1) * HD, n, :, :], a[name][0].rearrange("(l d) e -> d l e", d=HD), s_cmpw)
                      for half in (0, 1) for n, name in enumerate(("e_cmp_wk", "e_cmp_wv"))]
            pieces.append((pool_w[:, :, :], a["e_pool_w"][0].rearrange("g c d -> c g d"), s_poolw))
            done = RING
            for i, (dst, src, signal) in enumerate(pieces):
                weights(done, CHUNK0["ein1"] + 2 * i)
                done = CHUNK0["ein1"] + 2 * i
                sp.dma_start(dst, src).then_inc(signal, 16)
            weights(done, CHUNK0["ein3"])
            ln_params(0, 0)
            weights(CHUNK0["ein3"], CHUNK0["q0_1"])
            sp.wait_ge(x_whole, TT * 1)
            ln_params(0, 1)
            weights(CHUNK0["q0_1"], CHUNK0["up0_1"])
            sp.wait_ge(x_whole, TT * 2)
            ln_params(0, 2)
            up_weights(0)
            weights(CHUNK0["dn0_0"], CHUNK0["oin1"])
            sp.wait_ge(x_whole, TT * 3)
            sp.dma_start(w_gates[:, 0, :, :], a["o_wa"][0].rearrange("h i j -> i h j")).then_inc(s_wgates, 16)
            sp.dma_start(w_gates[:, 1, :, :], a["o_wx"][0].rearrange("h i j -> i h j")).then_inc(s_wgates, 16)
            sp.dma_start(posb[:, :], a["positions"][0].partition_broadcast(P)).then_inc(s_posb, 16)
            weights(CHUNK0["oin1"], CHUNK0["oout0"])
            sp.wait_ge(filled, TURNED["ra2"])
            ln_params(1, 0)
            weights(CHUNK0["oout0"], CHUNK0["q1_1"])
            sp.wait_ge(x_whole, TT * 4)
            ln_params(1, 1)
            weights(CHUNK0["q1_1"], CHUNK0["up1_1"])
            sp.wait_ge(x_whole, TT * 5)
            ln_params(1, 2)
            up_weights(1)
            weights(CHUNK0["dn1_0"], len(CHUNKS))
            for t in range(TT - 1):
                sp.wait_ge(x_whole_pool, t + 1)
                part = HALVES[0] if t == TT - 2 else slice(0, D)
                sp.dma_start(out[0, t * P:(t + 1) * P, part], x_res[:, t, part]).then_inc(s_out, 16)
            for n, (t, part) in enumerate(((TT - 2, HALVES[1]), (TT - 1, HALVES[0]), (TT - 1, HALVES[1]))):
                sp.wait_ge(x_whole, TT * (3 * DEPTH - 1) + n + 1)
                sp.dma_start(out[0, t * P:(t + 1) * P, part], x_res[:, t, part]).then_inc(s_out, 16)
            sp.wait_ge(s_out, 16 * (TT + 2))

        def group_filled(eng, name):
            if PLAN[INDEX[name]][1]:
                eng.wait_ge(w_used, CHUNK0[name] + PLAN[INDEX[name]][1])
            else:
                eng.wait_ge(filled, TURNED[name])

        def probs_of(u, r):
            n = unit_width(u)
            return probs[:, u % 2, r * n:(r + 1) * n]

        def bank(name, j):
            return ps[:, 4 * (INDEX[name] % 2) + j, :]

        def tile_of(g, tile, m):
            return g[:, tile, :] if isinstance(m, int) else g[:, bass.ds(tile + PAIR_TILES * m, 1), :].rearrange("p o s -> p (o s)")

        def x_halves(l):
            return 4 * (INDEX[f"q{l}_0"] % 2), 4 * (INDEX[f"q{l}_1"] % 2)

        def fm_target(tile_hi, name, j):
            t, k = 2 * int(name[-1] if name != "tm" else 0) + j // 2, 4 * (j % 2)
            return tile_hi[:, k:k + 4, t * P:(t + 1) * P]

        def quarter(p):
            return p.rearrange("p (k s) -> p k s", s=P)

        @block.gpsimd
        def _(pool):
            for half in (0, 1):
                pool.dma_start(rows_posk[:, half, :], a["e_cmp_pos_k"][0]).then_inc(s_rows, 16)
                pool.dma_start(rows_posv[:, half, :], a["e_cmp_pos_v"][0]).then_inc(s_rows, 16)
            pool.dma_start(rows_ps[:, :], a["e_pool_scale"][0].rearrange("(g p) -> g p", p=P)).then_inc(s_rows, 16)
            pool.dma_start(rows_rg[0:CONV * RT, :], a["o_conv_w"][0].rearrange("n (j p) -> (n j) p", p=P)).then_inc(s_rows, 16)
            for n, name in enumerate(("o_conv_b", "o_ba", "o_bx", "o_lambda")):
                pool.dma_start(rows_rg[(CONV + n) * RT:(CONV + n + 1) * RT, :],
                               a[name][0].rearrange("(j p) -> j p", p=P)).then_inc(s_rows, 16)
            def split(first, last, m=0):
                for c in range(first, last):
                    for i, following in enumerate(("q1_0", "up1_0")):
                        if c == CHUNK0[following] + RING:
                            turned_lows(i)
                    s, n = c % RING, WIDTH[c]
                    pool.wait_ge(w_rounded, c + 1 + RING * m)
                    nc.gpsimd.tensor_tensor(w_lo[:, s, :n], w_raw[:, s, :n], w_hi[:, s, :n].bitcast(F32),
                                            ALU.subtract).then_inc(w_split, 1)

            def turned_lows(i):
                for t in range(TT - 1):
                    name = f"ln1{i}_{t // 2}"
                    for j in (2 * (t % 2), 2 * (t % 2) + 1):
                        pool.wait_ge(evac_a, ACT_BEFORE[name] + 2 * j + 2)
                        nc.gpsimd.tensor_tensor(fm_target(fm_lo, name, j), turned_raw[:, t, 4 * (j % 2):4 * (j % 2) + 4, :],
                                                fm_target(fm_hi, name, j).bitcast(F32), ALU.subtract).then_inc(lows_p, 1)

            done = 0
            for l in range(DEPTH):
                first, last = CHUNK0[f"up{l}_{UP_FIRST}"], CHUNK0[f"v1_1" if l == 0 else "dn1_1"]
                last = first + (last - first) // RING * RING
                split(done, first)
                with pool.Fori(0, (last - first) // RING) as m:
                    split(first, first + RING, m)
                done = last
            split(done, len(CHUNKS))
            pool.wait_ge(s_lnp, 64 * 3 * DEPTH)
            for t in range(TT - 1):
                part = HALVES[0] if t == TT - 2 else slice(0, D)
                pool.wait_ge(x_ready, TT * (3 * DEPTH - 1) + t + 1)
                nc.gpsimd.tensor_tensor(x_res[:, t, part], x_res[:, t, part], ln_b[:, part], ALU.add).then_inc(x_whole_pool, 1)

        @block.tensor
        def _(pe):
            def begin(name, m=0):
                i = INDEX[name]
                if i >= 2:
                    evacuated(PLAN[i - 2][0], m)
                return 4 * (i % 2)

            def evacuated(name, m=0):
                if ACT_AFTER[name]:
                    pe.wait_ge(evac_a, ACT_AFTER[name] + PAIR_EVACS * m)
                if DVE_AFTER[name]:
                    pe.wait_ge(evac_d, DVE_AFTER[name] + PAIR_EVACS * m)
                if name in POOL_AFTER:
                    pe.wait_ge(lows_p, POOL_AFTER[name])

            def passes(outp, k, steps, w, x, w_first, clear=True):
                for n, (i, j) in enumerate(((0, 0), (0, 1), (1, 0))):
                    lhsT, rhs = (w[i], x[j]) if w_first else (x[j], w[i])
                    last = nc.tensor.matmul(outp, lhsT, rhs, start=(clear and k == 0 and n == 0),
                                            stop=(k == steps - 1 and n == 2), skip_group_check=True)
                return last

            def keep_clock(b, n):
                for _ in range(n):
                    nc.tensor.matmul(ps[:, b, :].rearrange("p (k s) -> p k s", s=P), ident_b[:, :],
                                     ident_b[:, :].unsqueeze(1).to_broadcast([P, 4, P]), start=True, stop=True,
                                     skip_group_check=True)

            def turn(out_, in_, n=P):
                return nc.tensor.transpose(out_, in_, ident[0:n, 0:n])

            def turn_tokens(name, tok, tiles):
                b0 = begin(name)
                for i, t in enumerate(tiles):
                    for k in range(KT):
                        last = turn(ps[:, b0 + 2 * i + k // 4, (k % 4) * P:(k % 4 + 1) * P], tok[:, t, k * P:(k + 1) * P])
                last.then_inc(filled, 1)

            fm = (fm_hi, fm_lo)
            mem = (mem_hi, mem_lo)

            def product(name, act, tokens, feature_major, col0=(0, P, 2 * P, 3 * P), ready=None, order=None, early=0, m=0,
                        by_tile=False):
                b0, steps = 4 * (INDEX[name] % 2) if early else begin(name, m), PLAN[INDEX[name]][1]
                hi, lo = act
                for k in range(steps):
                    c = CHUNK0[name] + k
                    s, n = c % RING, WIDTH[c]
                    pe.wait_ge(w_split, c + 1 + PAIR_CHUNKS * m)
                    if ready:
                        ready(k)
                    kk = order[k] if order else k
                    nb = len(col0) if feature_major else tokens // P
                    for j in range(nb):
                        if feature_major:
                            w = [w_[:, s, col0[j]:col0[j] + P] for w_ in (w_hi, w_lo)]
                            if k < early:
                                last = passes(ps[:, b0 + j, tokens // 2:tokens], k, steps, w,
                                              [x_[:, kk, tokens // 2:tokens] for x_ in (hi, lo)], True, clear=False)
                            else:
                                last = passes(ps[:, b0 + j, :tokens], k, steps, w, (hi[:, kk, :], lo[:, kk, :]), True)
                        else:
                            x = [x_[:, kk, j * P:(j + 1) * P] for x_ in (hi, lo)]
                            last = passes(ps[:, b0 + j, :n], k, steps, (w_hi[:, s, :n], w_lo[:, s, :n]), x, False)
                            if by_tile and k == steps - 1 and j < nb - 1:
                                last.then_inc(tile_filled, 1)
                    last.then_inc(w_used, 1)

            def early_half(name, k0, k1):
                b0 = 4 * (INDEX[name] % 2)
                for k in range(k0, k1):
                    c = CHUNK0[name] + k
                    pe.wait_ge(w_split, c + 1)
                    for j in range(4):
                        w = [w_[:, c % RING, j * P:(j + 1) * P] for w_ in (w_hi, w_lo)]
                        passes(ps[:, b0 + j, :SEQ // 2], k, KT, w, [x_[:, k, :SEQ // 2] for x_ in fm], True)

            pe.wait_ge(s_consts, 16)
            pe.wait_ge(s_x[0], 16)
            pe.wait_ge(s_x[1], 16)
            turn_tokens("x0", x_res, (0, 1))
            pe.wait_ge(s_x[2], 16)
            pe.wait_ge(s_x[3], 16)
            turn_tokens("x1", x_res, (2, 3))

            evacuated("x0")
            early_half("ein0", 0, RING)
            evacuated("x1")
            product("ein0", fm, SEQ, True, early=RING)
            pe.wait_ge(s_mem, 16)
            turn_tokens("tm", mem_tok, (0, 1))
            product("ein1", fm, SEQ, False)
            product("ein2", fm, SEQ, False)
            product("ein3", fm, SEQ, True, (0, GATES, GATES + P))
            b0 = 4 * (INDEX["ein3"] % 2) + 3
            pe.wait_ge(s_rows, 16 * 10)
            turn(ps[:, b0, V_POSK:V_POSK + CMP_BLOCK], rows_posk[:, :, :].rearrange("l a d -> l (a d)"), CMP_BLOCK)
            turn(ps[:, b0, V_POSV:V_POSV + CMP_BLOCK], rows_posv[:, :, :].rearrange("l a d -> l (a d)"), CMP_BLOCK)
            turn(ps[:, b0, V_PSCALE:V_PSCALE + 4], rows_ps[:, :], 4)
            turn(ps[:, b0, V_CONVW:V_END], rows_rg[:, :], V_END - V_CONVW).then_inc(filled, 1)
            product("k0_0", mem, MEM, True)
            b0 = begin("mix")
            pe.wait_ge(s_poolw, 16)
            pe.wait_ge(pooled_ready, 4)
            for g in range(4):
                last = nc.tensor.matmul(ps[:, b0 + g, :], pool_w[:, g, :], pool_in[:, g, PAD:], start=True, stop=True)
            last.then_inc(filled, 1)
            pe.wait_ge(q_ready, 1)
            for n in (0, 1):
                b0 = begin(f"tq{n}")
                for j in range(4):
                    for t in range(TT):
                        hh = 4 * n + j
                        last = turn(ps[:, b0 + j, t * P:(t + 1) * P], q_tok[:, t, hh, :, :].rearrange("p i d -> p (i d)").bitcast(F32))
                last.then_inc(filled, 1)
            b0 = begin("tk")
            pe.wait_ge(kdup_ready, 2)
            for b in (0, 1):
                for g in range(KV_HEADS):
                    for t in range(TT):
                        last = turn(ps[:, b0 + 2 * b + g, t * P:(t + 1) * P],
                                    kdup[:, b, t, g, :, :].rearrange("p a d -> p (a d)"))
            last.then_inc(filled, 1)
            b0 = begin("cmp")
            pe.wait_ge(rawpos_ready, 4)
            pe.wait_ge(s_cmpw, 64)
            for n in (0, 1):
                for g in range(KV_HEADS):
                    half = slice(g * HD, (g + 1) * HD)
                    for l in range(CMP_BLOCK):
                        src = raw_pos[half, n, l // CMP_STRIDE, l:l + (NCMP - 1) * CMP_STRIDE + 1:CMP_STRIDE]
                        nc.tensor.matmul(ps[0:NCMP, b0 + g, n * HD:(n + 1) * HD], src, cmp_w[half, n, l, :],
                                         start=(l == 0), stop=(l == CMP_BLOCK - 1))
            for t in range(TT):
                last = turn(ps[:, b0 + 2, t * GATES:(t + 1) * GATES], gateT[:, t * P:(t + 1) * P], GATES)
            last.then_inc(filled, 1)
            product("k0_1", mem, MEM, True)
            b0 = begin("tkc")
            pe.wait_ge(kcdup_ready, 1)
            for g in range(KV_HEADS):
                last = turn(ps[:, b0 + g, 0:NCMP], kc_dup[:, g, :, :].rearrange("p a d -> p (a d)"), NCMP)
            last.then_inc(filled, 1)

            evacuated("tkc")
            pe.wait_ge(tables_ready, 3)

            def scores(u):
                qb, b, h0, heads = UNITS[u]
                b0 = 2 * (u % 2)
                if b == "cmp":
                    for i in (0, 1):
                        nc.tensor.matmul(ps[:, b0 + i, 0:P].rearrange("p (r n) -> p r n", n=32)[:, :, 0:NCMP], ident_b[:, :],
                                         cmask_b[:, qb, 0:NCMP].unsqueeze(1).to_broadcast([P, HEADS // 2, NCMP]),
                                         start=True, stop=False, skip_group_check=True)
                for hh in range(h0, h0 + heads):
                    c0 = (hh - h0) // 2 * unit_width(u)
                    q, g, bank_ = qT[:, hh, qb * P:(qb + 1) * P], hh // GROUP, b0 + hh % 2
                    if b == "cmp":
                        last = nc.tensor.matmul(ps[:, bank_, c0:c0 + NCMP], q.bitcast(F32), kcT[:, g, :], start=False, stop=True,
                                                skip_group_check=True)
                    else:
                        n = (qb + 1) * P
                        m = max(n, 2 * P) if c0 + 2 * P <= BANK else n
                        for i, k_ in enumerate((kT_hi, kT_lo)):
                            nc.tensor.matmul(ps[:, bank_, c0:c0 + m], q, k_[:, BRANCHES.index(b), g, :m], start=(i == 0),
                                             stop=False, skip_group_check=True)
                        last = nc.tensor.matmul(ps[:, bank_, c0 + qb * P:c0 + n], ident_b[:, :], causal_b[:, :], start=False,
                                                stop=True, skip_group_check=True)
                last.then_inc(scored, 1)

            def turn_probs(u):
                qb, b, h0, heads = UNITS[u]
                pe.wait_ge(exped, u + 1)
                blocks = unit_blocks(u)
                n = NCMP if b == "cmp" else P
                for j in (0, 4):
                    if u:
                        pe.wait_ge(copied_a if j else copied_d, u)
                    for jj, (kb, r) in enumerate(blocks[j:j + 4]):
                        p = probs_of(u, r)[:, kb * P:kb * P + n]
                        last = nc.tensor.matmul(ps[0:n, 4 + j // 4, jj * P:(jj + 1) * P], p, ident, start=True, stop=True,
                                                is_transpose=True if n == P else None)
                    last.then_inc(turned, 1)

            def weigh(u):
                qb, b, h0, heads = UNITS[u]
                pe.wait_ge(copied_d, u + 1)
                pe.wait_ge(copied_a, u + 1)
                if u >= 2:
                    pe.wait_ge(o_evac, u - 1)
                blocks = unit_blocks(u)
                for r in range(heads):
                    g = (h0 + r) // GROUP
                    mine = [(i, kb) for i, (kb, rr) in enumerate(blocks) if rr == r]
                    for i, kb in mine:
                        if b == "cmp":
                            p, v = probsT[0:NCMP, u % 2, i, :], vc_tok[:, g * HD:(g + 1) * HD]
                        else:
                            c0 = 256 * BRANCHES.index(b) + P + g * HD
                            p, v = probsT[:, u % 2, i, :], kv_tok[:, kb, c0:c0 + HD]
                        last = nc.tensor.matmul(ps[:, 6 + u % 2, r * HD:(r + 1) * HD], p, v, start=(i == mine[0][0]),
                                                stop=(i == mine[-1][0]))
                last.then_inc(pv_done, 1)

            scores(0)
            scores(1)
            for u in range(len(UNITS)):
                turn_probs(u)
                if u + 2 < len(UNITS):
                    scores(u + 2)
                weigh(u)
            pe.wait_ge(o_ready, len(UNITS) - TT)
            b0 = 4 * (INDEX["to"] % 2)
            for t in range(TT):
                for k in range(4):
                    last = turn(ps[:, b0 + t, k * P:(k + 1) * P], o_tok[:, t, k * P:(k + 1) * P])
            last.then_inc(filled, 1)
            product("eout0", fm, SEQ, False, ready=lambda k: evacuated(("mix", "to")[k // 4]) if k % 4 == 0 else None)
            product("eout1", fm, SEQ, False, by_tile=True)
            product("v0_0", mem, MEM, False)

            for l in range(DEPTH):
                if l:
                    def recurrence_gates(n):
                        first, tiles, _, _ = RG_SETS[n]
                        pe.wait_ge(s_wgates, 32)
                        pe.wait_ge(conv_ready, sum(s[1] for s in RG_SETS[:n + 1]))
                        for i, kind in enumerate(("ra", "ia")):
                            b0 = begin(f"{kind}{n}") if (n, i) != (2, 1) else b0 + tiles
                            for j in range(tiles):
                                last = nc.tensor.matmul(ps[:, b0 + j, :], w_gates[:, i, first + j, :], h[:, first + j, :],
                                                        start=True, stop=True)
                            if (n, i) != (2, 0):
                                last.then_inc(filled, 1)

                    product("oin0", fm, SEQ, True)
                    product("oin1", fm, SEQ, True)
                    recurrence_gates(0)
                    product("oin2", fm, SEQ, True)
                    recurrence_gates(1)
                    product("oin3", fm, SEQ, True)
                    recurrence_gates(2)
                    product("oin4", fm, SEQ, True)
                    for n in (0, 1):
                        product(f"oout{n}", (y_hi, y_lo), SEQ, False, order=Y_ORDER, by_tile=(n == 1),
                                ready=None if n else lambda k: pe.wait_ge(y_ready, k + 1))

                def turn_normed(i, following):
                    v = 3 * l + i
                    pe.wait_ge(bias_ready, v + 1)
                    for t in range(TT):
                        if t % 2 == 0:
                            b0 = begin(f"ln{l}{i}_{t // 2}")
                        if l:
                            keep_clock(b0 + 3, (16, 6, 6, 0)[t])
                        pe.wait_ge(x_ready, TT * v + t + 1)
                        for half in (0, 1):
                            dst = ps[:, b0 + 2 * (t % 2) + half, :]
                            for kk in range(4):
                                k = 4 * half + kk
                                nc.tensor.matmul(dst[:, kk * P:(kk + 1) * P], x_res[:, t, k * P:(k + 1) * P], ident,
                                                 start=(kk == 0), stop=False, is_transpose=True, skip_group_check=True)
                            last = nc.tensor.matmul(dst.rearrange("p (k s) -> p k s", s=P), bias_rows[:, :],
                                                    bias_sel[:, 4 * half:4 * half + 4].unsqueeze(2).to_broadcast([2 * KT, 4, P]),
                                                    start=False, stop=True, skip_group_check=True)
                        last.then_inc(tile_turned, 1)
                        if following and t >= 2:
                            if t == 2:
                                evacuated(f"ln{l}{i}_0")
                            early_half(following, *((0, 1), (1, RING))[t - 2])

                turn_normed(0, f"q{l}_0" if l else None)
                if l == 0:
                    product("v0_1", mem, MEM, False)
                evacuated(f"ln{l}0_1")
                product(f"q{l}_0", fm, SEQ, True, early=RING * l)
                product(f"q{l}_1", fm, SEQ, True)
                sb, tb = x_halves(l)

                def x_scores(u, heads):
                    for r in heads:
                        for k in (0, 1):
                            i = 2 * r + k
                            last = passes(ps[:, sb + 2 * (u % 2) + r // 2, (r % 2) * MEM:(r % 2 + 1) * MEM], k, 2,
                                          (k_hi[:, i, :], k_lo[:, i, :]), [q_[:, i, u * P:(u + 1) * P] for q_ in (q_hi, q_lo)], False)
                    return last

                def x_scores_again(u):
                    pe.wait_ge(x_exped, l * TT + u - 1)
                    x_scores(u, range(X_HEADS)).then_inc(x_scored, 1)

                def x_turn(u):
                    pe.wait_ge(x_scaled, l * TT + u + 1)
                    if u >= 2:
                        copied(u - 2)
                    for m in range(MT):
                        for r in range(X_HEADS):
                            last = turn(ps[:, tb + 2 * (u % 2) + m, r * P:(r + 1) * P], px[:, u % 2, r, m * P:(m + 1) * P])
                        last.then_inc(x_turned, 1)

                def copied(u):
                    pe.wait_ge(x_split, MT * (l * TT + u + 1))

                def x_weigh(b0, j, r, t0, t1):
                    for m in range(MT):
                        c0 = r * X_HD + (j % 2) * P
                        last = passes(ps[:, b0 + j, t0 * P:t1 * P], m, MT, [v_[:, m, c0:c0 + P] for v_ in (v_hi, v_lo)],
                                      [p_[:, m, r, t0 * P:t1 * P] for p_ in (pxT_hi, pxT_lo)], True, clear=(t0 == 0))
                    return last

                pe.wait_ge(kv_ready, 8 * (l + 1))
                evacuated(f"q{l}_0")
                x_scores(0, (0, 1))
                x_scores(1, (0, 1))
                evacuated(f"q{l}_1")
                x_scores(0, (2, 3)).then_inc(x_scored, 1)
                x_scores(1, (2, 3)).then_inc(x_scored, 1)
                x_scores_again(2)
                x_turn(0)
                x_scores_again(3)
                x_turn(1)
                x_turn(2)
                copied(1)
                for j in (0, 1):
                    x_weigh(sb, j, 2, 0, 2)
                copied(2)
                for j in (0, 1):
                    x_weigh(tb, j, 0, 0, 2)
                x_turn(TT - 1)
                for j in (2, 3):
                    x_weigh(sb, j, 3, 0, 2)
                copied(TT - 1)
                for j in (0, 1):
                    x_weigh(tb, j, 0, 2, TT)
                for j in (2, 3):
                    last = x_weigh(tb, j, 1, 0, TT)
                last.then_inc(filled, 1)
                for j in (0, 1):
                    x_weigh(sb, j, 2, 2, TT)
                for j in (2, 3):
                    last = x_weigh(sb, j, 3, 2, TT)
                last.then_inc(filled, 1)
                product(f"wo{l}_0", fm, SEQ, False, ready=lambda k: evacuated(f"xo{l}_{k // 4}") if k % 4 == 0 else None)
                product(f"wo{l}_1", fm, SEQ, False, by_tile=True)
                if l == 0:
                    product("k1_0", mem, MEM, True)
                turn_normed(1, f"up{l}_0" if l else None)
                if l == 0:
                    product("k1_1", mem, MEM, True)
                evacuated(f"ln{l}1_1")
                for n in range(UP_FIRST):
                    product(f"up{l}_{n}", fm, SEQ, True, early=0 if n else RING * l)
                with pe.Fori(0, UP_PAIRS) as m:
                    for n in (UP_FIRST, UP_FIRST + 1):
                        product(f"up{l}_{n}", fm, SEQ, True, m=m)
                product(f"dn{l}_0", (g_hi, g_lo), SEQ, False, ready=lambda k: pe.wait_ge(g_ready, l * FT + k + 1))
                product(f"dn{l}_1", (g_hi, g_lo), SEQ, False, by_tile=True)
                if l == 0:
                    product("v1_0", mem, MEM, False)
                    turn_normed(2, None)
                    product("v1_1", mem, MEM, False)
                    evacuated("ln02_1")

        @block.scalar
        def _(act):
            chain = [0]

            def settle(ins):
                chain[0] += 1
                ins.then_inc(a_chain, 1)
                act.wait_ge(a_chain, chain[0])

            rounded = [0]

            def round_chunk(c, m=0):
                s, n = c % RING, WIDTH[c]
                act.wait_ge(w_landed[s], LANDED[c] + PAIR_LANDS * m)
                if c >= RING:
                    act.wait_ge(w_used, c - RING + 1 + PAIR_CHUNKS * m)
                nc.scalar.activation(w_hi[:, s, :n], w_raw[:, s, :n], ACT.Copy).then_inc(w_rounded, 1)

            def round_weights(last):
                for c in range(rounded[0], min(last, len(CHUNKS))):
                    round_chunk(c)
                rounded[0] = max(rounded[0], last)

            def round_on(n, name, step=None):
                limit = CHUNK0[name] + (PLAN[INDEX[name]][1] if step is None else step) + RING - 1
                round_weights(min(rounded[0] + n, limit))

            def filled_by(name):
                round_weights(CHUNK0[name] + PLAN[INDEX[name]][1] + RING - 1)
                group_filled(act, name)

            def turn_evac(name, hi):
                filled_by(name)
                for j in range(4):
                    copy_turned(name, hi, j)

            def copy_turned(name, hi, j):
                nc.scalar.activation(fm_target(hi, name, j), quarter(bank(name, j)), ACT.Copy).then_inc(evac_a, 1)

            def keys_evac(l, n):
                filled_by(f"k{l}_{n}")
                for j in range(4):
                    nc.scalar.activation(k_mem[:, 4 * n + j, :], bank(f"k{l}_{n}", j)[:, :MEM], ACT.Copy).then_inc(evac_a, 1)

            for name in ("x0", "x1"):
                group_filled(act, name)
                if name == "x1":
                    round_weights(2)
                for j in range(4):
                    copy_turned(name, fm_hi, j)
            round_weights(RING)
            act.wait_ge(ang_ready, 1)
            nc.scalar.activation(trig[:, 1, :, :].rearrange("p t f -> p (t f)"), ang[:, 0, :], ACT.Sin).then_inc(trig_ready, 1)
            nc.scalar.activation(trig[:, 0, :, :].rearrange("p t f -> p (t f)"), ang[:, 1, :], ACT.Sin).then_inc(trig_ready, 1)
            act.wait_ge(pads_ready, 1)
            filled_by("ein0")
            for j in range(4):
                nc.scalar.activation(pool_in[:, j, PAD:], bank("ein0", j), ACT.Copy).then_inc(evac_a, 1)
            turn_evac("tm", mem_hi)
            filled_by("ein1")
            for j in range(4):
                nc.scalar.activation(q_tok[:, j, :, 1, :].bitcast(F32), bank("ein1", j).rearrange("p (h d) -> p h d", d=HD), ACT.Copy, scale=HD ** -0.5).then_inc(evac_a, 1)
            filled_by("ein2")
            for j in range(4):
                nc.scalar.activation(kv_tok[:, j, :], bank("ein2", j), ACT.Copy).then_inc(evac_a, 1)
            for t in range(TT):
                act.wait_ge(q_rotated, t + 1)
                nc.scalar.activation(q_tok[:, t, :, 0, :], q_tok[:, t, :, 1, :].bitcast(F32), ACT.Copy).then_inc(q_hi_ready, 1)
            filled_by("ein3")
            nc.scalar.activation(gateT[:, :], bank("ein3", 0)[0:GATES, :], ACT.Sigmoid).then_inc(evac_a, 1)
            for n in (0, 1):
                nc.scalar.activation(raw_cmp[:, n, :], bank("ein3", 1 + n), ACT.Copy).then_inc(evac_a, 1)
            act.wait_ge(filled, TURNED["chan"])
            nc.scalar.activation(chan[:, :], bank("ein3", 3)[:, 0:V_END], ACT.Copy).then_inc(evac_a, 1)
            keys_evac(0, 0)
            filled_by("mix")
            for j in range(4):
                nc.scalar.activation(fm_hi[:, j, :], bank("mix", j), ACT.Copy,
                                     scale=chan[:, V_PSCALE + j:V_PSCALE + j + 1]).then_inc(evac_a, 1)
            for n in (0, 1):
                filled_by(f"tq{n}")
                for j in (0, 1):
                    nc.scalar.activation(qT[:, 4 * n + j, :], bank(f"tq{n}", j), ACT.Copy).then_inc(evac_a, 1)
            filled_by("tk")
            for j in range(4):
                nc.scalar.activation(kT_hi[:, j // 2, j % 2, :], bank("tk", j), ACT.Copy).then_inc(evac_a, 1)
            filled_by("cmp")
            b0 = 4 * (INDEX["cmp"] % 2)
            cmp_banks = ps[0:NCMP, b0:b0 + 2, :]
            nc.scalar.activation(kc_tok[:, :, :], cmp_banks[:, :, 0:HD], ACT.Copy).then_inc(evac_a, 1)
            nc.scalar.activation(vc_tok[:, :].rearrange("n (g d) -> n g d", d=HD), cmp_banks[:, :, HD:2 * HD], ACT.Copy).then_inc(evac_a, 1)
            nc.scalar.activation(gates[:, :, :].rearrange("p t c -> p (t c)"), bank("cmp", 2)[:, 0:TT * GATES], ACT.Copy).then_inc(evac_a, 1)
            keys_evac(0, 1)
            filled_by("tkc")
            for g in range(KV_HEADS):
                nc.scalar.activation(kcT[:, g, :], bank("tkc", g)[:, 0:NCMP], ACT.Copy).then_inc(evac_a, 1)

            def exps(u):
                qb, b, h0, heads = UNITS[u]
                act.wait_ge(maxed, u + 1)
                for r in range(heads):
                    hh = h0 + r
                    n, c0 = NCMP if b == "cmp" else (qb + 1) * P, r // 2 * unit_width(u)
                    last = nc.scalar.activation(probs_of(u, r)[:, :n], ps[:, 2 * (u % 2) + hh % 2, c0:c0 + n], ACT.Exp,
                                                bias=negmax[:, u % 2, r:r + 1], accum_out=rowsum[:, u % 2, r:r + 1])
                last.then_inc(exped, 1)

            def turned_copy(u):
                n, m = NCMP if UNITS[u][1] == "cmp" else P, len(unit_blocks(u)) - 4
                act.wait_ge(turned, 2 * u + 2)
                nc.scalar.activation(probsT[0:n, u % 2, 4:4 + m, :].rearrange("p b q -> p (b q)"), ps[0:n, 5, 0:m * P],
                                     ACT.Copy).then_inc(copied_a, 1)

            exps(0)
            exps(1)
            for u in range(len(UNITS)):
                turned_copy(u)
                if u + 2 < len(UNITS):
                    act.wait_ge(summed, u + 1)
                    exps(u + 2)
            filled_by("to")
            for t in range(TT):
                nc.scalar.activation(fm_hi[:, 4:8, t * P:(t + 1) * P], quarter(bank("to", t)), ACT.Copy).then_inc(evac_a, 1)

            def values_evac(l, n):
                filled_by(f"v{l}_{n}")
                for m in range(MT):
                    nc.scalar.activation(v_mem[:, m, 512 * n:512 * (n + 1)], bank(f"v{l}_{n}", m), ACT.Copy).then_inc(evac_a, 1)

            def norm(l, i, fillers=None):
                v = 3 * l + i
                last = (("eout1", "oout1")[l], f"wo{l}_1", f"dn{l}_1")[i]
                round_weights(CHUNK0[last] + PLAN[INDEX[last]][1] + RING - (1 if fillers else 0))
                if fillers:
                    round_weights(rounded[0] + 2)
                settle(nc.scalar.activation(lnc[:, 1, 0:1], consts[:, C_ROWOK + 1:C_ROWOK + 2], ACT.Sqrt))

                def turned_copies(t):
                    act.wait_ge(tile_turned, TT * v + t + 1)
                    for j in (0, 1):
                        name, b = f"ln{l}{i}_{t // 2}", 2 * (t % 2) + j
                        copy_turned(name, fm_hi, b)
                        if l and t < TT - 1:
                            nc.scalar.activation(turned_raw[:, t, 4 * j:4 * j + 4, :], quarter(bank(name, b)), ACT.Copy).then_inc(evac_a, 1)

                for t in range(TT):
                    act.wait_ge(ln_var, TT * v + t + 1)
                    nc.scalar.activation(lnc[:, 1, t:t + 1], lnc[:, 0, t:t + 1], ACT.Sqrt).then_inc(ln_sd, 1)
                    if fillers:
                        round_weights(rounded[0] + 1)
                    act.wait_ge(ln_coef, TT * v + t + 1)
                    for part in HALVES if (l, i, t) == (DEPTH - 1, 2, TT - 1) else (slice(0, D),):
                        nc.scalar.activation(x_res[:, t, part], x_res[:, t, part], ACT.Copy, scale=lnc[:, 2, t:t + 1]).then_inc(x_ready, 1)
                    if fillers:
                        if t == TT - 2:
                            fillers[0]()
                        elif t < TT - 2:
                            round_weights(rounded[0] + 1)
                    elif t and (l, i) != (DEPTH - 1, 2):
                        turned_copies(t - 1)
                if fillers:
                    for t in range(TT):
                        turned_copies(t)
                    fillers[1]()
                elif (l, i) != (DEPTH - 1, 2):
                    turned_copies(TT - 1)

            for l in range(DEPTH):
                if l:
                    def gelus(n):
                        first, tiles, name = GATE_SETS[n]
                        filled_by(name)
                        for j in range(tiles):
                            nc.scalar.activation(gelu[:, first + j, :], bank(name, j), ACT.Gelu_apprx_tanh).then_inc(evac_a, 1)

                    def y_rounded(n, meanwhile):
                        first, tiles, _ = GATE_SETS[n]
                        for j in range(tiles):
                            i = sum(s[1] for s in GATE_SETS[:n]) + j
                            act.wait_ge(y_full, i + 1)
                            nc.scalar.activation(y_hi[:, first + j, :], h[:, first + j, :], ACT.Copy).then_inc(y_hi_ready, 1)
                            if n == 2:
                                round_on(1, "oout0", i)
                            elif j % 2:
                                round_on(1, meanwhile)

                    def x_evac(n):
                        first, tiles, name, b = RG_SETS[n]
                        if n >= 2:
                            act.wait_ge(conv_ready, sum(s[1] for s in RG_SETS[:n - 1]))
                        act.wait_ge(pads_ready, 2)
                        filled_by(name)
                        for j in range(tiles):
                            nc.scalar.activation(x_pad[:, n % 2, j, CONV - 1:], bank(name, b + j), ACT.Copy).then_inc(evac_a, 1)

                    def decays(n, meanwhile):
                        first, tiles, _, _ = RG_SETS[n]
                        filled_by(f"ra{n}")
                        for j in range(tiles):
                            nc.scalar.activation(RA[n][:, j, :], bank(f"ra{n}", j), ACT.Sigmoid,
                                                 bias=chan[:, V_BA + first + j:V_BA + first + j + 1]).then_inc(evac_a, 1)
                        round_on(1, meanwhile)
                        if n < 2:
                            group_filled(act, f"ia{n}")
                        for j in range(tiles):
                            src = bank(f"ia{n}", j) if n < 2 else bank("ra2", tiles + j)
                            nc.scalar.activation(IB[n][:, j, :], src, ACT.Sigmoid,
                                                 bias=chan[:, V_BX + first + j:V_BX + first + j + 1]).then_inc(evac_a, 1)
                        round_on(1, meanwhile)
                        act.wait_ge(evac_a, ACT_BEFORE[f"ra{n}"] + tiles)
                        act.wait_ge(lru_ready, 1)
                        for j in range(tiles):
                            if n:
                                act.wait_ge(h_ready, sum(s[1] for s in RG_SETS[:n - 1]) + j + 1)
                            last = nc.scalar.activation(tm[:, j, :], RA[n][:, j, :], ACT.Tanh, scale=lru_c[:, 0, first + j:first + j + 1])
                        settle(last)
                        round_on(1, meanwhile)
                        for j in range(tiles):
                            nc.scalar.activation(RA[n][:, j, :], RA[n][:, j, :], ACT.Exp,
                                                 scale=lru_c[:, 1, first + j:first + j + 1]).then_inc(decay_ready, 1)

                    def multipliers(n, meanwhile):
                        done = sum(s[1] for s in RG_SETS[:n])
                        for j in range(RG_SETS[n][1]):
                            round_on(1 + (j == 0), meanwhile)
                            act.wait_ge(m2_ready, done + j + 1)
                            nc.scalar.activation(tm[:, j, :], tm[:, j, :], ACT.Sqrt).then_inc(mult_ready, 1)

                    act.wait_ge(sp_ready, 1)
                    nc.scalar.activation(lru_c[:, 1, :], lru_c[:, 0, :], ACT.Exp).then_inc(sp_exp, 1)
                    x_evac(0)
                    x_evac(1)
                    decays(0, "oin2")
                    multipliers(0, "oin2")
                    gelus(0)
                    x_evac(2)
                    decays(1, "oin3")
                    y_rounded(0, "oin3")
                    multipliers(1, "oin3")
                    gelus(1)
                    decays(2, "oin4")
                    y_rounded(1, "oin4")
                    multipliers(2, "oin4")
                    gelus(2)
                    y_rounded(2, "oout0")
                norm(l, 0, None if l else (lambda: values_evac(0, 0), lambda: values_evac(0, 1)))
                act.wait_ge(evac_a, ACT_BEFORE[f"q{l}_0"])
                for i in range(8):
                    if i < 4:
                        hi, full = k_hi[:, 2 * i:2 * i + 2, :], k_mem[:, 2 * i:2 * i + 2, :]
                    else:
                        m, n = (i - 4) // 2, i % 2
                        hi, full = v_hi[:, m, 512 * n:512 * (n + 1)], v_mem[:, m, 512 * n:512 * (n + 1)]
                    nc.scalar.activation(hi, full, ACT.Copy).then_inc(kv_hi_ready, 1)
                for n in (0, 1):
                    filled_by(f"q{l}_{n}")
                    for j in range(4):
                        nc.scalar.activation(q_hi[:, 4 * n + j, :], bank(f"q{l}_{n}", j), ACT.Copy, scale=X_HD ** -0.5).then_inc(evac_a, 1)

                def x_exps(u):
                    v = l * TT + u
                    act.wait_ge(x_maxed, v + 1)
                    if u >= 2:
                        act.wait_ge(x_turned, MT * (v - 1))
                    for r in range(X_HEADS):
                        c0 = (r % 2) * MEM
                        last = nc.scalar.activation(px[:, u % 2, r, :], ps[:, x_halves(l)[0] + 2 * (u % 2) + r // 2, c0:c0 + MEM], ACT.Exp,
                                                    bias=negmax[:, u % 2, r:r + 1], accum_out=rowsum[:, u % 2, r:r + 1])
                    last.then_inc(x_exped, 1)

                def x_copy(u):
                    act.wait_ge(x_turned, MT * (l * TT + u) + 2)
                    for m in range(MT):
                        nc.scalar.activation(pxT_hi[:, m, :, u * P:(u + 1) * P], quarter(ps[:, x_halves(l)[1] + 2 * (u % 2) + m, :]),
                                             ACT.Copy).then_inc(x_rounded, 1)

                x_exps(0)
                x_exps(1)
                x_copy(0)
                x_exps(2)
                x_copy(1)
                x_exps(3)
                x_copy(2)
                x_copy(3)
                for n in (0, 1):
                    filled_by(f"xo{l}_{n}")
                    for j in range(4):
                        nc.scalar.activation(fm_hi[:, 4 * n + j, :], bank(f"xo{l}_{n}", j), ACT.Copy).then_inc(evac_a, 1)
                norm(l, 1, None if l else (lambda: keys_evac(1, 0), lambda: keys_evac(1, 1)))
                def up_evac(n, m=0):
                    name = f"up{l}_{n}"
                    act.wait_ge(w_used, CHUNK0[name] + KT + PAIR_CHUNKS * m)
                    for j in (0, 1):
                        if n:
                            act.wait_ge(evac_d, DVE_BEFORE[name] - 1 + j + PAIR_EVACS * m)
                        nc.scalar.activation(silu[:, j, :], bank(name, j), ACT.Silu).then_inc(evac_a, 1)
                    for j in (0, 1):
                        act.wait_ge(evac_d, DVE_BEFORE[name] + j + 1 + PAIR_EVACS * m)
                        nc.scalar.activation(tile_of(g_hi, 2 * n + j, m), gf[:, j, :], ACT.Copy).then_inc(g_hi_ready, 1)

                for n in range(UP_FIRST):
                    round_weights(CHUNK0[f"up{l}_{n + 1}"] + RING - 1)
                    up_evac(n)
                with act.Fori(0, UP_PAIRS - 1) as m:
                    for n in (UP_FIRST, UP_FIRST + 1):
                        for k in range(KT):
                            round_chunk(CHUNK0[f"up{l}_{n}"] + RING - 1 + k, m)
                        up_evac(n, m)
                rounded[0] = CHUNK0[f"up{l}_{FT // 2 - 2}"] + RING - 1
                for n in (FT // 2 - 2, FT // 2 - 1):
                    round_weights(CHUNK0[f"up{l}_{n}"] + KT + RING - 1)
                    up_evac(n)
                norm(l, 2, None if l else (lambda: values_evac(1, 0), lambda: values_evac(1, 1)))

        @block.vector
        def _(dve):
            chain = [0]

            def settle(ins):
                chain[0] += 1
                ins.then_inc(d_chain, 1)
                dve.wait_ge(d_chain, chain[0])

            def low_part(lo, full, hi, done):
                nc.vector.tensor_tensor(lo, full, hi.bitcast(F32), ALU.subtract).then_inc(done, 1)

            def turn_evac(name, hi, lo):
                for j in range(4):
                    dve.wait_ge(evac_a, ACT_BEFORE[name] + j + 1)
                    low_part(fm_target(lo, name, j), quarter(bank(name, j)), fm_target(hi, name, j), evac_d)

            dve.wait_ge(s_consts, 16)
            nc.vector.tensor_copy(ident_b[:, :], consts[:, C_ID:C_ID + P]).then_inc(tables_ready, 1)
            nc.vector.tensor_copy(bias_sel[:, :], consts[0:2 * KT, C_SEL:C_SEL + KT])
            nc.vector.tensor_copy(causal_b[:, :], consts[:, C_CAUSAL:C_CAUSAL + P]).then_inc(tables_ready, 1)
            nc.vector.tensor_copy(cmask_b[:, :, :].rearrange("p t n -> p (t n)"),
                                  consts[:, C_CMASK:C_CMASK + TT * 32]).then_inc(tables_ready, 1)
            nc.vector.memset(pool_sum[:, :, 0:PAD], 0.0)
            nc.vector.memset(pool_in[:, :, 0:PAD], 0.0).then_inc(pads_ready, 1)
            turn_evac("x0", fm_hi, fm_lo)
            turn_evac("x1", fm_hi, fm_lo)
            dve.wait_ge(s_pos, 32)
            settle(nc.vector.memset(pos_f[:, :], 0.0))
            nc.vector.tensor_copy(pos_f[:, 0:TT], pos_i[:, 0:TT])
            settle(nc.vector.tensor_copy(pos_f[0:NCMP, TT:TT + 1], pos_i[0:NCMP, TT:TT + 1]))
            settle(nc.vector.tensor_tensor(ang[:, 0, :].rearrange("p (t f) -> p t f", f=HALF),
                                           pos_f[:, :].unsqueeze(2).to_broadcast([P, TT + 1, HALF]),
                                           consts[:, C_INVF:C_INVF + HALF].unsqueeze(1).to_broadcast([P, TT + 1, HALF]), ALU.mult))
            magic = 1.5 * 2.0 ** 23
            settle(nc.vector.tensor_scalar(ang[:, 1, :], ang[:, 0, :], 1.0 / (2.0 * np.pi), magic, ALU.mult, ALU.add))
            settle(nc.vector.tensor_scalar(ang[:, 1, :], ang[:, 1, :], magic, None, ALU.subtract))
            c1 = 6.28125
            c2 = float(np.float32(np.round((2 * np.pi - c1) * 2 ** 20) / 2 ** 20))
            c3 = 2 * np.pi - c1 - c2
            for c in (c1, c2, c3):
                settle(nc.vector.scalar_tensor_tensor(out=ang[:, 0, :], in0=ang[:, 1, :], scalar=-c, in1=ang[:, 0, :],
                                                      op0=ALU.mult, op1=ALU.add))
            edge = 3.1415925
            settle(nc.vector.tensor_scalar(ang[:, 0, :], ang[:, 0, :], edge, -edge, ALU.min, ALU.max))
            settle(nc.vector.scalar_tensor_tensor(out=ang[:, 1, :], in0=ang[:, 0, :], scalar=-1.0, in1=ang[:, 0, :],
                                                  op0=ALU.mult, op1=ALU.max))
            nc.vector.tensor_scalar(ang[:, 1, :], ang[:, 1, :], -1.0, np.pi / 2, ALU.mult, ALU.add).then_inc(ang_ready, 1)

            turn_evac("tm", mem_hi, mem_lo)

            for g, win in enumerate(WINDOWS):
                dve.wait_ge(evac_a, ACT_BEFORE["ein0"] + g + 1)
                src, sh, n = pool_in[:, g, :], 1, 0
                while sh < win:
                    dst = pool_sum[:, n % 2, :]
                    settle(nc.vector.tensor_tensor(dst[:, PAD:], src[:, PAD:], src[:, PAD - sh:PAD + SEQ - sh], ALU.add))
                    src, sh, n = dst, 2 * sh, n + 1
                u = pool_in[:, g, :]
                settle(nc.vector.tensor_tensor(src[:, PAD:2 * PAD], src[:, PAD:2 * PAD],
                                               consts[:, C_PINV + g * PAD:C_PINV + (g + 1) * PAD], ALU.mult))
                settle(nc.vector.tensor_tensor(u[:, PAD:2 * PAD], src[:, PAD:2 * PAD], u[:, PAD:2 * PAD], ALU.subtract))
                nc.vector.scalar_tensor_tensor(out=u[:, 2 * PAD:], in0=src[:, 2 * PAD:], scalar=1.0 / win, in1=u[:, 2 * PAD:],
                                               op0=ALU.mult, op1=ALU.subtract).then_inc(pooled_ready, 1)
                dve.wait_ge(pooled_ready, g + 1)

            def rotate(x1, x2, cos, sin, tmp, done=None):
                t0, t1, t2 = tmp
                nc.vector.tensor_tensor(t0, x1, sin, ALU.mult)
                nc.vector.tensor_tensor(t1, x2, sin, ALU.mult)
                settle(nc.vector.tensor_tensor(t2, x1, cos, ALU.mult))
                settle(nc.vector.tensor_tensor(x2, x2, cos, ALU.mult))
                nc.vector.tensor_tensor(x1, t2, t1, ALU.subtract)
                last = nc.vector.tensor_tensor(x2, x2, t0, ALU.add)
                if done is None:
                    settle(last)
                else:
                    last.then_inc(done, 1)

            dve.wait_ge(trig_ready, 2)
            dve.wait_ge(evac_a, ACT_AFTER["ein1"])
            for t in range(TT):
                qh = q_tok[:, t, :, 1, :].bitcast(F32)
                tmp = [rot_tmp[:, i, t * 64:(t + 1) * 64].rearrange("p (h d) -> p h d", d=HALF) for i in range(3)]
                cs = [trig[:, i, t, :].unsqueeze(1).to_broadcast([P, HEADS, HALF]) for i in (0, 1)]
                rotate(qh[:, :, 0:HALF], qh[:, :, HALF:ROT], cs[0], cs[1], tmp, q_rotated)
            dve.wait_ge(evac_a, ACT_AFTER["ein2"])
            for b in (0, 1):
                for t in range(TT):
                    kh = kv_tok[:, t, 256 * b:256 * b + P].rearrange("p (g d) -> p g d", d=HD)
                    tmp = [rot_tmp[:, i, (b * TT + t) * 16:(b * TT + t + 1) * 16].rearrange("p (g d) -> p g d", d=HALF) for i in range(3)]
                    cs = [trig[:, i, t, :].unsqueeze(1).to_broadcast([P, KV_HEADS, HALF]) for i in (0, 1)]
                    rotate(kh[:, :, 0:HALF], kh[:, :, HALF:ROT], cs[0], cs[1], tmp)
                for t in range(TT):
                    src = kv_tok[:, t, 256 * b:256 * b + P].rearrange("p (g d) -> p g d", d=HD)
                    last = nc.vector.tensor_copy(kdup[:, b, t, :, 0, :], src)
                    last = nc.vector.tensor_copy(kdup[:, b, t, :, 1, :], src)
                last.then_inc(kdup_ready, 1)
            for t in range(TT):
                dve.wait_ge(q_hi_ready, t + 1)
                last = nc.vector.tensor_tensor(q_tok[:, t, :, 1, :], q_tok[:, t, :, 1, :].bitcast(F32),
                                               q_tok[:, t, :, 0, :].bitcast(F32), ALU.subtract)
            last.then_inc(q_ready, 1)
            dve.wait_ge(evac_a, ACT_AFTER["ein3"])
            for n in (0, 1):
                for part in (0, 1):
                    c0 = (V_POSK, V_POSV)[n] + part * CMP_STRIDE
                    nc.vector.tensor_tensor(raw_pos[:, n, part, :].rearrange("p (b l) -> p b l", l=CMP_STRIDE),
                                            raw_cmp[:, n, :].rearrange("p (b l) -> p b l", l=CMP_STRIDE),
                                            chan[:, c0:c0 + CMP_STRIDE].unsqueeze(1).to_broadcast([P, SEQ // CMP_STRIDE, CMP_STRIDE]),
                                            ALU.add).then_inc(rawpos_ready, 1)
            for j in range(4):
                dve.wait_ge(evac_a, ACT_BEFORE["mix"] + j + 1)
                nc.vector.scalar_tensor_tensor(out=fm_lo[:, j, :], in0=bank("mix", j), scalar=chan[:, V_PSCALE + j:V_PSCALE + j + 1],
                                               in1=fm_hi[:, j, :].bitcast(F32), op0=ALU.mult, op1=ALU.subtract).then_inc(evac_d, 1)
            for n in (0, 1):
                group_filled(dve, f"tq{n}")
                for j in (2, 3):
                    nc.vector.tensor_copy(qT[:, 4 * n + j, :], bank(f"tq{n}", j)).then_inc(evac_d, 1)
            for j in range(4):
                dve.wait_ge(evac_a, ACT_BEFORE["tk"] + j + 1)
                low_part(kT_lo[:, j // 2, j % 2, :], bank("tk", j), kT_hi[:, j // 2, j % 2, :], evac_d)
            dve.wait_ge(evac_a, ACT_BEFORE["cmp"] + 1)
            kc = kc_tok[:, :, :]
            tmp = [kc_tmp[:, i, :].rearrange("p (g d) -> p g d", d=HALF) for i in range(3)]
            cs = [trig[0:NCMP, i, TT, :].unsqueeze(1).to_broadcast([NCMP, KV_HEADS, HALF]) for i in (0, 1)]
            rotate(kc[:, :, 0:HALF], kc[:, :, HALF:ROT], cs[0], cs[1], tmp)
            nc.vector.tensor_copy(kc_dup[:, :, 0, :], kc)
            nc.vector.tensor_copy(kc_dup[:, :, 1, :], kc).then_inc(kcdup_ready, 1)

            def row_max(u):
                qb, b, h0, heads = UNITS[u]
                dve.wait_ge(scored, u + 1)
                w, n = unit_width(u), NCMP if b == "cmp" else (qb + 1) * P
                s = ps[:, 2 * (u % 2):2 * (u % 2) + 2, 0:heads // 2 * w].rearrange("p i (r n) -> p i r n", n=w)[:, :, :, 0:n]
                m = negmax[:, u % 2, 0:heads].rearrange("p (r i) -> p i r", i=2)
                nc.vector.tensor_reduce(m, s, AX.X, ALU.max, negate=True).then_inc(maxed, 1)

            dve.wait_ge(evac_a, ACT_AFTER["cmp"])
            added = 0
            row_max(0)
            row_max(1)
            for u, (qb, b, h0, heads) in enumerate(UNITS):
                n = NCMP if b == "cmp" else P
                dve.wait_ge(turned, 2 * u + 1)
                nc.vector.tensor_copy(probsT[0:n, u % 2, 0:4, :].rearrange("p b q -> p (b q)"), ps[0:n, 4, :]).then_inc(copied_d, 1)
                if u + 2 < len(UNITS):
                    row_max(u + 2)
                wt = weight[:, u % 2, 0:heads]
                nc.vector.reciprocal(wt, rowsum[:, u % 2, 0:heads]).then_inc(summed, 1)
                dve.wait_ge(summed, u + 1)
                gt = gates[:, qb, h0 * 3:(h0 + heads) * 3].rearrange("p (r c) -> p r c", c=3)[:, :, GATE_OF[b]]
                settle(nc.vector.tensor_tensor(wt, wt, gt, ALU.mult))
                if b == "cmp":
                    settle(nc.vector.tensor_scalar(wt, wt, consts[:, C_ROWOK + qb:C_ROWOK + qb + 1], None, ALU.mult))
                dve.wait_ge(pv_done, u + 1)
                o = ps[:, 6 + u % 2, 0:heads * HD].rearrange("p (r d) -> p r d", d=HD)
                wb = wt.unsqueeze(2).to_broadcast([P, heads, HD])
                dst = o_tok[:, qb, h0 * HD:(h0 + heads) * HD]
                if b == "cmp":
                    nc.vector.tensor_tensor(dst.rearrange("p (r d) -> p r d", d=HD), o, wb, ALU.mult).then_inc(o_evac, 1)
                    dve.wait_ge(o_evac, u + 1)
                else:
                    nc.vector.tensor_tensor(o_tmp[:, 0:heads * HD].rearrange("p (r d) -> p r d", d=HD), o, wb, ALU.mult).then_inc(o_evac, 1)
                    dve.wait_ge(o_evac, u + 1)
                    added += 1
                    nc.vector.tensor_tensor(dst, dst, o_tmp[:, 0:heads * HD], ALU.add).then_inc(o_ready, 1)
                    dve.wait_ge(o_ready, added)
            for t in range(TT):
                dve.wait_ge(evac_a, ACT_BEFORE["to"] + t + 1)
                low_part(fm_lo[:, 4:8, t * P:(t + 1) * P], quarter(bank("to", t)), fm_hi[:, 4:8, t * P:(t + 1) * P], evac_d)

            def add_residual(n, name, t):
                xs = x_res[:, t, 512 * n:512 * (n + 1)]
                if whole[0]:
                    dve.wait_ge(x_whole, whole[0])
                nc.vector.scalar_tensor_tensor(out=xs, in0=xs, scalar=ALPHA, in1=bank(name, t), op0=ALU.mult,
                                               op1=ALU.add).then_inc(evac_d, 1)

            def half_stats(n, name, t):
                dve.wait_ge(evac_d, DVE_BEFORE[name] + t + 1)
                return nc.vector.bn_stats(stats[:, t, n, :], x_res[:, t, 512 * n:512 * (n + 1)])

            whole = [0]

            def norm(l, i, names):
                v = 3 * l + i
                group_filled(dve, names[0])
                for t in range(TT):
                    add_residual(0, names[0], t)
                for t in range(TT):
                    half_stats(0, names[0], t)
                dve.wait_ge(s_lnp, 64 * (v + 1))
                settle(nc.vector.tensor_copy(bias_hi[:, :], bias_raw[:, :]))
                rows = slice(0, 2 * KT)
                settle(nc.vector.tensor_scalar(bias_raw[:, :], bias_raw[:, :], consts[rows, C_LOW:C_LOW + 1], None, ALU.mult))
                nc.vector.scalar_tensor_tensor(out=bias_rows[:, :], in0=bias_hi[:, :].bitcast(F32), scalar=consts[rows, C_LOW + 1:C_LOW + 2],
                                               in1=bias_raw[:, :], op0=ALU.mult, op1=ALU.add).then_inc(bias_ready, 1)
                def turned_low(t):
                    name = f"ln{l}{i}_{t // 2}"
                    for j in (2 * (t % 2), 2 * (t % 2) + 1):
                        dve.wait_ge(evac_a, ACT_BEFORE[name] + j + 1 + 2 * l)
                        low_part(fm_target(fm_lo, name, j), quarter(bank(name, j)), fm_target(fm_hi, name, j), evac_d)

                def add_second(t):
                    if t < TT - 1:
                        dve.wait_ge(tile_filled, (TT - 1) * v + t + 1)
                    else:
                        group_filled(dve, names[1])
                    add_residual(1, names[1], t)

                add_second(0)
                settle(half_stats(1, names[1], 0))
                for t in range(TT):
                    if t + 1 < TT:
                        add_second(t + 1)
                    settle(nc.vector.bn_aggr(mv[:, t, :], stats[:, t, :, :].rearrange("p a b -> p (a b)")))
                    nc.vector.tensor_scalar(lnc[:, 0, t:t + 1], mv[:, t, 1:2], EPS, None, ALU.add).then_inc(ln_var, 1)
                    settle(nc.vector.scalar_tensor_tensor(out=x_res[:, t, :], in0=x_res[:, t, :], scalar=mv[:, t, 0:1], in1=ln_g[:, :],
                                                          op0=ALU.subtract, op1=ALU.mult))
                    dve.wait_ge(ln_sd, TT * v + t + 1)
                    nc.vector.reciprocal(lnc[:, 2, t:t + 1], lnc[:, 1, t:t + 1]).then_inc(ln_coef, 1)
                    if t + 1 < TT:
                        settle(half_stats(1, names[1], t + 1))

                def bias(t, part=slice(0, D)):
                    nc.vector.tensor_tensor(x_res[:, t, part], x_res[:, t, part], ln_b[:, part], ALU.add).then_inc(x_whole, 1)

                if (l, i) == (DEPTH - 1, 2):
                    dve.wait_ge(x_ready, TT * v + TT - 1)
                    bias(TT - 2, HALVES[1])
                    for n, part in enumerate(HALVES):
                        dve.wait_ge(x_ready, TT * (v + 1) + n)
                        bias(TT - 1, part)
                else:
                    for t in (range(TT - 1, TT) if l else range(TT)):
                        turned_low(t)
                    for t in range(TT):
                        bias(t)
                    whole[0] += TT

            for l in range(DEPTH):
                if l == 0:
                    norm(0, 0, ("eout0", "eout1"))
                if l:
                    lam = chan[:, V_LAM:V_LAM + RT]
                    settle(nc.vector.tensor_scalar(lru_c[:, 0, :], lam, -1.0, None, ALU.mult))
                    nc.vector.tensor_tensor(lru_c[:, 0, :], lru_c[:, 0, :], lam, ALU.min).then_inc(sp_ready, 1)
                    dve.wait_ge(sp_exp, 1)
                    z, w = lru_c[:, 1, :], lru_c[:, 0, :]
                    w2, acc = a_sq[:, 0:RT], a_sq[:, RT:2 * RT]
                    settle(nc.vector.tensor_scalar(w, z, 2.0, None, ALU.add))
                    settle(nc.vector.reciprocal(w, w))
                    settle(nc.vector.tensor_tensor(w, w, z, ALU.mult))
                    settle(nc.vector.tensor_tensor(w2, w, w, ALU.mult))
                    settle(nc.vector.tensor_scalar(acc, w2, 1.0 / 17, 1.0 / 15, ALU.mult, ALU.add))
                    for n in (13, 11, 9, 7, 5, 3, 1):
                        settle(nc.vector.tensor_tensor(acc, acc, w2, ALU.mult))
                        settle(nc.vector.tensor_scalar(acc, acc, 1.0 / n, None, ALU.add))
                    settle(nc.vector.scalar_tensor_tensor(out=acc, in0=acc, scalar=2.0, in1=w, op0=ALU.mult, op1=ALU.mult))
                    settle(nc.vector.tensor_scalar(z, lam, -1.0, 0.0, ALU.mult, ALU.max))
                    settle(nc.vector.tensor_tensor(acc, acc, z, ALU.add))
                    nc.vector.tensor_scalar(lru_c[:, 0, :], acc, 8.0, None, ALU.mult)
                    nc.vector.tensor_scalar(lru_c[:, 1, :], acc, -8.0, None, ALU.mult).then_inc(lru_ready, 1)
                    dve.wait_ge(lru_ready, 1)
                    group_filled(dve, "v1_1")
                    nc.vector.memset(x_pad[:, :, :, 0:CONV - 1].rearrange("p i j c -> p (i j) c"), 0.0).then_inc(pads_ready, 1)
                    dve.wait_ge(s_posb, 16)
                    settle(nc.vector.tensor_copy(keep[:, :], posb[:, :]))
                    settle(nc.vector.tensor_scalar(keep[:, :], keep[:, :], 0.0, None, ALU.not_equal))

                    def conv(n):
                        first, tiles, name, b = RG_SETS[n]
                        for j in range(tiles):
                            dve.wait_ge(evac_a, ACT_BEFORE[name] + b + j + 1)
                            cw = lambda k: chan[:, V_CONVW + k * RT + first + j:V_CONVW + k * RT + first + j + 1]
                            settle(nc.vector.tensor_scalar(h[:, first + j, :], x_pad[:, n % 2, j, 0:SEQ], cw(0),
                                                           chan[:, V_CONVB + first + j:V_CONVB + first + j + 1], ALU.mult, ALU.add))
                            for k in range(1, CONV):
                                ins = nc.vector.scalar_tensor_tensor(out=h[:, first + j, :], in0=x_pad[:, n % 2, j, k:k + SEQ], scalar=cw(k),
                                                                     in1=h[:, first + j, :], op0=ALU.mult, op1=ALU.add)
                                if k < CONV - 1:
                                    settle(ins)
                            ins.then_inc(conv_ready, 1)

                    def multipliers_squared(n):
                        first, tiles, _, _ = RG_SETS[n]
                        done = sum(s[1] for s in RG_SETS[:n])
                        dve.wait_ge(evac_a, ACT_AFTER[f"ia{n}" if n < 2 else "ra2"])
                        for j in range(tiles):
                            a_, i_ = RA[n][:, j, :], IB[n][:, j, :]
                            dve.wait_ge(decay_ready, done + j + 1)
                            settle(nc.vector.tensor_tensor(a_, a_, keep[:, :], ALU.mult))
                            nc.vector.tensor_tensor(a_sq[:, :], a_, a_, ALU.mult)
                            nc.vector.tensor_tensor(i_, i_, h[:, first + j, :], ALU.mult)
                            settle(nc.vector.scalar_tensor_tensor(out=tm[:, j, :], in0=keep[:, :], scalar=0.0, in1=tm[:, j, :],
                                                                  op0=ALU.is_equal, op1=ALU.max))
                            nc.vector.scalar_tensor_tensor(out=tm[:, j, :], in0=a_sq[:, :], scalar=1.0, in1=tm[:, j, :],
                                                           op0=ALU.add, op1=ALU.mult).then_inc(m2_ready, 1)
                            dve.wait_ge(m2_ready, done + j + 1)

                    def recurrence(n):
                        first, tiles, _, _ = RG_SETS[n]
                        done = sum(s[1] for s in RG_SETS[:n])
                        for j in range(tiles):
                            a_, i_ = RA[n][:, j, :], IB[n][:, j, :]
                            dve.wait_ge(mult_ready, done + j + 1)
                            settle(nc.vector.tensor_tensor(i_, i_, tm[:, j, :], ALU.mult))
                            nc.vector.tensor_tensor_scan(h[:, first + j, :], a_, i_, 0.0, ALU.mult, ALU.add).then_inc(h_ready, 1)
                        dve.wait_ge(h_ready, done + tiles)

                    def y_tile(n, j):
                        first, _, name = GATE_SETS[n]
                        dve.wait_ge(evac_a, ACT_BEFORE[name] + j + 1)
                        hj = h[:, first + j, :]
                        nc.vector.tensor_tensor(hj, hj, gelu[:, first + j, :], ALU.mult).then_inc(y_full, 1)

                    def y_low(n, j):
                        first = GATE_SETS[n][0]
                        i = sum(s[1] for s in GATE_SETS[:n]) + j
                        dve.wait_ge(y_hi_ready, i + 1)
                        low_part(y_lo[:, first + j, :], h[:, first + j, :], y_hi[:, first + j, :], y_ready)

                    conv(0)
                    conv(1)
                    multipliers_squared(0)
                    recurrence(0)
                    y_tile(0, 0)
                    y_tile(0, 1)
                    conv(2)
                    multipliers_squared(1)
                    y_low(0, 0)
                    y_low(0, 1)
                    recurrence(1)
                    for j in range(4):
                        y_tile(1, j)
                    multipliers_squared(2)
                    for j in range(4):
                        y_low(1, j)
                    recurrence(2)
                    for j in range(5):
                        if j < 4:
                            y_tile(2, j)
                        if j:
                            y_low(2, j - 1)
                    norm(1, 0, ("oout0", "oout1"))

                def x_max(u):
                    dve.wait_ge(x_scored, l * TT + u + 1)
                    b0 = x_halves(l)[0] + 2 * (u % 2)
                    s = ps[:, b0:b0 + 2, :].rearrange("p b (h m) -> p (b h) m", m=MEM)
                    nc.vector.tensor_reduce(negmax[:, u % 2, 0:X_HEADS], s, AX.X, ALU.max, negate=True).then_inc(x_maxed, 1)

                def x_scale(u):
                    dve.wait_ge(x_exped, l * TT + u + 1)
                    wt = weight[:, u % 2, 0:X_HEADS]
                    settle(nc.vector.reciprocal(wt, rowsum[:, u % 2, 0:X_HEADS]))
                    nc.vector.tensor_tensor(px[:, u % 2, :, :], px[:, u % 2, :, :], wt.unsqueeze(2).to_broadcast([P, X_HEADS, MEM]),
                                            ALU.mult).then_inc(x_scaled, 1)

                def x_copy(u):
                    for m in range(MT):
                        dve.wait_ge(x_rounded, MT * (l * TT + u) + m + 1)
                        low_part(pxT_lo[:, m, :, u * P:(u + 1) * P], quarter(ps[:, x_halves(l)[1] + 2 * (u % 2) + m, :]),
                                 pxT_hi[:, m, :, u * P:(u + 1) * P], x_split)

                for i in range(8):
                    dve.wait_ge(kv_hi_ready, 8 * l + i + 1)
                    if i < 4:
                        k = slice(2 * i, 2 * i + 2)
                        low_part(k_lo[:, k, :], k_mem[:, k, :], k_hi[:, k, :], kv_ready)
                    else:
                        m, n = (i - 4) // 2, slice(512 * (i % 2), 512 * (i % 2 + 1))
                        low_part(v_lo[:, m, n], v_mem[:, m, n], v_hi[:, m, n], kv_ready)
                for n in (0, 1):
                    for j in range(4):
                        dve.wait_ge(evac_a, ACT_BEFORE[f"q{l}_{n}"] + j + 1)
                        nc.vector.scalar_tensor_tensor(out=q_lo[:, 4 * n + j, :], in0=bank(f"q{l}_{n}", j), scalar=X_HD ** -0.5,
                                                       in1=q_hi[:, 4 * n + j, :].bitcast(F32), op0=ALU.mult,
                                                       op1=ALU.subtract).then_inc(evac_d, 1)
                x_max(0)
                x_max(1)
                x_scale(0)
                x_scale(1)
                x_max(2)
                x_copy(0)
                x_scale(2)
                x_max(3)
                x_copy(1)
                x_copy(2)
                x_scale(3)
                x_copy(3)
                for n in (0, 1):
                    name = f"xo{l}_{n}"
                    for j in range(4):
                        dve.wait_ge(evac_a, ACT_BEFORE[name] + j + 1)
                        low_part(fm_lo[:, 4 * n + j, :], bank(name, j), fm_hi[:, 4 * n + j, :], evac_d)
                norm(l, 1, (f"wo{l}_0", f"wo{l}_1"))
                def up_product(n, m=0):
                    name = f"up{l}_{n}"
                    dve.wait_ge(w_used, CHUNK0[name] + KT + PAIR_CHUNKS * m)
                    for j in (0, 1):
                        i = l * FT + 2 * n + j
                        dve.wait_ge(evac_a, ACT_BEFORE[name] + j + 1 + PAIR_EVACS * m)
                        if i >= 2:
                            dve.wait_ge(g_ready, i - 1 + PAIR_TILES * m)
                            dve.wait_ge(g_hi_ready, i - 1 + PAIR_TILES * m)
                        nc.vector.tensor_tensor(gf[:, j, :], silu[:, j, :], bank(name, 2 + j), ALU.mult).then_inc(evac_d, 1)
                    for j in (0, 1):
                        dve.wait_ge(g_hi_ready, l * FT + 2 * n + j + 1 + PAIR_TILES * m)
                        low_part(tile_of(g_lo, 2 * n + j, m), gf[:, j, :], tile_of(g_hi, 2 * n + j, m), g_ready)

                for n in range(UP_FIRST):
                    up_product(n)
                with dve.Fori(0, UP_PAIRS) as m:
                    for n in (UP_FIRST, UP_FIRST + 1):
                        up_product(n, m)
                norm(l, 2, (f"dn{l}_0", f"dn{l}_1"))


INPUTS = ["x", "mem", "positions", "e_w_in", "e_pool_w", "e_pool_scale", "e_cmp_pos_k", "e_cmp_pos_v", "e_cmp_wk",
          "e_cmp_wv", "e_w_out", "o_w_in", "o_conv_w", "o_conv_b", "o_wa", "o_ba", "o_wx", "o_bx", "o_lambda",
          "o_w_out", "x_wq", "x_wkv", "x_wo", "f_w_up", "f_w_down", "ln_g", "ln_b"]


def kernel(**inputs):
    import concourse.bacc as bacc
    from concourse.bass_utils import run_bass_kernel_spmd

    nc = bacc.Bacc("TRN2", target_bir_lowering=False, num_devices=1)
    arrays, aps = {}, {}
    for name in INPUTS + ["consts"]:
        v = shape_constants() if name == "consts" else np.ascontiguousarray(inputs[name])
        arrays[f"in_{name}"] = v
        aps[name] = nc.dram_tensor(f"in_{name}", v.shape, mybir.dt.from_np(v.dtype), kind="ExternalInput").ap()
    out = nc.dram_tensor("out_x", (1, SEQ, D), F32, kind="ExternalOutput").ap()
    hybrid_trunk(nc, aps, out)
    r = run_bass_kernel_spmd(nc, [arrays], core_ids=[0])
    return r.results[0]["out_x"]
```
